# Optimizing a Trainium2 kernel written in Bass

```python
import math
import jax, jax.numpy as jnp
from jax import lax
import numpy as np

D_MODEL = 1024
BATCH = 1
SEQ = 512
DEPTH = 1

SSD_EXPAND = 2
SSD_D_INNER = SSD_EXPAND * D_MODEL
SSD_HEAD_DIM = 64
SSD_HEADS = SSD_D_INNER // SSD_HEAD_DIM
SSD_GROUPS = 4
SSD_HEADS_PER_GROUP = SSD_HEADS // SSD_GROUPS
SSD_STATE = 128
SSD_CONV = 4
SSD_CHUNK = 128
SSD_CONV_CH = SSD_D_INNER + 2 * SSD_GROUPS * SSD_STATE
SSD_DT_MIN = 0.001
SSD_DT_MAX = 0.1

DA_HEAD_DIM = 64
DA_HEADS = D_MODEL // (2 * DA_HEAD_DIM)
DA_V_DIM = 2 * DA_HEAD_DIM
DA_WIDTH = DA_HEADS * 2 * DA_HEAD_DIM
Q_BLOCK = 128

N_BRANCH = 2
D_FF = 2816
EPS = 1e-6

IN_SIZES = [SSD_D_INNER, SSD_CONV_CH, SSD_HEADS, DA_WIDTH, DA_WIDTH, DA_WIDTH, N_BRANCH * D_MODEL]
D_IN_PROJ = sum(IN_SIZES)
IN_SPLITS = np.cumsum(IN_SIZES)[:-1].tolist()


def rmsnorm(x, g):
    xf = x.astype(jnp.float32)
    y = xf * lax.rsqrt(jnp.mean(xf * xf, axis=-1, keepdims=True) + EPS)
    return y.astype(x.dtype) * g

def swiglu(x, w_gate, w_up, w_down):
    return (jax.nn.silu(x @ w_gate) * (x @ w_up)) @ w_down

def alibi_slopes(n_heads):
    return jnp.asarray(2.0 ** (-8.0 * np.arange(1, n_heads + 1) / n_heads), dtype=jnp.float32)

def causal_dwconv(x, w, b):
    k = w.shape[0]
    y = lax.conv_general_dilated(x, w[:, None, :], window_strides=(1,), padding=[(k - 1, 0)],
                                 dimension_numbers=("NWC", "WIO", "NWC"),
                                 feature_group_count=x.shape[-1])
    return y + b

def ssd_chunked(x, dt, a_head, bm, cm):
    b, L, H, P = x.shape
    G, N, E, Q = SSD_GROUPS, SSD_STATE, SSD_HEADS_PER_GROUP, SSD_CHUNK
    nc = L // Q
    X = (x.astype(jnp.float32) * dt[..., None]).reshape(b, nc, Q, G, E, P)
    a = (dt * a_head).reshape(b, nc, Q, G, E).transpose(0, 3, 4, 1, 2)
    Bc = bm.astype(jnp.float32).reshape(b, nc, Q, G, N)
    Cc = cm.astype(jnp.float32).reshape(b, nc, Q, G, N)
    a_cum = jnp.cumsum(a, axis=-1)
    seg = a_cum[..., :, None] - a_cum[..., None, :]
    causal = jnp.tril(jnp.ones((Q, Q), dtype=bool))
    Lmat = jnp.exp(jnp.where(causal, seg, -jnp.inf))
    CB = jnp.einsum('bclgn,bcsgn->bgcls', Cc, Bc)
    y_diag = jnp.einsum('bgcls,bgecls,bcsgep->bclgep', CB, Lmat, X)
    decay_states = jnp.exp(a_cum[..., -1:] - a_cum)
    states = jnp.einsum('bclgn,bgecl,bclgep->bcgepn', Bc, decay_states, X)
    chunk_decay = jnp.exp(a_cum[..., -1])

    def step(h, inp):
        s, d = inp
        return h * d[..., None, None] + s, h

    _, prev = lax.scan(step, jnp.zeros(states.shape[:1] + states.shape[2:], jnp.float32),
                       (jnp.moveaxis(states, 1, 0), jnp.moveaxis(chunk_decay, 3, 0)))
    prev = jnp.moveaxis(prev, 0, 1)
    y_off = jnp.einsum('bclgn,bcgepn,bgecl->bclgep', Cc, prev, jnp.exp(a_cum))
    return (y_diag + y_off).reshape(b, L, H, P)

def ssd_branch(z, xbc, dt_raw, conv_w, conv_b, dt_bias, a_log, d_skip, norm_g, w_branch):
    b, L, _ = z.shape
    xbc = jax.nn.silu(causal_dwconv(xbc, conv_w, conv_b))
    xs, bm, cm = jnp.split(xbc, [SSD_D_INNER, SSD_D_INNER + SSD_GROUPS * SSD_STATE], axis=-1)
    dt = jax.nn.softplus(dt_raw.astype(jnp.float32) + dt_bias.astype(jnp.float32))
    a_head = -jnp.exp(a_log.astype(jnp.float32))
    xh = xs.reshape(b, L, SSD_HEADS, SSD_HEAD_DIM)
    y = ssd_chunked(xh, dt, a_head,
                    bm.reshape(b, L, SSD_GROUPS, SSD_STATE), cm.reshape(b, L, SSD_GROUPS, SSD_STATE))
    y = (y + d_skip.astype(jnp.float32)[:, None] * xh.astype(jnp.float32)).astype(z.dtype)
    y = y.reshape(b, L, SSD_D_INNER) * jax.nn.silu(z)
    y = rmsnorm(y.reshape(b, L, SSD_GROUPS, SSD_D_INNER // SSD_GROUPS), 1.0).reshape(b, L, SSD_D_INNER) * norm_g
    return y @ w_branch

def diff_attn_branch(q, k, v, lq1, lk1, lq2, lk2, subln_g, w_branch, lam_init):
    b, L, _ = q.shape
    H, d = DA_HEADS, DA_HEAD_DIM
    q = q.reshape(b, L, H, 2, d)
    k = k.reshape(b, L, H, 2, d)
    v = v.reshape(b, L, H, DA_V_DIM)
    lam = (jnp.exp(jnp.sum(lq1.astype(jnp.float32) * lk1.astype(jnp.float32)))
           - jnp.exp(jnp.sum(lq2.astype(jnp.float32) * lk2.astype(jnp.float32))) + lam_init)
    slopes = alibi_slopes(H)
    scale = 1.0 / math.sqrt(d)
    nb = L // Q_BLOCK
    qb = q.reshape(b, nb, Q_BLOCK, H, 2, d).transpose(1, 0, 2, 3, 4, 5)
    key_pos = jnp.arange(L)

    def one_block(args):
        q_blk, i = args
        q_pos = i * Q_BLOCK + jnp.arange(Q_BLOCK)
        s = jnp.einsum('bqhmd,bkhmd->bhmqk', q_blk, k).astype(jnp.float32) * scale
        dist = (q_pos[:, None] - key_pos[None, :]).astype(jnp.float32)
        s = s - slopes[None, :, None, None, None] * dist
        s = jnp.where(dist >= 0, s, -jnp.inf)
        p = jax.nn.softmax(s, axis=-1)
        attn = p[:, :, 0] - lam * p[:, :, 1]
        return jnp.einsum('bhqk,bkhe->bqhe', attn.astype(v.dtype), v)

    out = lax.map(one_block, (qb, jnp.arange(nb)))
    out = out.transpose(1, 0, 2, 3, 4).reshape(b, L, H, DA_V_DIM)
    out = rmsnorm(out, subln_g) * (1.0 - lam_init)
    return out.reshape(b, L, DA_WIDTH) @ w_branch

def first_inputs(seed: int = 0) -> dict:
    key = jax.random.key(seed)
    ks = iter(jax.random.split(key, 40))
    f32 = jnp.float32

    def nrm(shape, fan_in):
        return jax.random.normal(next(ks), (DEPTH,) + shape, f32) * fan_in ** -0.5

    def gain(n):
        return 1.0 + 0.05 * jax.random.normal(next(ks), (DEPTH, n), f32)

    x = jax.random.normal(next(ks), (BATCH, SEQ, D_MODEL), f32)
    dt0 = jnp.exp(jax.random.uniform(next(ks), (DEPTH, SSD_HEADS), f32)
                  * (math.log(SSD_DT_MAX) - math.log(SSD_DT_MIN)) + math.log(SSD_DT_MIN))
    dt0 = jnp.maximum(dt0, 1e-4)
    return {
        "x": x,
        "ffn1_pre_g": gain(D_MODEL),
        "ffn1_w_gate": nrm((D_MODEL, D_FF), D_MODEL),
        "ffn1_w_up": nrm((D_MODEL, D_FF), D_MODEL),
        "ffn1_w_down": nrm((D_FF, D_MODEL), D_FF),
        "ffn1_post_g": gain(D_MODEL),
        "mix_pre_g": gain(D_MODEL),
        "w_in": nrm((D_MODEL, D_IN_PROJ), D_MODEL),
        "gate_b": 0.02 * jax.random.normal(next(ks), (DEPTH, N_BRANCH * D_MODEL), f32),
        "ssd_conv_w": nrm((SSD_CONV, SSD_CONV_CH), SSD_CONV),
        "ssd_conv_b": 0.02 * jax.random.normal(next(ks), (DEPTH, SSD_CONV_CH), f32),
        "ssd_dt_bias": dt0 + jnp.log(-jnp.expm1(-dt0)),
        "ssd_A_log": jnp.log(jax.random.uniform(next(ks), (DEPTH, SSD_HEADS), f32, 1.0, 16.0)),
        "ssd_D": gain(SSD_HEADS),
        "ssd_norm_g": gain(SSD_D_INNER),
        "ssd_w_branch": nrm((SSD_D_INNER, D_MODEL), SSD_D_INNER),
        "da_lambda_q1": 0.1 * jax.random.normal(next(ks), (DEPTH, DA_HEAD_DIM), f32),
        "da_lambda_k1": 0.1 * jax.random.normal(next(ks), (DEPTH, DA_HEAD_DIM), f32),
        "da_lambda_q2": 0.1 * jax.random.normal(next(ks), (DEPTH, DA_HEAD_DIM), f32),
        "da_lambda_k2": 0.1 * jax.random.normal(next(ks), (DEPTH, DA_HEAD_DIM), f32),
        "da_subln_g": gain(DA_V_DIM),
        "da_w_branch": nrm((DA_WIDTH, D_MODEL), DA_WIDTH),
        "w_out": nrm((D_MODEL, D_MODEL), D_MODEL),
        "mix_post_g": gain(D_MODEL),
        "ffn2_pre_g": gain(D_MODEL),
        "ffn2_w_gate": nrm((D_MODEL, D_FF), D_MODEL),
        "ffn2_w_up": nrm((D_MODEL, D_FF), D_MODEL),
        "ffn2_w_down": nrm((D_FF, D_MODEL), D_FF),
        "ffn2_post_g": gain(D_MODEL),
    }

def first_block(x, ffn1_pre_g, ffn1_w_gate, ffn1_w_up, ffn1_w_down, ffn1_post_g,
              mix_pre_g, w_in, gate_b,
              ssd_conv_w, ssd_conv_b, ssd_dt_bias, ssd_A_log, ssd_D, ssd_norm_g, ssd_w_branch,
              da_lambda_q1, da_lambda_k1, da_lambda_q2, da_lambda_k2, da_subln_g, da_w_branch,
              w_out, mix_post_g,
              ffn2_pre_g, ffn2_w_gate, ffn2_w_up, ffn2_w_down, ffn2_post_g):
    h = x
    b, L, _ = x.shape
    for l in range(DEPTH):
        lam_init = 0.8 - 0.6 * math.exp(-0.3 * l)
        h = h + 0.5 * rmsnorm(swiglu(rmsnorm(h, ffn1_pre_g[l]), ffn1_w_gate[l], ffn1_w_up[l], ffn1_w_down[l]),
                              ffn1_post_g[l])
        u = rmsnorm(h, mix_pre_g[l])
        z, xbc, dt_raw, q, k, v, gate_logits = jnp.split(u @ w_in[l], IN_SPLITS, axis=-1)
        y_ssd = ssd_branch(z, xbc, dt_raw, ssd_conv_w[l], ssd_conv_b[l], ssd_dt_bias[l], ssd_A_log[l],
                           ssd_D[l], ssd_norm_g[l], ssd_w_branch[l])
        y_att = diff_attn_branch(q, k, v, da_lambda_q1[l], da_lambda_k1[l], da_lambda_q2[l], da_lambda_k2[l],
                                 da_subln_g[l], da_w_branch[l], lam_init)
        gates = jax.nn.sigmoid(gate_logits + gate_b[l]).reshape(b, L, N_BRANCH, D_MODEL)
        merged = gates[:, :, 0] * y_ssd + gates[:, :, 1] * y_att
        h = h + rmsnorm(merged @ w_out[l], mix_post_g[l])
        h = h + 0.5 * rmsnorm(swiglu(rmsnorm(h, ffn2_pre_g[l]), ffn2_w_gate[l], ffn2_w_up[l], ffn2_w_down[l]),
                              ffn2_post_g[l])
    return h


GDN_HEADS = 8
GDN_DK = 128
GDN_DV = 128
GDN_CONV = 4
GDN_CHUNK = 64
DSA_HEADS = 8
DSA_KV_HEADS = 2
DSA_DH = 128
IDX_HEADS = 8
IDX_DIM = 64
TOPK_MAX = 256
FFN_CONV = 3

GDN_QK_W = GDN_HEADS * GDN_DK
GDN_V_W = GDN_HEADS * GDN_DV
GDN_CONV_CH = 2 * GDN_QK_W + GDN_V_W
DSA_Q_W = DSA_HEADS * DSA_DH
DSA_KV_W = DSA_KV_HEADS * DSA_DH
IDX_Q_W = IDX_HEADS * IDX_DIM
IN_SPLITS_2 = (GDN_CONV_CH, GDN_V_W, GDN_HEADS, GDN_HEADS,
             DSA_Q_W, DSA_KV_W, DSA_KV_W, IDX_Q_W, IDX_DIM, IDX_HEADS,
             D_MODEL, D_MODEL)
N_IN = GDN_CONV_CH + GDN_V_W + 2 * GDN_HEADS + DSA_Q_W + 2 * DSA_KV_W + IDX_Q_W + IDX_DIM + IDX_HEADS + 2 * D_MODEL


def rmsnorm_2(x, g):
    xf = x.astype(jnp.float32)
    y = xf * lax.rsqrt(jnp.mean(xf * xf, axis=-1, keepdims=True) + EPS)
    return (y * g.astype(jnp.float32)).astype(x.dtype)

def layernorm_nobias(x, g):
    xf = x.astype(jnp.float32)
    xc = xf - jnp.mean(xf, axis=-1, keepdims=True)
    y = xc * lax.rsqrt(jnp.mean(xc * xc, axis=-1, keepdims=True) + EPS)
    return (y * g.astype(jnp.float32)).astype(x.dtype)

def l2norm(x):
    xf = x.astype(jnp.float32)
    return xf * lax.rsqrt(jnp.sum(xf * xf, axis=-1, keepdims=True) + EPS)

def causal_dwconv_2(x, w):
    width, ch = w.shape
    return lax.conv_general_dilated(
        x, w[:, None, :].astype(x.dtype), window_strides=(1,),
        padding=[(width - 1, 0)], dimension_numbers=("NWC", "WIO", "NWC"),
        feature_group_count=ch)

def gated_delta_rule_chunked(q, k, v, g, beta):
    B, S, H, dk = q.shape
    dv = v.shape[-1]
    C = GDN_CHUNK
    N = S // C
    q = q * (dk ** -0.5)

    def chunks(t):
        return jnp.swapaxes(t.reshape((B, N, C) + t.shape[2:]), 2, 3)

    qc, kc, vc, gc, bc = chunks(q), chunks(k), chunks(v), chunks(g), chunks(beta)
    G = jnp.cumsum(gc, axis=-1)
    tri = jnp.tril(jnp.ones((C, C), dtype=bool))
    strict = jnp.tril(jnp.ones((C, C), dtype=bool), -1)
    gamma = jnp.exp(jnp.where(tri, G[..., :, None] - G[..., None, :], -jnp.inf))
    kb = kc * bc[..., None]
    A = jnp.where(strict, jnp.einsum("bnhid,bnhjd->bnhij", kb, kc) * gamma, 0.0)
    eye = jnp.eye(C, dtype=jnp.float32)
    T = lax.linalg.triangular_solve(A + eye, jnp.broadcast_to(eye, A.shape),
                                    left_side=True, lower=True)
    eG = jnp.exp(G)[..., None]
    u = jnp.einsum("bnhij,bnhje->bnhie", T, vc * bc[..., None])
    w = jnp.einsum("bnhij,bnhjd->bnhid", T, kb * eG)
    qg = qc * eG
    kd = kc * jnp.exp(G[..., -1:] - G)[..., None]
    att = jnp.einsum("bnhid,bnhjd->bnhij", qc, kc) * gamma
    dlast = jnp.exp(G[..., -1])

    def step(state, inp):
        u_i, w_i, qg_i, kd_i, att_i, dl_i = inp
        v_new = u_i - jnp.einsum("bhcd,bhde->bhce", w_i, state)
        o = jnp.einsum("bhcd,bhde->bhce", qg_i, state) + jnp.einsum("bhij,bhje->bhie", att_i, v_new)
        state = state * dl_i[..., None, None] + jnp.einsum("bhcd,bhce->bhde", kd_i, v_new)
        return state, o

    xs = (jnp.swapaxes(u, 0, 1), jnp.swapaxes(w, 0, 1), jnp.swapaxes(qg, 0, 1),
          jnp.swapaxes(kd, 0, 1), jnp.swapaxes(att, 0, 1), jnp.swapaxes(dlast, 0, 1))
    s0 = jnp.zeros((B, H, dk, dv), jnp.float32)
    _, o = lax.scan(step, s0, xs)
    return jnp.transpose(o, (1, 0, 3, 2, 4)).reshape(B, S, H, dv)

def dsa_sparse_attention(q, k, v, iq, ik, iw):
    B, S, Hq, dh = q.shape
    L, Hkv = k.shape[1], k.shape[2]
    k_top = min(TOPK_MAX, L // 4)
    rep = Hq // Hkv
    nb = S // Q_BLOCK
    key_pos = jnp.arange(L, dtype=jnp.int32)
    starts = jnp.arange(nb, dtype=jnp.int32) * Q_BLOCK
    iw = iw * ((IDX_HEADS ** -0.5) * (IDX_DIM ** -0.5))

    def blocks(t):
        return jnp.swapaxes(t.reshape((B, nb, Q_BLOCK) + t.shape[2:]), 0, 1)

    def one_block(args):
        q_b, iq_b, iw_b, start = args
        t_pos = start + jnp.arange(Q_BLOCK, dtype=jnp.int32)
        causal = key_pos[None, :] <= t_pos[:, None]
        rel = jax.nn.relu(jnp.einsum("bqhd,bsd->bqhs", iq_b, ik))
        score = jnp.einsum("bqh,bqhs->bqs", iw_b, rel).astype(jnp.float32)
        score = jnp.where(causal[None], score, -jnp.inf)
        _, idx = lax.top_k(score, k_top)
        valid = idx <= t_pos[None, :, None]
        k_sel = jax.vmap(lambda kb, ib: kb[ib])(k, idx)
        v_sel = jax.vmap(lambda vb, ib: vb[ib])(v, idx)
        qg = q_b.reshape(B, Q_BLOCK, Hkv, rep, dh)
        logits = jnp.einsum("bqgrd,bqkgd->bqgrk", qg, k_sel).astype(jnp.float32) * (dh ** -0.5)
        logits = jnp.where(valid[:, :, None, None, :], logits, -jnp.inf)
        p = jax.nn.softmax(logits, axis=-1).astype(v.dtype)
        o = jnp.einsum("bqgrk,bqkgd->bqgrd", p, v_sel)
        return o.reshape(B, Q_BLOCK, Hq * dh)

    out = lax.map(one_block, (blocks(q), blocks(iq), blocks(iw), starts))
    return jnp.swapaxes(out, 0, 1).reshape(B, S, Hq * dh)

def second_inputs(seed: int = 0) -> dict:
    key = jax.random.key(seed)
    ks = jax.random.split(key, 16)
    f32 = jnp.float32

    def nrm(k, shape, scale):
        return jax.random.normal(k, shape, f32) * scale

    x = nrm(ks[0], (BATCH, SEQ, D_MODEL), 1.0)
    norm1_g = 1.0 + nrm(ks[1], (DEPTH, D_MODEL), 0.02)
    w_in = nrm(ks[2], (DEPTH, D_MODEL, N_IN), D_MODEL ** -0.5)
    gdn_conv_w = nrm(ks[3], (DEPTH, GDN_CONV, GDN_CONV_CH), GDN_CONV ** -0.5)
    gdn_a_log = jnp.log(jax.random.uniform(ks[4], (DEPTH, GDN_HEADS), f32, 1.0, 16.0))
    dt = jnp.exp(jax.random.uniform(ks[5], (DEPTH, GDN_HEADS), f32, math.log(1e-3), math.log(1e-1)))
    gdn_dt_bias = dt + jnp.log(-jnp.expm1(-dt))
    gdn_norm_g = 1.0 + nrm(ks[6], (DEPTH, GDN_DV), 0.02)
    idx_k_norm_g = 1.0 + nrm(ks[7], (DEPTH, IDX_DIM), 0.02)
    branch_gate_b = nrm(ks[8], (DEPTH, 2 * D_MODEL), 0.02)
    w_out = nrm(ks[9], (DEPTH, D_MODEL, D_MODEL), D_MODEL ** -0.5)
    norm2_g = 1.0 + nrm(ks[10], (DEPTH, D_MODEL), 0.02)
    ffn_w_up = nrm(ks[11], (DEPTH, D_MODEL, 2 * D_FF), D_MODEL ** -0.5)
    ffn_conv_w = nrm(ks[12], (DEPTH, FFN_CONV, 2 * D_FF), FFN_CONV ** -0.5)
    ffn_conv_b = nrm(ks[13], (DEPTH, 2 * D_FF), 0.02)
    ffn_w_down = nrm(ks[14], (DEPTH, D_FF, D_MODEL), D_FF ** -0.5)
    final_g = 1.0 + nrm(ks[15], (D_MODEL,), 0.02)
    return {"x": x, "norm1_g": norm1_g, "w_in": w_in, "gdn_conv_w": gdn_conv_w,
            "gdn_a_log": gdn_a_log, "gdn_dt_bias": gdn_dt_bias, "gdn_norm_g": gdn_norm_g,
            "idx_k_norm_g": idx_k_norm_g, "branch_gate_b": branch_gate_b, "w_out": w_out,
            "norm2_g": norm2_g, "ffn_w_up": ffn_w_up, "ffn_conv_w": ffn_conv_w,
            "ffn_conv_b": ffn_conv_b, "ffn_w_down": ffn_w_down, "final_g": final_g}

def second_block(x, norm1_g, w_in, gdn_conv_w, gdn_a_log, gdn_dt_bias, gdn_norm_g,
              idx_k_norm_g, branch_gate_b, w_out, norm2_g, ffn_w_up, ffn_conv_w,
              ffn_conv_b, ffn_w_down, final_g):
    B, S, _ = x.shape
    offsets = [int(o) for o in np.cumsum(IN_SPLITS_2)[:-1]]
    h = x
    for l in range(DEPTH):
        u = rmsnorm_2(h, norm1_g[l])
        proj = jnp.einsum("bsd,de->bse", u, w_in[l])
        (g_qkv, g_z, g_a, g_b, d_q, d_k, d_v, i_q, i_k, i_w, gate_a, gate_b) = jnp.split(proj, offsets, axis=-1)

        qkv = jax.nn.silu(causal_dwconv_2(g_qkv, gdn_conv_w[l]))
        gq, gk, gv = jnp.split(qkv, [GDN_QK_W, 2 * GDN_QK_W], axis=-1)
        gq = l2norm(gq.reshape(B, S, GDN_HEADS, GDN_DK))
        gk = l2norm(gk.reshape(B, S, GDN_HEADS, GDN_DK))
        gv = gv.reshape(B, S, GDN_HEADS, GDN_DV).astype(jnp.float32)
        beta = jax.nn.sigmoid(g_b.astype(jnp.float32))
        logdecay = -jnp.exp(gdn_a_log[l].astype(jnp.float32)) * jax.nn.softplus(
            g_a.astype(jnp.float32) + gdn_dt_bias[l].astype(jnp.float32))
        o_gdn = gated_delta_rule_chunked(gq, gk, gv, logdecay, beta)
        z = g_z.reshape(B, S, GDN_HEADS, GDN_DV).astype(jnp.float32)
        o_gdn = (rmsnorm_2(o_gdn, gdn_norm_g[l]) * jax.nn.silu(z)).reshape(B, S, GDN_V_W).astype(x.dtype)

        o_dsa = dsa_sparse_attention(
            d_q.reshape(B, S, DSA_HEADS, DSA_DH),
            d_k.reshape(B, S, DSA_KV_HEADS, DSA_DH),
            d_v.reshape(B, S, DSA_KV_HEADS, DSA_DH),
            i_q.reshape(B, S, IDX_HEADS, IDX_DIM),
            layernorm_nobias(i_k, idx_k_norm_g[l]),
            i_w)

        gb = branch_gate_b[l]
        mixed = (jax.nn.sigmoid(gate_a + gb[:D_MODEL]) * o_gdn
                 + jax.nn.sigmoid(gate_b + gb[D_MODEL:]) * o_dsa)
        h = h + jnp.einsum("bse,ed->bsd", mixed, w_out[l])

        hn = rmsnorm_2(h, norm2_g[l])
        up = causal_dwconv_2(jnp.einsum("bsd,df->bsf", hn, ffn_w_up[l]), ffn_conv_w[l]) + ffn_conv_b[l]
        f_gate, f_val = jnp.split(up, [D_FF], axis=-1)
        h = h + jnp.einsum("bsf,fd->bsd", jax.nn.silu(f_gate) * f_val, ffn_w_down[l])
    return rmsnorm_2(h, final_g)


def setup_inputs(seed=0):
    out = dict(first_inputs(seed))
    for name, value in second_inputs(seed + 1).items():
        if name != "x":
            out[name + "_2"] = value
    return out


def reference(
    x, ffn1_pre_g, ffn1_w_gate, ffn1_w_up, ffn1_w_down, ffn1_post_g, mix_pre_g, w_in, gate_b,
    ssd_conv_w, ssd_conv_b, ssd_dt_bias, ssd_A_log, ssd_D, ssd_norm_g, ssd_w_branch,
    da_lambda_q1, da_lambda_k1, da_lambda_q2, da_lambda_k2, da_subln_g, da_w_branch, w_out,
    mix_post_g, ffn2_pre_g, ffn2_w_gate, ffn2_w_up, ffn2_w_down, ffn2_post_g, norm1_g_2, w_in_2,
    gdn_conv_w_2, gdn_a_log_2, gdn_dt_bias_2, gdn_norm_g_2, idx_k_norm_g_2, branch_gate_b_2,
    w_out_2, norm2_g_2, ffn_w_up_2, ffn_conv_w_2, ffn_conv_b_2, ffn_w_down_2, final_g_2,
):
    x = first_block(
        x, ffn1_pre_g, ffn1_w_gate, ffn1_w_up, ffn1_w_down, ffn1_post_g, mix_pre_g, w_in,
        gate_b, ssd_conv_w, ssd_conv_b, ssd_dt_bias, ssd_A_log, ssd_D, ssd_norm_g, ssd_w_branch,
        da_lambda_q1, da_lambda_k1, da_lambda_q2, da_lambda_k2, da_subln_g, da_w_branch, w_out,
        mix_post_g, ffn2_pre_g, ffn2_w_gate, ffn2_w_up, ffn2_w_down, ffn2_post_g,
    )
    return second_block(
        x, norm1_g_2, w_in_2, gdn_conv_w_2, gdn_a_log_2, gdn_dt_bias_2, gdn_norm_g_2,
        idx_k_norm_g_2, branch_gate_b_2, w_out_2, norm2_g_2, ffn_w_up_2, ffn_conv_w_2,
        ffn_conv_b_2, ffn_w_down_2, final_g_2,
    )


_drawn_inputs = setup_inputs


def setup_inputs(seed=0):
    import zlib

    import numpy as np

    out = dict(_drawn_inputs(seed))
    spreads = {}
    factors = {'gate_b': 7.844,
     'ssd_conv_b': 3.274,
     'ffn2_post_g': 2.987,
     'norm1_g_2': 5.691,
     'gdn_norm_g_2': 8.0,
     'idx_k_norm_g_2': 8.0,
     'branch_gate_b_2': 8.0,
     'norm2_g_2': 15.345,
     'ffn_conv_b_2': 29.912,
     'final_g_2': 23.83}
    for name, (base, spread) in spreads.items():
        noise = np.random.default_rng([zlib.crc32(name.encode()), seed]).standard_normal(out[name].shape)
        drawn = base * np.exp(spread * noise) if base else spread * noise
        out[name] = __import__('jax').numpy.asarray(drawn.astype(out[name].dtype))
    for name, factor in factors.items():
        out[name] = (out[name] * factor).astype(out[name].dtype)
    return out
```

```python
from contextlib import ExitStack

import numpy as np

import concourse.bass as bass
from concourse import mybir

F = mybir.dt.float32
R = mybir.dt.float32r
ALU = mybir.AluOpType
ACT = mybir.ActivationFunctionType
AX = mybir.AxisListType

L = 512
T4 = 4
KB = 8
FB = 22
NRAW = 3
NHL = 3
EPS = 1e-6
NEGBIG = -1.0e30
LAM_INIT = 0.2

PCOLS = {}


def _layout():
    at = 0
    for name, n in (
        ("ffn1_pre", 8), ("ffn1_post", 8), ("mix_pre", 8), ("gate_b", 16), ("conv_w", 96), ("conv_b", 24),
        ("norm_g", 16), ("subln", 1), ("mix_post", 8), ("ffn2_pre", 8), ("ffn2_post", 8),
        ("dt_bias", 1), ("a_log", 1), ("D", 32), ("lam", 256),
        ("norm1", 8), ("gconv_w", 96), ("g_bias", 1), ("g_alog", 1), ("gnorm", 1), ("ikg", 1), ("bgb", 16),
        ("norm2", 8), ("fconv_w", 132), ("fconv_b", 44), ("final", 8),
    ):
        PCOLS[name] = (at, n)
        at += n
    return at


NPAR = _layout()
CCOLS = {"ident": (0, 128), "ssdmask": (128, 128), "dist": (256, 512), "reset128": (768, 512),
         "neg": (128, 128), "bdincl": (256, 128), "level": (384, 768), "reset64": (1152, 512)}
NCA, NCB = 1280, 1664


class Tok:
    __slots__ = ("eng", "used", "val")

    def __init__(self, eng):
        self.eng, self.used, self.val = eng, False, 0


class Call:
    __slots__ = ("fn", "a", "k", "inc")

    def __init__(self, fn, a, k):
        self.fn, self.a, self.k, self.inc = fn, a, k, None

    def then_inc(self, sem, n):
        self.inc = (sem, n)
        return self

    def issue(self):
        ins = self.fn(*self.a, **self.k)
        if self.inc is not None:
            ins.then_inc(*self.inc)
        return ins


class Ops:

    def __init__(self, eng):
        self.eng = eng

    def dma_start(self, *a, **k):
        return Call(self.eng.dma_start, a, k)

    def matmul(self, *a, **k):
        return Call(self.eng.matmul, a, k)

    def transpose(self, *a, **k):
        return Call(self.eng.transpose, a, k)

    def activation(self, *a, **k):
        return Call(self.eng.activation, a, k)

    def copy(self, *a, **k):
        return Call(self.eng.copy, a, k)

    def mul(self, *a, **k):
        return Call(self.eng.mul, a, k)

    def memset(self, *a, **k):
        return Call(self.eng.memset, a, k)

    def tensor_copy(self, *a, **k):
        return Call(self.eng.tensor_copy, a, k)

    def tensor_tensor(self, *a, **k):
        return Call(self.eng.tensor_tensor, a, k)

    def tensor_scalar(self, *a, **k):
        return Call(self.eng.tensor_scalar, a, k)

    def scalar_tensor_tensor(self, *a, **k):
        return Call(self.eng.scalar_tensor_tensor, a, k)

    def tensor_tensor_scan(self, *a, **k):
        return Call(self.eng.tensor_tensor_scan, a, k)

    def reciprocal(self, *a, **k):
        return Call(self.eng.reciprocal, a, k)

    def reduce_max(self, *a, **k):
        return Call(self.eng.reduce_max, a, k)

    def reduce_sum(self, *a, **k):
        return Call(self.eng.reduce_sum, a, k)

    def max(self, *a, **k):
        return Call(self.eng.max, a, k)

    def match_replace(self, *a, **k):
        return Call(self.eng.match_replace, a, k)

class Queue:

    def __init__(self, name, eng):
        self.name, self.e, self.ops = name, Ops(eng), []

    def __call__(self, fn, *deps):
        t = Tok(self)
        self.ops.append([fn(self.e), deps, t])
        return t

    def later(self):
        t = Tok(self)
        op = [None, (), t]
        self.ops.append(op)
        return op


def flat(deps, out):
    for d in deps:
        if d is None:
            continue
        if isinstance(d, list) or (isinstance(d, tuple) and not (len(d) == 2 and isinstance(d[1], int))):
            flat(d, out)
        else:
            out.append(d)
    return out


class Pages:

    def __init__(self, bufs, name):
        self.free = [(b, []) for b in bufs]
        self.name = name
        self.low = len(bufs)

    def take(self):
        if not self.free:
            raise RuntimeError("out of " + self.name)
        b, w = self.free.pop(0)
        self.low = min(self.low, len(self.free))
        return Page(b, w, self)


class Page:
    __slots__ = ("b", "w", "pool", "t")

    def __init__(self, b, w, pool):
        self.b, self.w, self.pool, self.t = b, w, pool, None

    def __getitem__(self, k):
        return self.b[k]

    def release(self, *toks):
        self.pool.free.append((self.b, list(toks)))


def build(nc, d, out):
    SP, PE, AC = Queue("sp", nc.sync), Queue("pe", nc.tensor), Queue("act", nc.scalar)
    DV, GP = Queue("dve", nc.vector), Queue("pool", nc.gpsimd)
    ctx = ExitStack()
    sems = {}

    def sem(name):
        if name not in sems:
            sems[name] = ctx.enter_context(nc.semaphore("s_" + name))
        return sems[name]

    def sb(stack, name, shape, dt=F):
        return stack.enter_context(nc.sbuf_tensor(name, shape, dt))

    par = sb(ctx, "par", [128, NPAR])
    onesc = sb(ctx, "onesc", [128, 4, 128])
    small = sb(ctx, "small", [128, 1024])
    hT = sb(ctx, "hT", [128, KB, L])
    raw = [sb(ctx, f"raw{i}", [128, KB * 128]) for i in range(NRAW)]
    hl = [sb(ctx, f"hl{i}", [128, 2, KB * 128], R) for i in range(NHL)]
    uR = sb(ctx, "uR", [128, 2, KB, L], R)
    NA = 10
    fA = sb(ctx, "fA", [128, NA, L])
    banks = [ctx.enter_context(nc.psum_tensor(f"bank{i}", [128, L], F)) for i in range(8)]
    MB = Pages([b for b in banks[:3]], "main banks")
    SB = Pages([b for b in banks[3:]], "side banks")
    fp = Pages([fA[:, i, :] for i in range(NA)], "fA")

    def pc(name, j=0, n=1, rows=slice(0, 128)):
        a = PCOLS[name][0] + j
        return par[rows, a:a + n]

    def cc(name, rows=slice(0, 128)):
        a, n = CCOLS[name]
        return con[rows, a:a + n]

    small_at = [0]

    def sm(n):
        a = small_at[0]
        small_at[0] += n
        assert small_at[0] <= 1024, "small"
        return small[:, a:a + n]

    SP(lambda e: e.dma_start(par[:, :], d["params"]).then_inc(sem("p"), 16))
    for k in range(KB):
        SP(lambda e, k=k: e.dma_start(hT[:, k, :], d["xT"][k * 128:(k + 1) * 128, :]).then_inc(sem(f"x{k % 4}"), 16))
    t_par = ("p", 16)
    t_h = [(f"x{k % 4}", 16 * (k // 4 + 1)) for k in range(KB)]
    t_ones = [GP(lambda e, i=i, v=v: e.memset(onesc[:, i, :], v))
              for i, v in enumerate((1.0 / 1024, 1.0 / 512, 1.0 / 128, 1.0))]
    O1024, O512, O128, O1 = range(4)

    stream = {"n": 0, "late": {}, "done": {}, "split": {}}

    def reserve(j):
        a, v = AC.later(), DV.later()
        stream["late"][j] = (a, v)

    for j in range(NHL - 1):
        reserve(j)

    def panel(src, width):
        j = stream["n"]
        stream["n"] += 1
        a, v = stream["late"].pop(j)
        rs, hs = raw[j % NRAW], hl[j % NHL]
        landed = (f"raw{j % NRAW}", 16 * (j // NRAW + 1))
        SP(lambda e: e.dma_start(rs[:, 0:width], src).then_inc(sem(f"raw{j % NRAW}"), 16),
           stream["split"].get(j - NRAW))
        a[0] = AC.e.copy(hs[:, 0, 0:width], rs[:, 0:width])
        a[1] = (landed, stream["done"].get(j - NHL))
        v[0] = DV.e.tensor_tensor(hs[:, 1, 0:width], rs[:, 0:width], hs[:, 0, 0:width].bitcast(F), ALU.subtract)
        v[1] = (landed, a[2], stream["done"].get(j - NHL))
        stream["split"][j] = (v[2], a[2])
        reserve(j + NHL - 1)
        return j, hs, (a[2], v[2])

    def matpanel(bank, bw, p, kbs, kfirst, xhi, xlo, tx, first, last, off=0):
        j, hs, tw = p
        tok = None
        for q in range(kbs):
            k = kfirst + q
            w = slice((off + q) * 128, (off + q + 1) * 128)
            for i, (wi, x) in enumerate(((0, xhi), (0, xlo), (1, xhi))):
                st = first and q == 0 and i == 0
                sp_ = last and q == kbs - 1 and i == 2
                tok = PE(lambda e, wi=wi, w=w, x=x(k), st=st, sp_=sp_:
                         e.matmul(bank[:, :], hs[:, wi, w], x, start=st, stop=sp_),
                         tw, tx(k), bw if st else None)
        stream["done"][j] = tok
        return tok

    def gemm(src, xhi, xlo, tx):
        b = MB.take()
        t = matpanel(b, b.w, panel(src, KB * 128), KB, 0, xhi, xlo, tx, True, True)
        return b, t

    t_u = [None] * KB
    t_ulast = []

    def uhi(k):
        return uR[:, 0, k, :]

    def ulo(k):
        return uR[:, 1, k, :]

    def tu(k):
        return t_u[k]

    def ugemm(src):
        b, t = gemm(src, uhi, ulo, tu)
        t_ulast[:] = [t]
        return b, t

    def rstd_of(bank, tok, eps=EPS):
        r = fp.take()
        s = AC(lambda e: e.activation(r[:, :], bank[:, :], ACT.Sqrt, bias=epsc), tok, r.w, t_eps)
        r.t = DV(lambda e: e.reciprocal(r[:, :], r[:, :]), s)
        bank.release(s)
        return r

    def sumsq(bank, wait, sources, which):
        t = None
        n = len(sources)
        for i, (x, tx) in enumerate(sources):
            q = fp.take()
            s = AC(lambda e, x=x, q=q: e.activation(q[:, :], x, ACT.Square), tx, q.w)
            t = PE(lambda e, q=q, i=i: e.matmul(bank[:, :], onesc[:, which, :], q[:, :], start=i == 0, stop=i == n - 1),
                   s, t_ones[which], wait if i == 0 else None)
            q.release(t)
        return t

    def split(hi, lo, x, tx, whi):
        a = AC(lambda e: e.copy(hi, x), tx, whi)
        v = DV(lambda e: e.tensor_tensor(lo, x, hi.bitcast(F), ALU.subtract), a, tx, whi)
        return (a, v)

    def norm_u(gname):
        b = SB.take()
        t = sumsq(b, b.w, [(hT[:, k, :], t_h[k]) for k in range(KB)], O1024)
        r = rstd_of(b, t)
        last = list(t_ulast)
        for k in range(KB):
            x = fp.take()
            v = DV(lambda e, k=k, x=x: e.scalar_tensor_tensor(out=x[:, :], in0=hT[:, k, :], scalar=pc(gname, k), in1=r[:, :],
                                                            op0=ALU.mult, op1=ALU.mult), t_h[k], r.t, x.w, t_par)
            t_u[k] = split(uhi(k), ulo(k), x[:, :], v, last)
            x.release(t_u[k])
        r.release(v)

    def post_norm(y, gn, half):
        b = SB.take()
        t = sumsq(b, b.w, [(y[k][:, :], y[k].t) for k in range(KB)], O1024)
        r = rstd_of(b, t)
        for k in range(KB):
            v = DV(lambda e, k=k: e.scalar_tensor_tensor(out=y[k][:, :], in0=y[k][:, :], scalar=pc(gn, k), in1=r[:, :],
                                                       op0=ALU.mult, op1=ALU.mult), y[k].t, t, r.t, t_par)
            v = DV(lambda e, k=k: e.scalar_tensor_tensor(out=hT[:, k, :], in0=y[k][:, :], scalar=0.5 if half else 1.0,
                                                       in1=hT[:, k, :], op0=ALU.mult, op1=ALU.add), v, t_h[k], t_u[k])
            t_h[k] = v
            y[k].release(v)
        r.release(t_h[KB - 1])

    def down(src, act, tact):
        for m in range(KB):
            b = MB.take()
            at = 0
            for n in (8, 8, 6):
                t = matpanel(b, b.w, panel(src[m, :, at * 128:(at + n) * 128], n * 128), n, at,
                             lambda k: act[:, 0, k, :], lambda k: act[:, 1, k, :], lambda k: tact[k],
                             at == 0, at + n == FB)
                at += n
            yield m, b, t

    def ffn(wg, wu, wd, gpre, gpost, act, wait):
        norm_u(gpre)
        tact = []
        for j in range(FB):
            bg, tg = ugemm(wg[j])
            s = fp.take()
            a = AC(lambda e, s=s, bg=bg: e.activation(s[:, :], bg[:, :], ACT.Silu), tg, s.w)
            bg.release(a)
            bu, tu_ = ugemm(wu[j])
            v = DV(lambda e, s=s, bu=bu: e.tensor_tensor(s[:, :], s[:, :], bu[:, :], ALU.mult), a, tu_)
            bu.release(v)
            tk = split(act[:, 0, j, :], act[:, 1, j, :], s[:, :], v, wait)
            s.release(tk)
            tact.append(tk)
        y = []
        for m, b, t in down(wd, act, tact):
            p = fp.take()
            p.t = AC(lambda e, p=p, b=b: e.copy(p[:, :], b[:, :]), t, p.w)
            b.release(p.t)
            y.append(p)
        post_norm(y, gpost, True)
        return t

    def conv(b, tb, wname, taps, col, ncol, bias, page):
        def w(i):
            return pc(wname, i * ncol + col)
        if bias is None:
            t = AC(lambda e: e.activation(page[:, :], b[:, :], ACT.Identity, scale=w(taps - 1)), tb, page.w, t_par)
        else:
            t = AC(lambda e: e.activation(page[:, :], b[:, :], ACT.Identity, scale=w(taps - 1), bias=pc(bias, col)),
                   tb, page.w, t_par)
        for s in range(1, taps):
            t = DV(lambda e, s=s: e.scalar_tensor_tensor(out=page[:, s:L], in0=b[:, 0:L - s], scalar=w(taps - 1 - s),
                                                       in1=page[:, s:L], op0=ALU.mult, op1=ALU.add), t)
        b.release(t)
        page.t = t
        return t

    def convsilu(b, tb, wname, col, bias):
        p = fp.take()
        t = conv(b, tb, wname, 4, col, 24, bias, p)
        p.t = AC(lambda e: e.activation(p[:, :], p[:, :], ACT.Silu), t)
        return p

    def turn(dst_bank, wait, src, tsrc, n=T4, cols=128):
        for t in range(n):
            tok = PE(lambda e, t=t: e.transpose(dst_bank[:, t * 128:(t + 1) * 128], src[:, t * 128:(t + 1) * 128], ident),
                     tsrc, wait, t_con)
        return tok

    def softplus(x, tx, rows):
        e1, w = fp.take(), fp.take()
        c = (rows, slice(0, L))
        t = DV(lambda e: e.scalar_tensor_tensor(out=e1[c], in0=x[c], scalar=-1.0, in1=x[c], op0=ALU.mult, op1=ALU.max), tx, e1.w)
        t = AC(lambda e: e.activation(e1[c], e1[c], ACT.Exp, scale=-1.0), t)
        ln = fp.take()
        tw = DV(lambda e: e.tensor_scalar(w[c], e1[c], 1.0, None, ALU.add), t, w.w)
        tl = AC(lambda e: e.activation(ln[c], w[c], ACT.Ln), tw, ln.w)
        t2 = DV(lambda e: e.scalar_tensor_tensor(out=e1[c], in0=w[c], scalar=-1.0, in1=e1[c], op0=ALU.add, op1=ALU.subtract), tw, t)
        t3 = DV(lambda e: e.reciprocal(w[c], w[c]), t2, tl)
        t4 = DV(lambda e: e.tensor_tensor(e1[c], e1[c], w[c], ALU.mult), t3, t2)
        t5 = DV(lambda e: e.tensor_tensor(ln[c], ln[c], e1[c], ALU.subtract), t4, tl)
        t6 = DV(lambda e: e.scalar_tensor_tensor(out=x[c], in0=x[c], scalar=0.0, in1=ln[c], op0=ALU.max, op1=ALU.add), t5)
        e1.release(t5)
        w.release(t4)
        ln.release(t6)
        return t6

    def finish(gen):
        for _ in gen:
            pass

    def interleave(main, side, nside, nmain):
        due = 0.0
        for _ in main:
            due += nside / nmain
            while due >= 1:
                due -= 1
                next(side, None)
        finish(side)

    def drop_pages():
        assert len(fp.free) == NA + NB_ and len(rp.free) == 16, (len(fp.free), len(rp.free))
        toks = [w for _, w in fp.free] + [w for _, w in rp.free]
        fp.free = [(fA[:, i, :], toks) for i in range(NA)]
        return toks

    def pv(P, W, i, V, ob):
        b = SB.take()
        for k in range(i + 1):
            tp = PE(lambda e, k=k: e.transpose(b[:, k * 128:(k + 1) * 128], P[:, k * 128:(k + 1) * 128], ident), P.t, b.w)
        P.release(tp)
        A = fp.take()
        a = AC(lambda e: e.copy(A[:, 0:W], b[:, 0:W]), tp, A.w)
        b.release(a)
        for k in range(i + 1):
            t = PE(lambda e, k=k: e.matmul(ob[:, i * 128:(i + 1) * 128], V[:, k * 128:(k + 1) * 128], A[:, k * 128:(k + 1) * 128],
                                         start=k == 0, stop=k == i), a, V.t, ob.w)
        A.release(t)
        return t

    epsc = sm(1)
    t_eps = DV(lambda e: e.memset(epsc, EPS))

    with ExitStack() as ph:
        act = sb(ph, "act1", [128, 2, FB, L], R)
        t_phase = ffn(d["w1g"], d["w1u"], d["w1d"], "ffn1_pre", "ffn1_post", act, None)

    stop = d.get("stop", 99)
    if stop >= 2:
      with ExitStack() as ph:
        con = sb(ph, "con1", [128, NCA])
        t_con = ("c1", 16)
        SP(lambda e: e.dma_start(con[:, :], d["consts1"]).then_inc(sem("c1"), 16), t_phase)
        ident = con[:, 0:128]
        SSDMASK = cc("ssdmask")
        mR = sb(ph, "mR1", [128, 16, L], R)
        NB_ = 25
        fB = sb(ph, "fB1", [128, NB_, L])
        for i in range(NB_):
            fp.free.append((fB[:, i, :], [t_phase]))
        rp = Pages([mR[:, i, :] for i in range(16)], "R pages")
        for i in range(16):
            rp.free[i] = (rp.free[i][0], [t_phase])
        acN, alast, cdec, ea, ddec = sm(128), sm(128), sm(128), sm(128), sm(128)
        dtN = sm(128)

        def n3(x):
            return x.rearrange("p (t h) -> p t h", t=T4)

        norm_u("mix_pre")
        WIN = d["win"]
        acum = {}

        def decay_side(dt):
            t = softplus(dt, dt.t, slice(0, 32))
            aex = sm(1)
            ta = AC(lambda e: e.activation(aex[0:32, :], pc("a_log", rows=slice(0, 32)), ACT.Exp), t_par)
            a, ac = fp.take(), fp.take()
            t1 = DV(lambda e: e.tensor_scalar(a[0:32, :], dt[0:32, :], aex[0:32, :], -1.0, ALU.mult, ALU.mult), t, ta, a.w)
            t2 = DV(lambda e: e.tensor_tensor_scan(ac[0:32, :], con[0:32, CCOLS["reset128"][0]:CCOLS["reset128"][0] + L],
                                                 a[0:32, :], 0.0, ALU.mult, ALU.add), t1, ac.w, t_con)
            a.release(t2)
            b = SB.take()
            for q in range(T4):
                PE(lambda e, q=q: e.transpose(b[:, q * 32:q * 32 + 32], ac[0:32, q * 128:(q + 1) * 128], con[0:32, 0:32]), t2, b.w)
            for q in range(T4):
                PE(lambda e, q=q: e.transpose(b[:, 128 + q * 32:160 + q * 32], dt[0:32, q * 128:(q + 1) * 128], con[0:32, 0:32]), t)
            for q in range(T4):
                lst = ac[0:32, q * 128 + 127:q * 128 + 128]
                tp = PE(lambda e, q=q, lst=lst: e.matmul(b[:, 256 + q * 32:288 + q * 32], lst.broadcast_to([32, 128]), con[0:32, 0:32],
                                              start=True, stop=True))
            t3 = DV(lambda e: e.tensor_copy(acN, b[:, 0:128]), tp)
            t4 = DV(lambda e: e.tensor_copy(dtN, b[:, 128:256]), tp)
            t5 = DV(lambda e: e.tensor_copy(alast, b[:, 256:384]), tp)
            b.release(t5)
            t6 = AC(lambda e: e.activation(cdec, alast, ACT.Exp), t5)
            t7 = AC(lambda e: e.activation(ea, acN, ACT.Exp), t3)
            t8 = DV(lambda e: e.tensor_tensor(ddec, alast, acN, ALU.subtract), t5, t3)
            t9 = AC(lambda e: e.activation(ddec, ddec, ACT.Exp), t8)
            dt.release(tp)
            acum.update(ac=ac, t=t2, tn=(t3, t4, t5, t6, t7, t9), users=[tp])

        grp = [dict() for _ in range(4)]

        def project_group(g):
            G = grp[g]
            xs = []
            for i in range(4):
                b, t = ugemm(WIN[16 + 4 * g + i])
                xs.append(convsilu(b, t, "conv_w", 4 * g + i, "conv_b"))
                yield
            b, t = ugemm(WIN[32 + g])
            G["B"] = convsilu(b, t, "conv_w", 16 + g, "conv_b")
            yield
            b, t = ugemm(WIN[36 + g])
            G["C"] = convsilu(b, t, "conv_w", 20 + g, "conv_b")
            G["xs"] = xs
            yield

        def project_dt():
            b, t = ugemm(WIN[80])
            dt = fp.take()
            dt.t = DV(lambda e: e.tensor_scalar(dt[0:32, :], b[0:32, :], pc("dt_bias", rows=slice(0, 32)), None, ALU.add),
                      t, dt.w, t_par)
            b.release(dt.t)
            yield
            decay_side(dt)
            yield

        def ssd_core(g):
            G = grp[g]
            xs, B, C = G["xs"], G["B"], G["C"]
            xsN, Xd = [], []
            hs = slice(8 * g, 8 * g + 8)
            tn = acum["tn"]
            for t in range(T4):
                b = SB.take()
                for i in range(4):
                    tp = PE(lambda e, i=i, t=t: e.transpose(b[:, i * 128:(i + 1) * 128], xs[i][:, t * 128:(t + 1) * 128], ident),
                            xs[i].t, b.w)
                y, x = fp.take(), fp.take()
                Db = pc("D", 8 * g, 8)[:, :, None].broadcast_to([128, 8, 64])
                v1 = DV(lambda e, b=b, x=x, t=t: e.tensor_tensor(
                    x[:, :].rearrange("p (h q) -> p h q", q=64), b[:, :].rearrange("p (h q) -> p h q", q=64),
                    n3(dtN)[:, t, hs][:, :, None].broadcast_to([128, 8, 64]), ALU.mult), tp, tn, x.w)
                v2 = DV(lambda e, b=b, y=y, Db=Db: e.tensor_tensor(
                    y[:, :].rearrange("p (h q) -> p h q", q=64), b[:, :].rearrange("p (h q) -> p h q", q=64), Db, ALU.mult),
                    tp, y.w)
                b.release(v1, v2)
                x.t, y.t = v1, v2
                xsN.append(y)
                Xd.append(x)
                yield
            for p in xs:
                p.release(tp)
            Y = xsN
            b = SB.take()
            tp = turn(b, b.w, B, B.t)
            BN = fp.take()
            BN.t = AC(lambda e: e.copy(BN[:, :], b[:, :]), tp, BN.w)
            b.release(BN.t)
            b = SB.take()
            for t in range(T4):
                c = slice(t * 128, (t + 1) * 128)
                tc = PE(lambda e, c=c: e.matmul(b[:, c], B[:, c], C[:, c], start=True, stop=True), B.t, C.t, b.w)
            B.release(tc)
            CB = fp.take()
            m = SSDMASK[:, None, :].broadcast_to([128, T4, 128])
            CB.t = DV(lambda e: e.tensor_tensor(CB[:, :].rearrange("p (t l) -> p t l", t=T4),
                                              b[:, :].rearrange("p (t l) -> p t l", t=T4), m, ALU.mult), tc, CB.w)
            b.release(CB.t)
            yield
            prev = None
            for t in range(1, T4):
                xd = fp.take()
                v = DV(lambda e, t=t, xd=xd: e.tensor_tensor(
                    xd[:, :].rearrange("p (h q) -> p h q", q=64), Xd[t - 1][:, :].rearrange("p (h q) -> p h q", q=64),
                    n3(ddec)[:, t - 1, hs][:, :, None].broadcast_to([128, 8, 64]), ALU.mult), Xd[t - 1].t, xd.w, tn)
                b = SB.take()
                ts = PE(lambda e, t=t, xd=xd, b=b: e.matmul(b[:, :], BN[:, (t - 1) * 128:t * 128], xd[:, :], start=True, stop=True),
                        v, BN.t, b.w)
                xd.release(ts)
                new = fp.take()
                if prev is None:
                    new.t = AC(lambda e, new=new, b=b: e.copy(new[:, :], b[:, :]), ts, new.w)
                else:
                    v = DV(lambda e, t=t, new=new, prev=prev: e.tensor_tensor(
                        new[:, :].rearrange("p (h q) -> p h q", q=64), prev[:, :].rearrange("p (h q) -> p h q", q=64),
                        n3(cdec)[:, t - 1, hs][:, :, None].broadcast_to([128, 8, 64]), ALU.mult), prev.t, new.w)
                    new.t = DV(lambda e, new=new, b=b: e.tensor_tensor(new[:, :], new[:, :], b[:, :], ALU.add), v, ts)
                    prev.release(v, prev_use)
                b.release(new.t)
                prev = new
                yield
                b = SB.take()
                prev_use = PE(lambda e, t=t, prev=prev, b=b: e.matmul(b[:, :], C[:, t * 128:(t + 1) * 128], prev[:, :],
                                                                   start=True, stop=True), prev.t, C.t, b.w)
                x = fp.take()
                v = DV(lambda e, t=t, x=x, b=b: e.tensor_tensor(
                    x[:, :].rearrange("p (h q) -> p h q", q=64), b[:, :].rearrange("p (h q) -> p h q", q=64),
                    n3(ea)[:, t, hs][:, :, None].broadcast_to([128, 8, 64]), ALU.mult), prev_use, x.w, tn)
                b.release(v)
                Y[t].t = DV(lambda e, t=t, x=x: e.tensor_tensor(Y[t][:, :], Y[t][:, :], x[:, :], ALU.add), v, Y[t].t)
                x.release(Y[t].t)
                yield
            prev.release(prev_use)
            BN.release(ts)
            C.release(prev_use)
            ac = acum["ac"]
            for e2 in range(4):
                yb = SB.take()
                for e1 in range(2):
                    H = 8 * g + 2 * e2 + e1
                    b = SB.take()
                    tp = PE(lambda e, H=H, b=b: e.matmul(b[:, :], con[0:32, H:H + 1].broadcast_to([32, 128]), ac[0:32, :],
                                                        start=True, stop=True), acum["t"], b.w)
                    acum["users"][:] = [tp]
                    E = fp.take()
                    v = DV(lambda e, H=H, E=E, b=b: e.tensor_tensor(
                        E[:, :].rearrange("p (t l) -> p t l", t=T4), b[:, :].rearrange("p (t l) -> p t l", t=T4),
                        n3(acN)[:, :, H][:, :, None].broadcast_to([128, T4, 128]), ALU.subtract), tp, E.w, tn)
                    b.release(v)
                    v = DV(lambda e, E=E: e.tensor_scalar(E[:, :], E[:, :], 0.0, None, ALU.min), v)
                    a = AC(lambda e, E=E: e.activation(E[:, :], E[:, :], ACT.Exp), v)
                    yield
                    v = DV(lambda e, E=E: e.tensor_tensor(E[:, :], E[:, :], CB[:, :], ALU.mult), a, CB.t)
                    for t in range(T4):
                        hh = 2 * e2 + e1
                        tp = PE(lambda e, t=t, E=E, yb=yb, hh=hh, e1=e1: e.matmul(
                            yb[:, t * 128 + e1 * 64:t * 128 + e1 * 64 + 64], E[:, t * 128:(t + 1) * 128],
                            Xd[t][:, hh * 64:hh * 64 + 64], start=True, stop=True), v, yb.w)
                    E.release(tp)
                for t in range(T4):
                    v = DV(lambda e, t=t, yb=yb, e2=e2: e.tensor_tensor(
                        Y[t][:, e2 * 128:(e2 + 1) * 128], Y[t][:, e2 * 128:(e2 + 1) * 128], yb[:, t * 128:(t + 1) * 128], ALU.add),
                        tp, Y[t].t)
                    Y[t].t = v
                yb.release(v)
                yield
            CB.release(v)
            for p in Xd:
                p.release(tp)
            G["Y"] = Y

        def project_z(g):
            G = grp[g]
            G["z"] = []
            for i in range(4):
                b, t = ugemm(WIN[4 * g + i])
                s = fp.take()
                s.t = AC(lambda e, s=s, b=b: e.activation(s[:, :], b[:, :], ACT.Silu), t, s.w)
                b.release(s.t)
                G["z"].append(s)
                yield

        def gate_group(g):
            G = grp[g]
            Y, z = G["Y"], G["z"]
            for i in range(4):
                b = SB.take()
                for t in range(T4):
                    tp = PE(lambda e, i=i, t=t, b=b: e.transpose(b[:, t * 128:(t + 1) * 128], Y[t][:, i * 128:(i + 1) * 128], ident),
                            Y[t].t, b.w)
                z[i].t = DV(lambda e, i=i, b=b: e.tensor_tensor(z[i][:, :], z[i][:, :], b[:, :], ALU.mult), tp, z[i].t)
                b.release(z[i].t)
                yield
            for p in Y:
                p.release(tp)
            b = SB.take()
            t = sumsq(b, b.w, [(z[i][:, :], z[i].t) for i in range(4)], O512)
            r = rstd_of(b, t)
            yield
            G["p"] = []
            for i in range(4):
                v = DV(lambda e, i=i: e.scalar_tensor_tensor(out=z[i][:, :], in0=z[i][:, :], scalar=pc("norm_g", 4 * g + i),
                                                           in1=r[:, :], op0=ALU.mult, op1=ALU.mult), r.t, z[i].t, t)
                hi, lo = rp.take(), rp.take()
                tk = split(hi[:, :], lo[:, :], z[i][:, :], v, [hi.w, lo.w])
                z[i].release(tk)
                G["p"].append((hi, lo, tk))
            r.release(v)
            yield

        yssd = []

        def branch_group(g):
            G = grp[g]
            P = G["p"]
            for m2 in range(4):
                p = panel(d["wssd"][g, m2], KB * 128)
                for mi in range(2):
                    m = 2 * m2 + mi
                    b = MB.take()
                    t = matpanel(b, b.w, p, 4, 0, lambda k: P[k][0][:, :], lambda k: P[k][1][:, :], lambda k: P[k][2],
                                 True, True, off=4 * mi)
                    if g == 0:
                        y = fp.take()
                        y.t = AC(lambda e, y=y, b=b: e.copy(y[:, :], b[:, :]), t, y.w)
                        yssd.append(y)
                    else:
                        y = yssd[m]
                        y.t = DV(lambda e, y=y, b=b: e.tensor_tensor(y[:, :], y[:, :], b[:, :], ALU.add), t, y.t)
                    b.release(y.t)
                yield
            for hi, lo, tk in P:
                hi.release(t)
                lo.release(t)

        def chain(*gens):
            for x in gens:
                yield from x

        finish(chain(project_dt(), project_group(0)))
        for g in range(4):
            nxt = chain(*([branch_group(g - 1)] if g else []),
                        *([project_group(g + 1)] if g < 3 else []), project_z(g))
            core = chain(ssd_core(g))
            interleave(nxt, core, 23, (8 if 0 < g < 3 else 6) + (0 if g else 4))
            for _ in gate_group(g):
                pass
        for _ in branch_group(3):
            pass
        acum["ac"].release(acum["users"])

        lam = sm(8)
        lt = fp.take()
        t1 = DV(lambda e: e.tensor_tensor(lt[:, 0:128].rearrange("p (a b) -> p a b", a=2),
                                        pc("lam", 0, 256).rearrange("p (a c b) -> p a c b", a=2, c=2)[:, :, 0, :],
                                        pc("lam", 0, 256).rearrange("p (a c b) -> p a c b", a=2, c=2)[:, :, 1, :], ALU.mult),
                lt.w, t_par)
        t2 = DV(lambda e: e.reduce_sum(lam[:, 0:2], lt[:, 0:128].rearrange("p (a b) -> p a b", a=2), AX.X), t1)
        lt.release(t2)
        t3 = AC(lambda e: e.activation(lam[:, 2:4], lam[:, 0:2], ACT.Exp), t2)
        t4 = DV(lambda e: e.tensor_tensor(lam[:, 4:5], lam[:, 3:4], lam[:, 2:3], ALU.subtract), t3)
        t_lam = DV(lambda e: e.tensor_scalar(lam[:, 5:6], lam[:, 4:5], -LAM_INIT, None, ALU.add), t4)
        nlam = lam[:, 5:6]
        t_sg = DV(lambda e: e.tensor_scalar(lam[:, 6:7], pc("subln"), 1.0 - LAM_INIT, None, ALU.mult), t_par)
        sg = lam[:, 6:7]
        st = sm(64)
        heads = [dict() for _ in range(8)]
        stat = {"k": 0}

        def project_head(h):
            Hd = heads[h]
            for name, j in (("q", 40 + h), ("k", 48 + h), ("v", 56 + h)):
                b, t = ugemm(WIN[j])
                s = fp.take()
                s.t = AC(lambda e, s=s, b=b, name=name: e.mul(s[:, :], b[:, :], 0.125) if name == "q" else e.copy(s[:, :], b[:, :]),
                         t, s.w)
                b.release(s.t)
                Hd[name] = s
                yield

        st_free = [None] * 4

        def att_head(h):
            Hd = heads[h]
            q, k, vT = Hd["q"], Hd["k"], Hd["v"]
            b = SB.take()
            tp = turn(b, b.w, vT, vT.t)
            vT.release(tp)
            V = fp.take()
            V.t = AC(lambda e: e.copy(V[:, :], b[:, :]), tp, V.w)
            b.release(V.t)
            yield
            ob = SB.take()
            slope = float(2.0 ** (-8.0 * (h + 1) / 8))
            for i in range(T4):
                W = 128 * (i + 1)
                s_i = stat["k"] % 4
                stat["k"] += 1
                s0 = st[:, 16 * s_i:16 * s_i + 16]
                wst = st_free[s_i]
                Ps = []
                tm = []
                for m in range(2):
                    b = SB.take()
                    r = slice(64 * m, 64 * m + 64)
                    tp = PE(lambda e, r=r, b=b, i=i, W=W: e.matmul(b[:, 0:W], q[r, i * 128:(i + 1) * 128], k[r, 0:W],
                                                                 start=True, stop=True), q.t, k.t, b.w)
                    P = fp.take()
                    a0 = CCOLS["dist"][0]
                    v = DV(lambda e, b=b, P=P, i=i, W=W: e.scalar_tensor_tensor(
                        out=P[:, 0:W], in0=con[:, a0 + 384 - 128 * i:a0 + 512], scalar=slope, in1=b[:, 0:W],
                        op0=ALU.mult, op1=ALU.add), tp, P.w)
                    b.release(v)
                    P.t = v
                    tm.append(DV(lambda e, P=P, m=m, W=W, s0=s0: e.reduce_max(s0[:, m:m + 1], P[:, 0:W], AX.X), v, wst))
                    Ps.append(P)
                tm = DV(lambda e, s0=s0: e.tensor_scalar(s0[:, 2:4], s0[:, 0:2], -1.0, None, ALU.mult), tm)
                te = []
                for m in range(2):
                    te.append(AC(lambda e, P=Ps[m], m=m, W=W, s0=s0: e.activation(
                        P[:, 0:W], P[:, 0:W], ACT.Exp, bias=s0[:, 2 + m:3 + m], accum_out=s0[:, 4 + m:5 + m]), tm))
                yield
                v = DV(lambda e, s0=s0: e.reciprocal(s0[:, 6:8], s0[:, 4:6]), te)
                v2 = DV(lambda e, s0=s0: e.tensor_tensor(s0[:, 8:9], s0[:, 7:8], nlam, ALU.mult), v, t_lam)
                v3 = DV(lambda e, P=Ps[1], W=W, s0=s0: e.tensor_scalar(P[:, 0:W], P[:, 0:W], s0[:, 8:9], None, ALU.mult), v2, te)
                v4 = DV(lambda e, P=Ps[0], Q=Ps[1], W=W, s0=s0: e.scalar_tensor_tensor(
                    out=P[:, 0:W], in0=P[:, 0:W], scalar=s0[:, 6:7], in1=Q[:, 0:W], op0=ALU.mult, op1=ALU.add), v3, te)
                st_free[s_i] = v4
                Ps[1].release(v4)
                Ps[0].t = v4
                yield
                tpv = pv(Ps[0], W, i, V, ob)
                yield
            q.release(tp)
            k.release(tp)
            V.release(tpv)
            o = fp.take()
            o.t = AC(lambda e: e.copy(o[:, :], ob[:, :]), tpv, o.w)
            ob.release(o.t)
            b = SB.take()
            t = sumsq(b, b.w, [(o[:, :], o.t)], O128)
            r = rstd_of(b, t)
            v = DV(lambda e: e.scalar_tensor_tensor(out=o[:, :], in0=o[:, :], scalar=sg, in1=r[:, :], op0=ALU.mult, op1=ALU.mult),
                   r.t, o.t, t, t_sg)
            r.release(v)
            hi, lo = rp.take(), rp.take()
            tk = split(hi[:, :], lo[:, :], o[:, :], v, [hi.w, lo.w])
            o.release(tk)
            Hd["o"] = (hi, lo, tk)
            yield

        def gates(names_m):
            for m in names_m:
                b, t = ugemm(WIN[64 + m])
                s = fp.take()
                a = AC(lambda e, s=s, b=b, m=m: e.activation(s[:, :], b[:, :], ACT.Sigmoid, bias=pc("gate_b", m)), t, s.w, t_par)
                b.release(a)
                y = yssd[m]
                y.t = DV(lambda e, s=s, y=y: e.tensor_tensor(y[:, :], y[:, :], s[:, :], ALU.mult), a, y.t)
                s.release(y.t)
                yield

        finish(project_head(0))
        for h in range(8):
            nxt = chain(*([project_head(h + 1)] if h < 7 else [gates(range(8))]))
            interleave(nxt, att_head(h), 14, 3 if h < 7 else 8)
        yatt = []
        for m in range(KB):
            b = MB.take()
            t = matpanel(b, b.w, panel(d["wda"][m], KB * 128), KB, 0, lambda k: heads[k]["o"][0][:, :],
                         lambda k: heads[k]["o"][1][:, :], lambda k: heads[k]["o"][2], True, True)
            y = fp.take()
            y.t = AC(lambda e, y=y, b=b: e.copy(y[:, :], b[:, :]), t, y.w)
            b.release(y.t)
            yatt.append(y)
        for k in range(8):
            heads[k]["o"][0].release(t)
            heads[k]["o"][1].release(t)
        mg = []
        for m in range(KB):
            b, t = ugemm(WIN[72 + m])
            s = fp.take()
            a = AC(lambda e, s=s, b=b, m=m: e.activation(s[:, :], b[:, :], ACT.Sigmoid, bias=pc("gate_b", 8 + m)), t, s.w, t_par)
            b.release(a)
            v = DV(lambda e, s=s, m=m: e.tensor_tensor(s[:, :], s[:, :], yatt[m][:, :], ALU.mult), a, yatt[m].t)
            yatt[m].release(v)
            v = DV(lambda e, s=s, m=m: e.tensor_tensor(s[:, :], s[:, :], yssd[m][:, :], ALU.add), v, yssd[m].t)
            yssd[m].release(v)
            hi, lo = rp.take(), rp.take()
            tk = split(hi[:, :], lo[:, :], s[:, :], v, [hi.w, lo.w])
            s.release(tk)
            mg.append((hi, lo, tk))
        y = []
        for m in range(KB):
            b = MB.take()
            t = matpanel(b, b.w, panel(d["wout"][m], KB * 128), KB, 0, lambda k: mg[k][0][:, :], lambda k: mg[k][1][:, :],
                         lambda k: mg[k][2], True, True)
            p = fp.take()
            p.t = AC(lambda e, p=p, b=b: e.copy(p[:, :], b[:, :]), t, p.w)
            b.release(p.t)
            y.append(p)
        for hi, lo, tk in mg:
            hi.release(t)
            lo.release(t)
        post_norm(y, "mix_post", False)
        t_all = drop_pages()

    if stop >= 3:
      with ExitStack() as ph:
        act = sb(ph, "act2", [128, 2, FB, L], R)
        t_phase = ffn(d["w2g"], d["w2u"], d["w2d"], "ffn2_pre", "ffn2_post", act, (t_all,))

    if stop >= 4:
      with ExitStack() as ph:
        con = sb(ph, "con2", [128, NCB])
        t_con = ("c2", 16)
        SP(lambda e: e.dma_start(con[:, :], d["consts2"]).then_inc(sem("c2"), 16), t_phase)
        ident = con[:, 0:128]
        BDI, NEG = cc("bdincl"), cc("neg")
        mR = sb(ph, "mR2", [128, 16, L], R)
        fB = sb(ph, "fB2", [128, NB_, L])
        for i in range(NB_):
            fp.free.append((fB[:, i, :], [t_phase]))
        rp = Pages([mR[:, i, :] for i in range(16)], "R pages")
        for i in range(16):
            rp.free[i] = (rp.free[i][0], [t_phase])
        norm_u("norm1")
        W2 = d["win2"]
        b, t = ugemm(W2[32])
        nar = fp.take()
        t0 = DV(lambda e: e.tensor_scalar(nar[:, :], b[:, :], pc("g_bias"), None, ALU.add), t, nar.w, t_par)
        t_b = AC(lambda e: e.activation(nar[32:64, :], nar[32:64, :], ACT.Sigmoid), t0)
        ISC = float((8 ** -0.5) * (64 ** -0.5))
        t_w = DV(lambda e: e.tensor_scalar(nar[64:96, :], nar[64:96, :], ISC, None, ALU.mult), t0)
        b.release(t0)
        gex = sm(1)
        ta = AC(lambda e: e.activation(gex, pc("g_alog"), ACT.Exp), t_par)
        tgs = []
        for r in (slice(0, 32), slice(96, 128)):
            t = softplus(nar, t0, r)
            t = DV(lambda e, r=r: e.tensor_scalar(nar[r, :], nar[r, :], gex[r, :], -1.0, ALU.mult, ALU.mult), t, ta)
            a0 = CCOLS["reset64"][0]
            g_ = fp.take()
            t = DV(lambda e, r=r, g_=g_: e.tensor_tensor_scan(g_[r, :], con[r, a0:a0 + L], nar[r, :], 0.0, ALU.mult, ALU.add), t, g_.w)
            if r.start == 0:
                t = DV(lambda e, r=r, g_=g_: e.tensor_copy(nar[r, :], g_[r, :]), t)
            else:
                t = DV(lambda e, r=r, g_=g_: e.tensor_tensor(
                    nar[r, :].rearrange("p (c l) -> p c l", l=64),
                    g_[r, :].rearrange("p (c l) -> p c l", l=64)[:, :, 63:64].broadcast_to([32, 8, 64]),
                    g_[r, :].rearrange("p (c l) -> p c l", l=64), ALU.subtract), t)
            g_.release(t)
            tgs.append(t)
        t_nar = [tgs, t_b, t_w]
        b = SB.take()
        tp = turn(b, b.w, nar, t_nar)
        NN = fp.take()
        t = AC(lambda e: e.copy(NN[:, :], b[:, :]), tp, NN.w)
        b.release(t)
        N3 = NN[:, :].rearrange("p (t c) -> p t c", t=T4)
        t1 = AC(lambda e: e.activation(N3[:, :, 8:16], N3[:, :, 0:8], ACT.Exp), t)
        t2 = DV(lambda e: e.tensor_tensor(N3[:, :, 8:16], N3[:, :, 8:16], N3[:, :, 32:40], ALU.mult), t1)
        t3 = AC(lambda e: e.activation(N3[:, :, 96:104], N3[:, :, 96:104], ACT.Exp), t)
        t_NN = [t, t1, t2, t3]

        def v3(p):
            return p[:, :].rearrange("p (t l) -> p t l", t=T4)

        def bc(col):
            return N3[:, :, col:col + 1].broadcast_to([128, T4, 128])

        def bm(ap):
            return ap[:, None, :].broadcast_to([128, T4, 128])

        S = [dict() for _ in range(8)]
        zg = [None] * 8

        def project_gdn(h):
            for name, j in (("q", h), ("k", 8 + h), ("v", 16 + h)):
                b, t = ugemm(W2[j])
                S[h][name] = convsilu(b, t, "gconv_w", j, None)
                yield

        def project_zg(h):
            b, t = ugemm(W2[24 + h])
            z = fp.take()
            a = AC(lambda e, z=z, b=b: e.activation(z[:, :], b[:, :], ACT.Silu), t, z.w)
            b.release(a)
            yield
            b, t = ugemm(W2[50 + h])
            s = fp.take()
            a2 = AC(lambda e, s=s, b=b, h=h: e.activation(s[:, :], b[:, :], ACT.Sigmoid, bias=pc("bgb", h)), t, s.w, t_par)
            b.release(a2)
            z.t = DV(lambda e, s=s, z=z: e.tensor_tensor(z[:, :], z[:, :], s[:, :], ALU.mult), a, a2)
            s.release(z.t)
            zg[h] = z
            yield

        def l2(x, scale):
            b = SB.take()
            t = sumsq(b, b.w, [(x[:, :], x.t)], O1)
            r = rstd_of(b, t)
            x.t = DV(lambda e: e.scalar_tensor_tensor(out=x[:, :], in0=x[:, :], scalar=scale, in1=r[:, :], op0=ALU.mult, op1=ALU.mult),
                     r.t, x.t, t)
            r.release(x.t)

        def gdn_prep(h):
            H = S[h]
            q, k, v = H["q"], H["k"], H["v"]
            l2(k, 1.0)
            l2(q, float(128 ** -0.5))
            yield
            gb = SB.take()
            tg = PE(lambda e: e.matmul(gb[:, :], con[0:32, h:h + 1].broadcast_to([32, 128]), nar[0:32, :], start=True, stop=True),
                    t_nar, gb.w)
            eg = fp.take()
            eg.t = AC(lambda e: e.activation(eg[:, :], gb[:, :], ACT.Exp), tg, eg.w)
            gm = fp.take()
            t = DV(lambda e: e.tensor_tensor(v3(gm), v3(gb), bc(h), ALU.subtract), tg, eg.t, gm.w, t_NN)
            gb.release(eg.t, t)
            t = DV(lambda e: e.tensor_scalar(gm[:, :], gm[:, :], 0.0, None, ALU.min), t)
            t_g = AC(lambda e: e.activation(gm[:, :], gm[:, :], ACT.Exp), t)
            t_gm = DV(lambda e: e.tensor_tensor(v3(gm), v3(gm), bm(BDI), ALU.mult), t_g)
            yield
            bb = SB.take()
            tb = PE(lambda e: e.matmul(bb[:, :], con[32:64, 32 + h:33 + h].broadcast_to([32, 128]), nar[32:64, :], start=True, stop=True),
                    t_nar, bb.w)
            AT = fp.take()
            ta = DV(lambda e: e.tensor_tensor(AT[:, :], gm[:, :], bb[:, :], ALU.mult), tb, t_gm, AT.w)
            bb.release(ta)
            kk, qk = SB.take(), SB.take()
            for t in range(T4):
                c = slice(t * 128, (t + 1) * 128)
                t1 = PE(lambda e, c=c: e.matmul(kk[:, c], k[:, c], k[:, c], start=True, stop=True), k.t, kk.w)
                t2 = PE(lambda e, c=c: e.matmul(qk[:, c], k[:, c], q[:, c], start=True, stop=True), q.t, qk.w)
            AT.t = DV(lambda e: e.tensor_tensor(AT[:, :], AT[:, :], kk[:, :], ALU.mult), t1, ta)
            kk.release(AT.t)
            gm.t = DV(lambda e: e.tensor_tensor(gm[:, :], gm[:, :], qk[:, :], ALU.mult), t2, t_gm, ta)
            qk.release(gm.t)
            H["att"] = gm
            q.t = DV(lambda e: e.tensor_tensor(q[:, :], q[:, :], eg[:, :], ALU.mult), q.t, eg.t, t2)
            H["qg"], H["eg"] = q, eg
            yield
            b = SB.take()
            tp = turn(b, b.w, k, k.t)
            k.release(tp)
            kbe, kd = fp.take(), fp.take()
            kbe.t = DV(lambda e: e.tensor_tensor(v3(kbe), v3(b), bc(8 + h), ALU.mult), tp, kbe.w, t_NN)
            kd.t = DV(lambda e: e.tensor_tensor(v3(kd), v3(b), bc(96 + h), ALU.mult), tp, kd.w, t_NN)
            b.release(kbe.t, kd.t)
            H["kd"] = kd
            b2 = SB.take()
            tp = turn(b2, b2.w, v, v.t)
            v.release(tp)
            vb = fp.take()
            vb.t = DV(lambda e: e.tensor_tensor(v3(vb), v3(b2), bc(32 + h), ALU.mult), tp, vb.w, t_NN)
            b2.release(vb.t)
            yield
            lv = CCOLS["level"][0]
            U, Tm, Y, Ak = fp.take(), fp.take(), fp.take(), fp.take()
            t = DV(lambda e: e.tensor_tensor(v3(U), v3(AT), bm(con[:, lv:lv + 128]), ALU.mult), AT.t, U.w)
            tU = DV(lambda e: e.tensor_tensor(v3(U), bm(ident), v3(U), ALU.subtract), t)
            b = SB.take()
            tp = turn(b, b.w, U, tU)
            tT = AC(lambda e, b=b: e.copy(Tm[:, :], b[:, :]), tp, Tm.w)
            b.release(tT)
            wY, wA = Y.w, Ak.w
            for lev in range(1, 6):
                m = con[:, lv + 128 * lev:lv + 128 * lev + 128]
                tA = GP(lambda e, m=m: e.tensor_tensor(v3(Ak), v3(AT), bm(m), ALU.mult), AT.t, wA)
                b = SB.take()
                for t in range(T4):
                    c = slice(t * 128, (t + 1) * 128)
                    tp = PE(lambda e, c=c, b=b: e.matmul(b[:, c], Ak[:, c], Tm[:, c], start=True, stop=True), tA, tT, b.w)
                wA = tp
                tY = AC(lambda e, b=b: e.copy(Y[:, :], b[:, :]), tp, wY)
                b.release(tY)
                yield
                b = SB.take()
                for t in range(T4):
                    c = slice(t * 128, (t + 1) * 128)
                    tp = PE(lambda e, c=c, b=b: e.matmul(b[:, c], Y[:, c], U[:, c], start=True, stop=True), tY, tU, b.w)
                if lev < 5:
                    b2 = SB.take()
                    for t in range(T4):
                        c = slice(t * 128, (t + 1) * 128)
                        tp2 = PE(lambda e, c=c, b2=b2: e.matmul(b2[:, c], U[:, c], Y[:, c], start=True, stop=True), b2.w)
                    tT = DV(lambda e, b2=b2: e.tensor_tensor(Tm[:, :], Tm[:, :], b2[:, :], ALU.subtract), tp2, tT, wA)
                    b2.release(tT)
                    tp = tp2
                wY = tp
                tU = DV(lambda e, b=b: e.tensor_tensor(U[:, :], U[:, :], b[:, :], ALU.subtract), tp, tU)
                b.release(tU)
                yield
            Tm.release(tT, wA)
            Y.release(wY)
            Ak.release(wA)
            AT.release(tA)
            b, b2 = SB.take(), SB.take()
            for t in range(T4):
                c = slice(t * 128, (t + 1) * 128)
                t1 = PE(lambda e, c=c: e.matmul(b[:, c], U[:, c], vb[:, c], start=True, stop=True), tU, vb.t, b.w)
                t2 = PE(lambda e, c=c: e.matmul(b2[:, c], kbe[:, c], U[:, c], start=True, stop=True), kbe.t, b2.w)
            uN, wT = fp.take(), fp.take()
            uN.t = AC(lambda e: e.copy(uN[:, :], b[:, :]), t1, uN.w)
            wT.t = AC(lambda e: e.copy(wT[:, :], b2[:, :]), t2, wT.w)
            b.release(uN.t)
            b2.release(wT.t)
            U.release(t2)
            vb.release(t1)
            kbe.release(t2)
            H["u"], H["w"] = uN, wT
            yield

        def gdn_scan(hs):
            n = len(hs)
            st_ = fp.take()
            vn = fp.take()
            o = {h: fp.take() for h in hs}
            t_S = [st_.w] * n
            t_Su = None
            wv = vn.w
            for c in range(8):
                t, half = c // 2, c % 2
                r = slice(64 * half, 64 * half + 64)
                cs = slice(c * 64, c * 64 + 64)
                if c:
                    b = SB.take()
                    for i, h in enumerate(hs):
                        tp = PE(lambda e, i=i, h=h, b=b, r=r, cs=cs: e.matmul(
                            b[r, i * 128:(i + 1) * 128], S[h]["w"][:, cs], st_[:, i * 128:(i + 1) * 128], start=True, stop=True),
                            S[h]["w"].t, t_S[i], b.w)
                tv = []
                for i, h in enumerate(hs):
                    ic = slice(i * 128, (i + 1) * 128)
                    tc = slice(t * 128, (t + 1) * 128)
                    if c:
                        tv.append(DV(lambda e, h=h, b=b, ic=ic, tc=tc, r=r: e.tensor_tensor(
                            vn[r, ic], S[h]["u"][r, tc], b[r, ic], ALU.subtract), tp, wv, S[h]["u"].t))
                    else:
                        tv.append(DV(lambda e, h=h, ic=ic, tc=tc, r=r: e.tensor_copy(vn[r, ic], S[h]["u"][r, tc]), wv, S[h]["u"].t))
                if c:
                    b.release(tv)
                yield
                if c < 7:
                    bs = SB.take()
                    for i, h in enumerate(hs):
                        ic = slice(i * 128, (i + 1) * 128)
                        tc = slice(t * 128, (t + 1) * 128)
                        ts = PE(lambda e, h=h, bs=bs, ic=ic, tc=tc, r=r: e.matmul(
                            bs[:, ic], S[h]["kd"][r, tc], vn[r, ic], start=True, stop=True), tv, S[h]["kd"].t, bs.w)
                bo = SB.take()
                for i, h in enumerate(hs):
                    ic = slice(i * 128, (i + 1) * 128)
                    oc = slice(i * 64, i * 64 + 64)
                    ac_ = slice(t * 128 + 64 * half, t * 128 + 64 * half + 64)
                    if c:
                        PE(lambda e, h=h, bo=bo, ic=ic, oc=oc, cs=cs: e.matmul(
                            bo[:, oc], st_[:, ic], S[h]["qg"][:, cs], start=True, stop=False), S[h]["qg"].t, bo.w, t_S[i])
                    to = PE(lambda e, h=h, bo=bo, ic=ic, oc=oc, ac_=ac_, r=r, c=c: e.matmul(
                        bo[:, oc], vn[r, ic], S[h]["att"][r, ac_], start=c == 0, stop=True), tv, S[h]["att"].t, bo.w)
                wv = to
                if c < 7:
                    for i, h in enumerate(hs):
                        ic = slice(i * 128, (i + 1) * 128)
                        if c:
                            t_S[i] = DV(lambda e, h=h, bs=bs, ic=ic, c=c: e.scalar_tensor_tensor(
                                out=st_[:, ic], in0=st_[:, ic], scalar=S[h]["eg"][:, c * 64 + 63:c * 64 + 64], in1=bs[:, ic],
                                op0=ALU.mult, op1=ALU.add), ts, to, t_S[i], S[h]["eg"].t)
                        else:
                            t_S[i] = DV(lambda e, bs=bs, ic=ic: e.tensor_copy(st_[:, ic], bs[:, ic]), ts, t_S[i])
                    bs.release(*t_S)
                for i, h in enumerate(hs):
                    o[h].t = AC(lambda e, h=h, bo=bo, i=i, cs=cs: e.copy(o[h][:, cs], bo[:, i * 64:i * 64 + 64]), to, o[h].w)
                bo.release(o[hs[-1]].t)
                yield
            st_.release(to)
            vn.release(to)
            for h in hs:
                for name in ("w", "u", "kd", "qg", "att", "eg"):
                    S[h][name].release(to, t_S, tv)
            for h in hs:
                b = SB.take()
                t = sumsq(b, b.w, [(o[h][:, :], o[h].t)], O128)
                r = rstd_of(b, t)
                v = DV(lambda e, h=h, r=r: e.scalar_tensor_tensor(out=o[h][:, :], in0=o[h][:, :], scalar=pc("gnorm"), in1=r[:, :],
                                                                op0=ALU.mult, op1=ALU.mult), r.t, o[h].t, t)
                r.release(v)
                S[h]["o"] = o[h]
                o[h].t = v
                yield

        NGH = [(0, 1), (2, 3), (4, 5), (6, 7)]

        def finish_heads(hs):
            for h in hs:
                z, o = zg[h], S[h]["o"]
                z.t = DV(lambda e, z=z, o=o: e.tensor_tensor(z[:, :], z[:, :], o[:, :], ALU.mult), z.t, o.t)
                o.release(z.t)

        dq, dk, dv_, iq = [None] * 8, [None] * 2, [None] * 2, [None] * 4
        ikp = [None]

        def plain(j):
            b, t = ugemm(W2[j])
            s = fp.take()
            s.t = AC(lambda e, s=s, b=b: e.copy(s[:, :], b[:, :]), t, s.w)
            b.release(s.t)
            return s

        def project_idx():
            x = plain(49)
            b = SB.take()
            t = PE(lambda e: e.matmul(b[:, :], onesc[:, O128, :], x[:, :], start=True, stop=True), x.t, b.w)
            x.t = DV(lambda e: e.tensor_tensor(x[:, :], x[:, :], b[:, :], ALU.subtract), t)
            b.release(x.t)
            b = SB.take()
            t = sumsq(b, b.w, [(x[:, :], x.t)], O128)
            r = rstd_of(b, t)
            x.t = DV(lambda e: e.scalar_tensor_tensor(out=x[:, :], in0=x[:, :], scalar=pc("ikg"), in1=r[:, :], op0=ALU.mult, op1=ALU.mult),
                     r.t, x.t, t)
            r.release(x.t)
            ikp[0] = x
            yield
            for i in range(4):
                iq[i] = plain(45 + i)
                yield

        def project_kv():
            for i in range(2):
                dk[i] = plain(41 + i)
                yield
            for i in range(2):
                s = plain(43 + i)
                b = SB.take()
                tp = turn(b, b.w, s, s.t)
                V = fp.take()
                V.t = AC(lambda e, V=V, b=b: e.copy(V[:, :], b[:, :]), tp, V.w)
                b.release(V.t)
                s.release(tp)
                dv_[i] = V
                yield

        masks = {}
        m8 = sm(8 * 3)
        cnt = sm(6)

        def indexer(i):
            W = 128 * (i + 1)
            x = ikp[0]
            sc = fp.take()
            sc.t = sc.w
            for h in range(8):
                r = slice(64 * (h % 2), 64 * (h % 2) + 64)
                b = SB.take()
                tp = PE(lambda e, h=h, r=r, b=b: e.matmul(b[:, 0:W], iq[h // 2][r, i * 128:(i + 1) * 128], x[r, 0:W],
                                                        start=True, stop=True), iq[h // 2].t, x.t, b.w)
                wcol = N3[:, i, 64 + h:65 + h]
                if h == 0:
                    v = DV(lambda e, b=b, wcol=wcol: e.tensor_scalar(sc[:, 0:W], b[:, 0:W], 0.0, wcol, ALU.max, ALU.mult),
                           tp, sc.t, t_NN)
                    b.release(v)
                else:
                    rl = fp.take()
                    a = AC(lambda e, b=b, rl=rl: e.activation(rl[:, 0:W], b[:, 0:W], ACT.Relu), tp, rl.w)
                    b.release(a)
                    v = DV(lambda e, rl=rl, wcol=wcol: e.scalar_tensor_tensor(
                        out=sc[:, 0:W], in0=rl[:, 0:W], scalar=wcol, in1=sc[:, 0:W], op0=ALU.mult, op1=ALU.add), a, sc.t, t_NN)
                    rl.release(v)
                sc.t = v
                if h % 2:
                    yield
            masks[i, "x"] = tp
            v = DV(lambda e: e.tensor_tensor(sc[:, W - 128:W], sc[:, W - 128:W], NEG, ALU.add), sc.t, t_con)
            wk = fp.take()
            top = m8[:, 8 * (i - 1):8 * i]
            t = DV(lambda e: e.max(top, sc[:, 0:W]), v)
            for n in range(15):
                src = sc if n == 0 else wk
                t = DV(lambda e, src=src: e.match_replace(out=wk[:, 0:W], in_to_replace=top, in_values=src[:, 0:W], imm_value=-3.0e38),
                       t, wk.w if n == 0 else None)
                t = DV(lambda e: e.max(top, wk[:, 0:W]), t)
                if n % 4 == 3:
                    yield
            c0, c1 = cnt[:, 2 * i - 2:2 * i - 1], cnt[:, 2 * i - 1:2 * i]
            gt, eq = wk, fp.take()
            thr = top[:, 7:8]
            t1 = DV(lambda e: e.tensor_scalar(gt[:, 0:W], sc[:, 0:W], thr, None, ALU.is_gt, ALU.add, accum_out=c0), t)
            t2 = DV(lambda e: e.tensor_scalar(eq[:, 0:W], sc[:, 0:W], thr, None, ALU.is_equal), t, eq.w)
            t3 = DV(lambda e: e.tensor_scalar(c1, c0, -1.0, 128.0, ALU.mult, ALU.add), t1)
            t4 = DV(lambda e: e.tensor_tensor_scan(sc[:, 0:W], onesc[:, O1, 0:1].broadcast_to([128, W]), eq[:, 0:W], 0.0, ALU.mult, ALU.add), t2, t_ones[O1])
            t5 = DV(lambda e: e.scalar_tensor_tensor(out=eq[:, 0:W], in0=sc[:, 0:W], scalar=c1, in1=eq[:, 0:W],
                                                   op0=ALU.is_le, op1=ALU.mult), t4, t3)
            t6 = DV(lambda e: e.tensor_tensor(gt[:, 0:W], gt[:, 0:W], eq[:, 0:W], ALU.add), t5, t1)
            t7 = DV(lambda e: e.tensor_scalar(gt[:, 0:W], gt[:, 0:W], -1.0, -NEGBIG, ALU.add, ALU.mult), t6)
            eq.release(t6)
            sc.release(t5)
            gt.t = t7
            masks[i] = gt
            yield

        stat2 = {"k": 0}
        st2_free = [None] * 4
        dsc = float(128 ** -0.5)

        def sparse_head(h):
            q, k, V = dq[h], dk[h // 4], dv_[h // 4]
            ob = SB.take()
            for i in range(T4):
                W = 128 * (i + 1)
                s_i = stat2["k"] % 4
                stat2["k"] += 1
                s0 = st2[:, 8 * s_i:8 * s_i + 8]
                wst = st2_free[s_i]
                b = SB.take()
                tp = PE(lambda e, b=b, i=i, W=W: e.matmul(b[:, 0:W], q[:, i * 128:(i + 1) * 128], k[:, 0:W], start=True, stop=True),
                        q.t, k.t, b.w)
                P = fp.take()
                mk = NEG if i == 0 else masks[i][:, 0:W]
                v = DV(lambda e, b=b, P=P, mk=mk, W=W: e.tensor_tensor(P[:, 0:W], b[:, 0:W], mk, ALU.add), tp, P.w,
                       masks[i].t if i else None)
                b.release(v)
                v = DV(lambda e, P=P, W=W, s0=s0: e.reduce_max(s0[:, 0:1], P[:, 0:W], AX.X), v, wst)
                v = DV(lambda e, s0=s0: e.tensor_scalar(s0[:, 1:2], s0[:, 0:1], -dsc, None, ALU.mult), v)
                a = AC(lambda e, P=P, W=W, s0=s0: e.activation(P[:, 0:W], P[:, 0:W], ACT.Exp, scale=dsc, bias=s0[:, 1:2],
                                                             accum_out=s0[:, 2:3]), v)
                yield
                v = DV(lambda e, s0=s0: e.reciprocal(s0[:, 3:4], s0[:, 2:3]), a)
                P.t = DV(lambda e, P=P, W=W, s0=s0: e.tensor_scalar(P[:, 0:W], P[:, 0:W], s0[:, 3:4], None, ALU.mult), v, a)
                st2_free[s_i] = P.t
                yield
                tpv = pv(P, W, i, V, ob)
                yield
            q.release(tp)
            o = fp.take()
            o.t = AC(lambda e: e.copy(o[:, :], ob[:, :]), tpv, o.w)
            ob.release(o.t)
            S[h]["od"] = o
            S[h]["tpv"] = (tp, tpv)
            yield

        st2 = sm(32)

        finish(chain(project_gdn(0), project_gdn(1)))
        for gi, hs in enumerate(NGH):
            side = chain(gdn_prep(hs[0]), gdn_prep(hs[1]), gdn_scan(hs))
            if gi < 3:
                main = chain(project_zg(hs[0]), project_zg(hs[1]), project_gdn(hs[0] + 2), project_gdn(hs[1] + 2))
                nm = 10
            else:
                main = chain(project_zg(6), project_zg(7), project_idx())
                nm = 9
            interleave(main, side, 46, nm)
            finish_heads(hs)

        def project_dq(h):
            dq[h] = plain(33 + h)
            yield

        interleave(chain(project_kv(), *[project_dq(h) for h in range(4)]), chain(indexer(1), indexer(2), indexer(3)), 24, 8)
        ikp[0].release(masks[3, "x"])
        for x in iq:
            x.release(masks[3, "x"])
        mg = [None] * 8

        def merge_heads(h):
            b, t = ugemm(W2[58 + h])
            s = fp.take()
            a = AC(lambda e, s=s, b=b: e.activation(s[:, :], b[:, :], ACT.Sigmoid, bias=pc("bgb", 8 + h)), t, s.w)
            b.release(a)
            S[h]["sg"] = s
            s.t = a
            yield

        def merge_fin(h):
            s, o = S[h]["sg"], S[h]["od"]
            v = DV(lambda e: e.tensor_tensor(s[:, :], s[:, :], o[:, :], ALU.mult), s.t, o.t)
            o.release(v)
            v = DV(lambda e: e.tensor_tensor(s[:, :], s[:, :], zg[h][:, :], ALU.add), v, zg[h].t)
            zg[h].release(v)
            hi, lo = rp.take(), rp.take()
            tk = split(hi[:, :], lo[:, :], s[:, :], v, [hi.w, lo.w])
            s.release(tk)
            mg[h] = (hi, lo, tk)

        for h in range(8):
            main = chain(*([project_dq(h + 4)] if h < 4 else []), merge_heads(h))
            interleave(main, sparse_head(h), 13, 2 if h < 4 else 1)
            merge_fin(h)
        for x in (*dk, *dv_):
            x.release(S[7]["tpv"])
        for i in (1, 2, 3):
            masks[i].release(S[7]["od"].t)
        nar.release(t_NN)
        NN.release(S[7]["od"].t)
        for m in range(KB):
            b = MB.take()
            t = matpanel(b, b.w, panel(d["wout2"][m], KB * 128), KB, 0, lambda k: mg[k][0][:, :], lambda k: mg[k][1][:, :],
                         lambda k: mg[k][2], True, True)
            t_h[m] = DV(lambda e, m=m, b=b: e.tensor_tensor(hT[:, m, :], hT[:, m, :], b[:, :], ALU.add), t, t_h[m])
            b.release(t_h[m])
        for hi, lo, tk in mg:
            hi.release(t)
            lo.release(t)
        t_all = drop_pages()

    if stop >= 5:
      with ExitStack() as ph:
        act = sb(ph, "act3", [128, 2, FB, L], R)
        norm_u("norm2")
        tact = []
        for j in range(FB):
            bg, tg = ugemm(d["w3"][j])
            g_ = fp.take()
            t = conv(bg, tg, "fconv_w", 3, j, 44, "fconv_b", g_)
            a = AC(lambda e, g_=g_: e.activation(g_[:, :], g_[:, :], ACT.Silu), t)
            bu, tu_ = ugemm(d["w3"][FB + j])
            u_ = fp.take()
            t = conv(bu, tu_, "fconv_w", 3, FB + j, 44, "fconv_b", u_)
            v = DV(lambda e, g_=g_, u_=u_: e.tensor_tensor(g_[:, :], g_[:, :], u_[:, :], ALU.mult), a, t)
            u_.release(v)
            tk = split(act[:, 0, j, :], act[:, 1, j, :], g_[:, :], v, [t_all])
            g_.release(tk)
            tact.append(tk)
        for m, b, t in down(d["w3d"], act, tact):
            t_h[m] = DV(lambda e, m=m, b=b: e.tensor_tensor(hT[:, m, :], hT[:, m, :], b[:, :], ALU.add), t, t_h[m])
            b.release(t_h[m])
        b = SB.take()
        t = sumsq(b, b.w, [(hT[:, k, :], t_h[k]) for k in range(KB)], O1024)
        r = rstd_of(b, t)
        for k in range(KB):
            t_h[k] = DV(lambda e, k=k: e.scalar_tensor_tensor(out=hT[:, k, :], in0=hT[:, k, :], scalar=pc("final", k), in1=r[:, :],
                                                            op0=ALU.mult, op1=ALU.mult), r.t, t_h[k], t)
    for k in range(KB):
        SP(lambda e, k=k: e.dma_start(out[k * 128:(k + 1) * 128, :], hT[:, k, :]).then_inc(sem("out"), 16), t_h[k])
    waits_at_end = [("out", 16 * KB)]

    queues = (SP, PE, AC, DV, GP)
    for q in queues:
        q.ops = [op for op in q.ops if op[0] is not None]
        for op in q.ops:
            op[1] = flat(op[1], [])
            for dep in op[1]:
                if isinstance(dep, Tok) and not (dep.eng is q and q is PE):
                    dep.used = True
    for q in queues:
        n = 0
        for op in q.ops:
            if op[2].used:
                n += 1
                op[2].val = n
        if n:
            sem(q.name)
    for q in queues:
        for op in q.ops:
            for dep in op[1]:
                if isinstance(dep, tuple):
                    sem(dep[0])

    def emit(q, eng):
        seen = {}
        for fn, deps, tok in q.ops:
            need = {}
            for dep in deps:
                if isinstance(dep, Tok):
                    if dep.eng is q and q is PE:
                        continue
                    assert dep.val > 0
                    need[dep.eng.name] = max(need.get(dep.eng.name, 0), dep.val)
                else:
                    need[dep[0]] = max(need.get(dep[0], 0), dep[1])
            for s, v in need.items():
                if seen.get(s, 0) < v:
                    eng.wait_ge(sem(s), v)
                    seen[s] = v
            ins = fn.issue()
            if tok.used:
                ins.then_inc(sem(q.name), 1)

    with ctx:
        block = ctx.enter_context(nc.Block())

        @block.sync
        def _(e):
            emit(SP, e)
            for s, v in waits_at_end:
                e.wait_ge(sem(s), v)

        @block.tensor
        def _(e):
            emit(PE, e)

        @block.scalar
        def _(e):
            emit(AC, e)

        @block.vector
        def _(e):
            emit(DV, e)

        @block.gpsimd
        def _(e):
            emit(GP, e)


def blocks(w, n=128):
    K, M = w.shape
    return np.ascontiguousarray(w.reshape(K // 128, 128, M // n, n).transpose(2, 1, 0, 3).reshape(M // n, 128, K // 128 * n))


def constants():
    p = np.arange(128)[:, None]
    f = np.arange(128)[None, :]
    a = np.zeros((128, NCA), np.float32)
    b = np.zeros((128, NCB), np.float32)

    def put(x, name, v):
        at, n = CCOLS[name]
        x[:, at:at + n] = v

    put(a, "ident", p == f)
    put(b, "ident", p == f)
    put(a, "ssdmask", p <= f)
    k = np.arange(512)[None, :] - 384
    put(a, "dist", np.where(k <= p, (k - p).astype(np.float64), NEGBIG))
    put(a, "reset128", np.arange(512)[None, :] % 128 != 0)
    put(b, "reset64", np.arange(512)[None, :] % 64 != 0)
    put(b, "neg", np.where(f <= p, 0.0, NEGBIG))
    put(b, "bdincl", (p <= f) & (p // 64 == f // 64))
    for lev in range(6):
        n = 1 << lev
        m = (p // (2 * n) == f // (2 * n)) & (f // n % 2 == 1) & (p // n % 2 == 0)
        at = CCOLS["level"][0] + 128 * lev
        b[:, at:at + 128] = m
    return a, b


def parameters(z):
    out = np.zeros((128, NPAR), np.float32)

    def put(name, v, rows=slice(0, 128)):
        at, n = PCOLS[name]
        out[rows, at:at + n] = v

    def cols(v):
        v = np.asarray(v).reshape(-1, 128)
        return v.T

    def taps(v):
        return np.concatenate([cols(v[0, i]) for i in range(v.shape[1])], axis=1)

    for name, src in (("ffn1_pre", "ffn1_pre_g"), ("ffn1_post", "ffn1_post_g"), ("mix_pre", "mix_pre_g"),
                      ("gate_b", "gate_b"), ("conv_b", "ssd_conv_b"), ("norm_g", "ssd_norm_g"),
                      ("subln", "da_subln_g"), ("mix_post", "mix_post_g"), ("ffn2_pre", "ffn2_pre_g"),
                      ("ffn2_post", "ffn2_post_g"), ("norm1", "norm1_g_2"), ("gnorm", "gdn_norm_g_2"),
                      ("bgb", "branch_gate_b_2"), ("norm2", "norm2_g_2"), ("fconv_b", "ffn_conv_b_2"),
                      ("final", "final_g_2")):
        put(name, cols(z[src]))
    put("conv_w", taps(z["ssd_conv_w"]))
    put("gconv_w", taps(z["gdn_conv_w_2"]))
    put("fconv_w", taps(z["ffn_conv_w_2"]))
    put("dt_bias", z["ssd_dt_bias"].reshape(32, 1), slice(0, 32))
    put("a_log", z["ssd_A_log"].reshape(32, 1), slice(0, 32))
    put("D", z["ssd_D"].reshape(1, 32))
    put("lam", np.concatenate([z[n].reshape(1, 64) for n in
                               ("da_lambda_q1", "da_lambda_k1", "da_lambda_q2", "da_lambda_k2")], axis=1))
    for r in (0, 96):
        put("g_bias", z["gdn_dt_bias_2"].reshape(8, 1), slice(r, r + 8))
        put("g_alog", z["gdn_a_log_2"].reshape(8, 1), slice(r, r + 8))
    put("ikg", np.concatenate([z["idx_k_norm_g_2"].reshape(64, 1)] * 2))
    return out


def layout(z):
    a = {"xT": np.ascontiguousarray(z["x"][0].T), "params": parameters(z)}
    a["consts1"], a["consts2"] = constants()
    w = z["w_in"][0]
    gap = np.zeros((1024, 96), np.float32)
    a["win"] = blocks(np.concatenate([w[:, 0:5120], w[:, 5152:], w[:, 5120:5152], gap], axis=1))
    a["w1g"], a["w1u"], a["w1d"] = (blocks(z[n][0]) for n in ("ffn1_w_gate", "ffn1_w_up", "ffn1_w_down"))
    a["w2g"], a["w2u"], a["w2d"] = (blocks(z[n][0]) for n in ("ffn2_w_gate", "ffn2_w_up", "ffn2_w_down"))
    a["wssd"] = np.ascontiguousarray(
        z["ssd_w_branch"][0].reshape(4, 4, 128, 4, 2, 128).transpose(0, 3, 2, 4, 1, 5).reshape(4, 4, 128, 1024))
    a["wda"], a["wout"] = blocks(z["da_w_branch"][0]), blocks(z["w_out"][0])
    w = z["w_in_2"][0]
    at = [0, 3072, 4096, 4104, 4112, 5136, 5392, 5648, 6160, 6224, 6232, 7256, 8280]
    qkv, zz, ga, gb, dq, dk, dv, iq, ik, iw, gta, gtb = (w[:, i:j] for i, j in zip(at[:-1], at[1:]))
    n24 = gap[:, 0:24]
    a["win2"] = blocks(np.concatenate([qkv, zz, ga, n24, gb, n24, iw, n24, ga, n24, dq, dk, dv, iq, ik, ik, gta, gtb], axis=1))
    a["wout2"], a["w3"], a["w3d"] = (blocks(z[n][0]) for n in ("w_out_2", "ffn_w_up_2", "ffn_w_down_2"))
    return a


def kernel(**inputs):
    import concourse.bacc as bacc
    from concourse.bass_utils import run_bass_kernel_spmd

    z = {k: np.asarray(v) for k, v in inputs.items()}
    nc = bacc.Bacc("TRN2", target_bir_lowering=False, num_devices=1)
    arrays = layout(z)
    d = {k: nc.dram_tensor("in_" + k, v.shape, F, kind="ExternalInput").ap() for k, v in arrays.items()}
    out = nc.dram_tensor("outT", (1024, 512), F, kind="ExternalOutput").ap()
    build(nc, d, out)
    r = run_bass_kernel_spmd(nc, [{"in_" + k: v for k, v in arrays.items()}], core_ids=[0])
    return np.ascontiguousarray(r.results[0]["outT"].T)[None]
```

```python
from contextlib import ExitStack

import numpy as np

import concourse.bass as bass
from concourse import mybir

F = mybir.dt.float32
R = mybir.dt.float32r
ALU = mybir.AluOpType
ACT = mybir.ActivationFunctionType
AX = mybir.AxisListType

L = 512
T4 = 4
KB = 8
FB = 22
NRAW = 3
RATES = (0.5, 0.5, 0.75, 0.25, 0.5)
NZ = 2
STEP = 2
NHL = 3
EPS = 1e-6
WAIT = "wait"
NEGBIG = -1.0e30
LAM_INIT = 0.2

PCOLS = {}


def _layout():
    at = 0
    for name, n in (
        ("ffn1_pre", 8), ("ffn1_post", 8), ("mix_pre", 8), ("gate_b", 16), ("conv_w", 96), ("conv_b", 24),
        ("norm_g", 16), ("subln", 1), ("mix_post", 8), ("ffn2_pre", 8), ("ffn2_post", 8),
        ("dt_bias", 1), ("a_log", 1), ("D", 32), ("lam", 256),
        ("norm1", 8), ("gconv_w", 96), ("g_bias", 1), ("g_alog", 1), ("gnorm", 1), ("ikg", 1), ("bgb", 16),
        ("norm2", 8), ("fconv_w", 132), ("fconv_b", 44), ("final", 8),
    ):
        PCOLS[name] = (at, n)
        at += n
    return at


NPAR = _layout()
CCOLS = {"ident": (0, 128), "ssdmask": (128, 128), "dist": (256, 512), "reset128": (768, 512),
         "neg": (128, 128), "bdincl": (256, 128), "level": (384, 768), "reset64": (1152, 512)}
NCA, NCB = 1280, 1664


class Tok:
    __slots__ = ("eng", "used", "val")

    def __init__(self, eng):
        self.eng, self.used, self.val = eng, False, 0


class Call:
    __slots__ = ("fn", "a", "k", "inc")

    def __init__(self, fn, a, k):
        self.fn, self.a, self.k, self.inc = fn, a, k, None

    def then_inc(self, sem, n):
        self.inc = (sem, n)
        return self

    def issue(self):
        ins = self.fn(*self.a, **self.k)
        if self.inc is not None:
            ins.then_inc(*self.inc)
        return ins


class Ops:

    def __init__(self, eng):
        self.eng = eng

    def dma_start(self, *a, **k):
        return Call(self.eng.dma_start, a, k)

    def matmul(self, *a, **k):
        return Call(self.eng.matmul, a, k)

    def transpose(self, *a, **k):
        return Call(self.eng.transpose, a, k)

    def activation(self, *a, **k):
        return Call(self.eng.activation, a, k)

    def copy(self, *a, **k):
        return Call(self.eng.copy, a, k)

    def mul(self, *a, **k):
        return Call(self.eng.mul, a, k)

    def memset(self, *a, **k):
        return Call(self.eng.memset, a, k)

    def tensor_copy(self, *a, **k):
        return Call(self.eng.tensor_copy, a, k)

    def tensor_tensor(self, *a, **k):
        return Call(self.eng.tensor_tensor, a, k)

    def tensor_scalar(self, *a, **k):
        return Call(self.eng.tensor_scalar, a, k)

    def scalar_tensor_tensor(self, *a, **k):
        return Call(self.eng.scalar_tensor_tensor, a, k)

    def tensor_tensor_scan(self, *a, **k):
        return Call(self.eng.tensor_tensor_scan, a, k)

    def reciprocal(self, *a, **k):
        return Call(self.eng.reciprocal, a, k)

    def reduce_max(self, *a, **k):
        return Call(self.eng.reduce_max, a, k)

    def reduce_sum(self, *a, **k):
        return Call(self.eng.reduce_sum, a, k)

    def max(self, *a, **k):
        return Call(self.eng.max, a, k)

    def match_replace(self, *a, **k):
        return Call(self.eng.match_replace, a, k)

class Queue:

    def __init__(self, name, eng):
        self.name, self.e, self.ops = name, Ops(eng), []

    def __call__(self, fn, *deps):
        t = Tok(self)
        self.ops.append([fn(self.e), deps, t])
        return t

    def later(self):
        t = Tok(self)
        op = [None, (), t]
        self.ops.append(op)
        return op


def flat(deps, out):
    for d in deps:
        if d is None:
            continue
        if isinstance(d, list) or (isinstance(d, tuple) and not (len(d) == 2 and isinstance(d[1], int))):
            flat(d, out)
        else:
            out.append(d)
    return out


class Pages:

    def __init__(self, bufs, name):
        self.free = [(b, []) for b in bufs]
        self.name = name
        self.low = len(bufs)

    def take(self):
        if not self.free:
            raise RuntimeError("out of " + self.name)
        b, w = self.free.pop(0)
        self.low = min(self.low, len(self.free))
        return Page(b, w, self)


class Page:
    __slots__ = ("b", "w", "pool", "t")

    def __init__(self, b, w, pool):
        self.b, self.w, self.pool, self.t = b, w, pool, None

    def __getitem__(self, k):
        return self.b[k]

    def release(self, *toks):
        self.pool.free.append((self.b, list(toks)))


def build(nc, d, out):
    SP, PE, AC = Queue("sp", nc.sync), Queue("pe", nc.tensor), Queue("act", nc.scalar)
    DV, GP = Queue("dve", nc.vector), Queue("pool", nc.gpsimd)
    ctx = ExitStack()
    sems = {}

    def sem(name):
        if name not in sems:
            sems[name] = ctx.enter_context(nc.semaphore("s_" + name))
        return sems[name]

    def sb(stack, name, shape, dt=F):
        return stack.enter_context(nc.sbuf_tensor(name, shape, dt))

    par = sb(ctx, "par", [128, NPAR])
    onesc = sb(ctx, "onesc", [128, 4, 128])
    small = sb(ctx, "small", [128, 1024])
    hT = sb(ctx, "hT", [128, KB, L])
    raw = [sb(ctx, f"raw{i}", [128, KB * 128]) for i in range(NRAW)]
    hl = [sb(ctx, f"hl{i}", [128, 2, KB * 128], R) for i in range(NHL)]
    uR = sb(ctx, "uR", [128, 2, KB, L], R)
    NA = 10
    fA = sb(ctx, "fA", [128, NA, L])
    banks = [ctx.enter_context(nc.psum_tensor(f"bank{i}", [128, L], F)) for i in range(8)]
    MB = Pages([b for b in banks[:3]], "main banks")
    SB = Pages([b for b in banks[3:]], "side banks")
    fp = Pages([fA[:, i, :] for i in range(NA)], "fA")

    def pc(name, j=0, n=1, rows=slice(0, 128)):
        a = PCOLS[name][0] + j
        return par[rows, a:a + n]

    def cc(name, rows=slice(0, 128)):
        a, n = CCOLS[name]
        return con[rows, a:a + n]

    small_at = [0]

    def sm(n):
        a = small_at[0]
        small_at[0] += n
        assert small_at[0] <= 1024, "small"
        return small[:, a:a + n]

    SP(lambda e: e.dma_start(par[:, :], d["params"]).then_inc(sem("p"), 16))
    for k in range(KB):
        SP(lambda e, k=k: e.dma_start(hT[:, k, :], d["xT"][k * 128:(k + 1) * 128, :]).then_inc(sem(f"x{k % 4}"), 16))
    t_par = ("p", 16)
    t_h = [(f"x{k % 4}", 16 * (k // 4 + 1)) for k in range(KB)]
    t_ones = [GP(lambda e, i=i, v=v: e.memset(onesc[:, i, :], v))
              for i, v in enumerate((1.0 / 1024, 1.0 / 512, 1.0 / 128, 1.0))]
    O1024, O512, O128, O1 = range(4)

    stream = {"n": 0, "late": {}, "done": {}, "split": {}}

    def reserve(j):
        a, v = AC.later(), DV.later()
        stream["late"][j] = (a, v)

    for j in range(NHL - 1):
        reserve(j)

    def panel(src, width):
        j = stream["n"]
        stream["n"] += 1
        a, v = stream["late"].pop(j)
        rs, hs = raw[j % NRAW], hl[j % NHL]
        landed = (f"raw{j % NRAW}", 16 * (j // NRAW + 1))
        SP(lambda e: e.dma_start(rs[:, 0:width], src).then_inc(sem(f"raw{j % NRAW}"), 16),
           stream["split"].get(j - NRAW))
        a[0] = AC.e.copy(hs[:, 0, 0:width], rs[:, 0:width])
        a[1] = (landed, stream["done"].get(j - NHL))
        v[0] = DV.e.tensor_tensor(hs[:, 1, 0:width], rs[:, 0:width], hs[:, 0, 0:width].bitcast(F), ALU.subtract)
        v[1] = (landed, a[2], stream["done"].get(j - NHL))
        stream["split"][j] = (v[2], a[2])
        reserve(j + NHL - 1)
        return j, hs, (a[2], v[2])

    def matpanel(bank, bw, p, kbs, kfirst, xhi, xlo, tx, first, last, off=0):
        j, hs, tw = p
        tok = None
        for q in range(kbs):
            k = kfirst + q
            w = slice((off + q) * 128, (off + q + 1) * 128)
            for i, (wi, x) in enumerate(((0, xhi), (0, xlo), (1, xhi))):
                st = first and q == 0 and i == 0
                sp_ = last and q == kbs - 1 and i == 2
                tok = PE(lambda e, wi=wi, w=w, x=x(k), st=st, sp_=sp_:
                         e.matmul(bank[:, :], hs[:, wi, w], x, start=st, stop=sp_),
                         tw, tx(k), bw if st else None)
        stream["done"][j] = tok
        return tok

    t_u = [None] * KB
    t_ulast = []

    def uhi(k):
        return uR[:, 0, k, :]

    def ulo(k):
        return uR[:, 1, k, :]

    def tu(k):
        return t_u[k]

    def ugemm(src):
        b = MB.take()
        p = panel(src, KB * 128)
        for q in range(0, KB, STEP):
            t = matpanel(b, b.w, p, STEP, q, uhi, ulo, tu, q == 0, q + STEP == KB, off=q)
            if q + STEP < KB:
                yield
        t_ulast[:] = [t]
        return b, t

    def rstd_of(bank, tok, eps=EPS):
        r = fp.take()
        s = AC(lambda e: e.activation(r[:, :], bank[:, :], ACT.Ln, bias=epsc), tok, r.w, t_eps)
        r.t = AC(lambda e: e.activation(r[:, :], r[:, :], ACT.Exp, scale=-0.5), s)
        bank.release(s)
        return r

    def sumsq(bank, wait, sources, which):
        t = None
        n = len(sources)
        for i, (x, tx) in enumerate(sources):
            q = fp.take()
            s = AC(lambda e, x=x, q=q: e.activation(q[:, :], x, ACT.Square), tx, q.w)
            t = PE(lambda e, q=q, i=i: e.matmul(bank[:, :], onesc[:, which, :], q[:, :], start=i == 0, stop=i == n - 1),
                   s, t_ones[which], wait if i == 0 else None)
            q.release(t)
        return t

    def split(hi, lo, x, tx, whi):
        a = AC(lambda e: e.copy(hi, x), tx, whi)
        v = DV(lambda e: e.tensor_tensor(lo, x, hi.bitcast(F), ALU.subtract), a, tx, whi)
        return (a, v)

    def side_rstd(sources, which):
        sq = []
        for x, tx in sources:
            q = fp.take()
            q.t = AC(lambda e: e.activation(q[:, :], x, ACT.Square), tx, q.w)
            sq.append(q)
        yield
        b = SB.take()
        n = len(sq)
        for i, q in enumerate(sq):
            t = PE(lambda e: e.matmul(b[:, :], onesc[:, which, :], q[:, :], start=i == 0, stop=i == n - 1),
                   q.t, t_ones[which], b.w)
            q.release(t)
        r = rstd_of(b, t)
        return r, t

    def norm_u(gname):
        b = SB.take()
        t = sumsq(b, b.w, [(hT[:, k, :], t_h[k]) for k in range(KB)], O1024)
        r = rstd_of(b, t)
        last = list(t_ulast)
        for k in range(KB):
            x = fp.take()
            v = DV(lambda e, k=k, x=x: e.scalar_tensor_tensor(out=x[:, :], in0=hT[:, k, :], scalar=pc(gname, k), in1=r[:, :],
                                                            op0=ALU.mult, op1=ALU.mult), t_h[k], r.t, x.w, t_par)
            t_u[k] = split(uhi(k), ulo(k), x[:, :], v, last)
            x.release(t_u[k])
        r.release(v)

    def post_norm(y, gn, half):
        b = SB.take()
        t = sumsq(b, b.w, [(y[k][:, :], y[k].t) for k in range(KB)], O1024)
        r = rstd_of(b, t)
        for k in range(KB):
            v = DV(lambda e, k=k: e.scalar_tensor_tensor(out=y[k][:, :], in0=y[k][:, :], scalar=pc(gn, k), in1=r[:, :],
                                                       op0=ALU.mult, op1=ALU.mult), y[k].t, t, r.t, t_par)
            v = DV(lambda e, k=k: e.scalar_tensor_tensor(out=hT[:, k, :], in0=y[k][:, :], scalar=0.5 if half else 1.0,
                                                       in1=hT[:, k, :], op0=ALU.mult, op1=ALU.add), v, t_h[k], t_u[k])
            t_h[k] = v
            y[k].release(v)
        r.release(t_h[KB - 1])

    def down(src, act, tact):
        for m in range(KB):
            b = MB.take()
            at = 0
            for n in (8, 8, 6):
                t = matpanel(b, b.w, panel(src[m, :, at * 128:(at + n) * 128], n * 128), n, at,
                             lambda k: act[:, 0, k, :], lambda k: act[:, 1, k, :], lambda k: tact[k],
                             at == 0, at + n == FB)
                at += n
            yield m, b, t

    def ffn(wg, wu, wd, gpre, gpost, act, wait):
        norm_u(gpre)
        tact = []
        for j in range(FB):
            bg, tg = yield from ugemm(wg[j])
            s = fp.take()
            a = AC(lambda e, s=s, bg=bg: e.activation(s[:, :], bg[:, :], ACT.Silu), tg, s.w)
            bg.release(a)
            bu, tu_ = yield from ugemm(wu[j])
            v = DV(lambda e, s=s, bu=bu: e.tensor_tensor(s[:, :], s[:, :], bu[:, :], ALU.mult), a, tu_)
            bu.release(v)
            tk = split(act[:, 0, j, :], act[:, 1, j, :], s[:, :], v, wait)
            s.release(tk)
            tact.append(tk)
        y = []
        for m, b, t in down(wd, act, tact):
            p = fp.take()
            p.t = AC(lambda e, p=p, b=b: e.copy(p[:, :], b[:, :]), t, p.w)
            b.release(p.t)
            y.append(p)
        post_norm(y, gpost, True)
        return t

    def conv(b, tb, wname, taps, col, ncol, bias, page):
        def w(i):
            return pc(wname, i * ncol + col)
        if bias is None:
            t = AC(lambda e: e.activation(page[:, :], b[:, :], ACT.Identity, scale=w(taps - 1)), tb, page.w, t_par)
        else:
            t = AC(lambda e: e.activation(page[:, :], b[:, :], ACT.Identity, scale=w(taps - 1), bias=pc(bias, col)),
                   tb, page.w, t_par)
        for s in range(1, taps):
            t = DV(lambda e, s=s: e.scalar_tensor_tensor(out=page[:, s:L], in0=b[:, 0:L - s], scalar=w(taps - 1 - s),
                                                       in1=page[:, s:L], op0=ALU.mult, op1=ALU.add), t)
        b.release(t)
        page.t = t
        return t

    def convsilu(b, tb, wname, col, bias):
        p = fp.take()
        t = conv(b, tb, wname, 4, col, 24, bias, p)
        p.t = AC(lambda e: e.activation(p[:, :], p[:, :], ACT.Silu), t)
        return p

    def turn(dst_bank, wait, src, tsrc, n=T4, cols=128):
        for t in range(n):
            tok = PE(lambda e, t=t: e.transpose(dst_bank[:, t * 128:(t + 1) * 128], src[:, t * 128:(t + 1) * 128], ident),
                     tsrc, wait, t_con)
        return tok

    def softplus(x, tx, rows):
        e1, w = fp.take(), fp.take()
        c = (rows, slice(0, L))
        t = DV(lambda e: e.scalar_tensor_tensor(out=e1[c], in0=x[c], scalar=-1.0, in1=x[c], op0=ALU.mult, op1=ALU.max), tx, e1.w)
        t = AC(lambda e: e.activation(e1[c], e1[c], ACT.Exp, scale=-1.0), t)
        ln = fp.take()
        tw = DV(lambda e: e.tensor_scalar(w[c], e1[c], 1.0, None, ALU.add), t, w.w)
        tl = AC(lambda e: e.activation(ln[c], w[c], ACT.Ln), tw, ln.w)
        t2 = DV(lambda e: e.scalar_tensor_tensor(out=e1[c], in0=w[c], scalar=-1.0, in1=e1[c], op0=ALU.add, op1=ALU.subtract), tw, t)
        t3 = DV(lambda e: e.reciprocal(w[c], w[c]), t2, tl)
        t4 = DV(lambda e: e.tensor_tensor(e1[c], e1[c], w[c], ALU.mult), t3, t2)
        t5 = DV(lambda e: e.tensor_tensor(ln[c], ln[c], e1[c], ALU.subtract), t4, tl)
        t6 = DV(lambda e: e.scalar_tensor_tensor(out=x[c], in0=x[c], scalar=0.0, in1=ln[c], op0=ALU.max, op1=ALU.add), t5)
        e1.release(t5)
        w.release(t4)
        ln.release(t6)
        return t6

    def finish(gen):
        for _ in gen:
            pass

    def value(gen):
        while True:
            try:
                next(gen)
            except StopIteration as e:
                return e.value

    def until(cond):
        while not cond():
            yield WAIT

    def room(n):
        yield from until(lambda: len(fp.free) >= n)

    def chain(*gens):
        for x in gens:
            yield from x

    def both(*gens):
        live = list(gens)
        while live:
            n = WAIT
            for x in list(live):
                try:
                    if next(x) is not WAIT:
                        n = None
                except StopIteration:
                    live.remove(x)
                    n = None
            if live:
                yield n

    def schedule(main, sides):
        END = object()
        sides = [[x, rate, 0.0] for x, rate in sides]
        going = True
        while going or sides:
            moved = False
            if going:
                r = next(main, END)
                going = r is not END
                moved = r is not WAIT and going
            for side in list(sides):
                side[2] += side[1]
                while side[2] >= 1:
                    side[2] -= 1
                    r = next(side[0], END)
                    if r is END:
                        sides.remove(side)
                        moved = True
                        break
                    if r is WAIT:
                        side[2] = 0.0
                        break
                    moved = True
                else:
                    moved = moved or not going
            assert moved or not (going or sides) or any(x[2] > 0 for x in sides), "streams wait for each other"

    def drop_pages():
        assert len(fp.free) == NA + NB_ and len(rp.free) == 16, (len(fp.free), len(rp.free))
        toks = [w for _, w in fp.free] + [w for _, w in rp.free]
        fp.free = [(fA[:, i, :], toks) for i in range(NA)]
        return toks

    def pv(P, W, i, V, o):
        b = SB.take()
        for k in range(i + 1):
            tp = PE(lambda e, k=k: e.transpose(b[:, k * 128:(k + 1) * 128], P[:, k * 128:(k + 1) * 128], ident), P.t, b.w)
        P.release(tp)
        A = fp.take()
        a = AC(lambda e: e.copy(A[:, 0:W], b[:, 0:W]), tp, A.w)
        b.release(a)
        yield
        b = SB.take()
        for k in range(i + 1):
            t = PE(lambda e, k=k: e.matmul(b[:, 0:128], V[:, k * 128:(k + 1) * 128], A[:, k * 128:(k + 1) * 128],
                                         start=k == 0, stop=k == i), a, V.t, b.w)
        A.release(t)
        o.t = AC(lambda e: e.copy(o[:, i * 128:(i + 1) * 128], b[:, 0:128]), t, o.w)
        b.release(o.t)
        return t

    epsc = sm(1)
    t_eps = DV(lambda e: e.memset(epsc, EPS))

    with ExitStack() as ph:
        act = sb(ph, "act1", [128, 2, FB, L], R)
        t_phase = value(ffn(d["w1g"], d["w1u"], d["w1d"], "ffn1_pre", "ffn1_post", act, None))

    stop = d.get("stop", 99)
    if stop >= 2:
      with ExitStack() as ph:
        con = sb(ph, "con1", [128, NCA])
        t_con = ("c1", 16)
        SP(lambda e: e.dma_start(con[:, :], d["consts1"]).then_inc(sem("c1"), 16), t_phase)
        ident = con[:, 0:128]
        SSDMASK = cc("ssdmask")
        mR = sb(ph, "mR1", [128, 16, L], R)
        NB_ = 25
        fB = sb(ph, "fB1", [128, NB_, L])
        for i in range(NB_):
            fp.free.append((fB[:, i, :], [t_phase]))
        rp = Pages([mR[:, i, :] for i in range(16)], "R pages")
        for i in range(16):
            rp.free[i] = (rp.free[i][0], [t_phase])
        acN, alast, cdec, ea, ddec = sm(128), sm(128), sm(128), sm(128), sm(128)
        dtN = sm(128)

        def n3(x):
            return x.rearrange("p (t h) -> p t h", t=T4)

        norm_u("mix_pre")
        WIN = d["win"]
        acum = {}

        def decay_side(dt):
            t = softplus(dt, dt.t, slice(0, 32))
            aex = sm(1)
            ta = AC(lambda e: e.activation(aex[0:32, :], pc("a_log", rows=slice(0, 32)), ACT.Exp), t_par)
            a, ac = fp.take(), fp.take()
            t1 = DV(lambda e: e.tensor_scalar(a[0:32, :], dt[0:32, :], aex[0:32, :], -1.0, ALU.mult, ALU.mult), t, ta, a.w)
            t2 = DV(lambda e: e.tensor_tensor_scan(ac[0:32, :], con[0:32, CCOLS["reset128"][0]:CCOLS["reset128"][0] + L],
                                                 a[0:32, :], 0.0, ALU.mult, ALU.add), t1, ac.w, t_con)
            a.release(t2)
            yield
            yield
            yield
            b = SB.take()
            for q in range(T4):
                PE(lambda e, q=q: e.transpose(b[:, q * 32:q * 32 + 32], ac[0:32, q * 128:(q + 1) * 128], con[0:32, 0:32]), t2, b.w)
            for q in range(T4):
                PE(lambda e, q=q: e.transpose(b[:, 128 + q * 32:160 + q * 32], dt[0:32, q * 128:(q + 1) * 128], con[0:32, 0:32]), t)
            for q in range(T4):
                lst = ac[0:32, q * 128 + 127:q * 128 + 128]
                tp = PE(lambda e, q=q, lst=lst: e.matmul(b[:, 256 + q * 32:288 + q * 32], lst.broadcast_to([32, 128]), con[0:32, 0:32],
                                              start=True, stop=True))
            t3 = DV(lambda e: e.tensor_copy(acN, b[:, 0:128]), tp)
            t4 = DV(lambda e: e.tensor_copy(dtN, b[:, 128:256]), tp)
            t5 = DV(lambda e: e.tensor_copy(alast, b[:, 256:384]), tp)
            b.release(t5)
            t6 = AC(lambda e: e.activation(cdec, alast, ACT.Exp), t5)
            t7 = AC(lambda e: e.activation(ea, acN, ACT.Exp), t3)
            t8 = DV(lambda e: e.tensor_tensor(ddec, alast, acN, ALU.subtract), t5, t3)
            t9 = AC(lambda e: e.activation(ddec, ddec, ACT.Exp), t8)
            dt.release(tp)
            acum.update(ac=ac, t=t2, tn=(t3, t4, t5, t6, t7, t9), users=[tp])

        grp = [dict() for _ in range(4)]

        def project_group(g):
            G = grp[g]
            xs = []
            for i in range(4):
                b, t = yield from ugemm(WIN[16 + 4 * g + i])
                xs.append(convsilu(b, t, "conv_w", 4 * g + i, "conv_b"))
                yield
            b, t = yield from ugemm(WIN[32 + g])
            G["B"] = convsilu(b, t, "conv_w", 16 + g, "conv_b")
            yield
            b, t = yield from ugemm(WIN[36 + g])
            G["C"] = convsilu(b, t, "conv_w", 20 + g, "conv_b")
            G["xs"] = xs
            yield

        def project_dt():
            b, t = yield from ugemm(WIN[80])
            dt = fp.take()
            dt.t = DV(lambda e: e.tensor_scalar(dt[0:32, :], b[0:32, :], pc("dt_bias", rows=slice(0, 32)), None, ALU.add),
                      t, dt.w, t_par)
            b.release(dt.t)
            acum["dt"] = dt
            yield

        def ssd_core(g):
            G = grp[g]
            xs, B, C = G["xs"], G["B"], G["C"]
            xsN, Xd = [], []
            hs = slice(8 * g, 8 * g + 8)
            tn = acum["tn"]
            for t in range(T4):
                b = SB.take()
                for i in range(4):
                    tp = PE(lambda e, i=i, t=t: e.transpose(b[:, i * 128:(i + 1) * 128], xs[i][:, t * 128:(t + 1) * 128], ident),
                            xs[i].t, b.w)
                y, x = fp.take(), fp.take()
                Db = pc("D", 8 * g, 8)[:, :, None].broadcast_to([128, 8, 64])
                v1 = DV(lambda e, b=b, x=x, t=t: e.tensor_tensor(
                    x[:, :].rearrange("p (h q) -> p h q", q=64), b[:, :].rearrange("p (h q) -> p h q", q=64),
                    n3(dtN)[:, t, hs][:, :, None].broadcast_to([128, 8, 64]), ALU.mult), tp, tn, x.w)
                v2 = DV(lambda e, b=b, y=y, Db=Db: e.tensor_tensor(
                    y[:, :].rearrange("p (h q) -> p h q", q=64), b[:, :].rearrange("p (h q) -> p h q", q=64), Db, ALU.mult),
                    tp, y.w)
                b.release(v1, v2)
                x.t, y.t = v1, v2
                xsN.append(y)
                Xd.append(x)
                yield
            for p in xs:
                p.release(tp)
            Y = xsN
            b = SB.take()
            tp = turn(b, b.w, B, B.t)
            BN = fp.take()
            BN.t = AC(lambda e: e.copy(BN[:, :], b[:, :]), tp, BN.w)
            b.release(BN.t)
            b = SB.take()
            for t in range(T4):
                c = slice(t * 128, (t + 1) * 128)
                tc = PE(lambda e, c=c: e.matmul(b[:, c], B[:, c], C[:, c], start=True, stop=True), B.t, C.t, b.w)
            B.release(tc)
            CB = fp.take()
            m = SSDMASK[:, None, :].broadcast_to([128, T4, 128])
            CB.t = DV(lambda e: e.tensor_tensor(CB[:, :].rearrange("p (t l) -> p t l", t=T4),
                                              b[:, :].rearrange("p (t l) -> p t l", t=T4), m, ALU.mult), tc, CB.w)
            b.release(CB.t)
            yield
            prev = None
            xds = []
            for t in range(1, T4):
                xd = fp.take()
                xd.t = DV(lambda e, t=t, xd=xd: e.tensor_tensor(
                    xd[:, :].rearrange("p (h q) -> p h q", q=64), Xd[t - 1][:, :].rearrange("p (h q) -> p h q", q=64),
                    n3(ddec)[:, t - 1, hs][:, :, None].broadcast_to([128, 8, 64]), ALU.mult), Xd[t - 1].t, xd.w, tn)
                xds.append(xd)
            yield
            for t in range(1, T4):
                xd = xds[t - 1]
                v = xd.t
                b = SB.take()
                ts = PE(lambda e, t=t, xd=xd, b=b: e.matmul(b[:, :], BN[:, (t - 1) * 128:t * 128], xd[:, :], start=True, stop=True),
                        v, BN.t, b.w)
                xd.release(ts)
                new = fp.take()
                if prev is None:
                    new.t = AC(lambda e, new=new, b=b: e.copy(new[:, :], b[:, :]), ts, new.w)
                else:
                    v = DV(lambda e, t=t, new=new, prev=prev: e.tensor_tensor(
                        new[:, :].rearrange("p (h q) -> p h q", q=64), prev[:, :].rearrange("p (h q) -> p h q", q=64),
                        n3(cdec)[:, t - 1, hs][:, :, None].broadcast_to([128, 8, 64]), ALU.mult), prev.t, new.w)
                    new.t = DV(lambda e, new=new, b=b: e.tensor_tensor(new[:, :], new[:, :], b[:, :], ALU.add), v, ts)
                    prev.release(v, prev_use)
                b.release(new.t)
                prev = new
                yield
                b = SB.take()
                prev_use = PE(lambda e, t=t, prev=prev, b=b: e.matmul(b[:, :], C[:, t * 128:(t + 1) * 128], prev[:, :],
                                                                   start=True, stop=True), prev.t, C.t, b.w)
                x = fp.take()
                v = DV(lambda e, t=t, x=x, b=b: e.tensor_tensor(
                    x[:, :].rearrange("p (h q) -> p h q", q=64), b[:, :].rearrange("p (h q) -> p h q", q=64),
                    n3(ea)[:, t, hs][:, :, None].broadcast_to([128, 8, 64]), ALU.mult), prev_use, x.w, tn)
                b.release(v)
                Y[t].t = DV(lambda e, t=t, x=x: e.tensor_tensor(Y[t][:, :], Y[t][:, :], x[:, :], ALU.add), v, Y[t].t)
                x.release(Y[t].t)
                yield
            prev.release(prev_use)
            BN.release(ts)
            C.release(prev_use)
            ac = acum["ac"]
            def front(hh):
                H = 8 * g + hh
                b = SB.take()
                tp = PE(lambda e: e.matmul(b[:, :], con[0:32, H:H + 1].broadcast_to([32, 128]), ac[0:32, :],
                                          start=True, stop=True), acum["t"], b.w)
                acum["users"][:] = [tp]
                E = fp.take()
                v = DV(lambda e: e.tensor_tensor(
                    E[:, :].rearrange("p (t l) -> p t l", t=T4), b[:, :].rearrange("p (t l) -> p t l", t=T4),
                    n3(acN)[:, :, H][:, :, None].broadcast_to([128, T4, 128]), ALU.subtract), tp, E.w, tn)
                b.release(v)
                v = DV(lambda e: e.tensor_scalar(E[:, :], E[:, :], 0.0, None, ALU.min), v)
                a = AC(lambda e: e.activation(E[:, :], E[:, :], ACT.Exp), v)
                E.t = DV(lambda e: e.tensor_tensor(E[:, :], E[:, :], CB[:, :], ALU.mult), a, CB.t)
                return E

            Es = [front(0)]
            yield
            yb = None
            for hh in range(8):
                if hh < 7:
                    Es.append(front(hh + 1))
                    yield
                e2, e1 = hh // 2, hh % 2
                if e1 == 0:
                    yb = SB.take()
                E = Es.pop(0)
                for t in range(T4):
                    tp = PE(lambda e, t=t: e.matmul(
                        yb[:, t * 128 + e1 * 64:t * 128 + e1 * 64 + 64], E[:, t * 128:(t + 1) * 128],
                        Xd[t][:, hh * 64:hh * 64 + 64], start=True, stop=True), E.t, yb.w)
                E.release(tp)
                if e1 == 1:
                    for t in range(T4):
                        v = DV(lambda e, t=t: e.tensor_tensor(
                            Y[t][:, e2 * 128:(e2 + 1) * 128], Y[t][:, e2 * 128:(e2 + 1) * 128],
                            yb[:, t * 128:(t + 1) * 128], ALU.add), tp, Y[t].t)
                        Y[t].t = v
                    yb.release(v)
                yield
            CB.release(v)
            for p in Xd:
                p.release(tp)
            G["Y"] = Y
            yield

        def project_z(g):
            G = grp[g]
            G["z"] = []
            for i in range(4):
                b, t = yield from ugemm(WIN[4 * g + i])
                s = fp.take()
                s.t = AC(lambda e, s=s, b=b: e.activation(s[:, :], b[:, :], ACT.Silu), t, s.w)
                b.release(s.t)
                G["z"].append(s)
                yield

        def gate_group(g):
            G = grp[g]
            Y, z = G["Y"], G["z"]
            for i in range(4):
                b = SB.take()
                for t in range(T4):
                    tp = PE(lambda e, i=i, t=t, b=b: e.transpose(b[:, t * 128:(t + 1) * 128], Y[t][:, i * 128:(i + 1) * 128], ident),
                            Y[t].t, b.w)
                z[i].t = DV(lambda e, i=i, b=b: e.tensor_tensor(z[i][:, :], z[i][:, :], b[:, :], ALU.mult), tp, z[i].t)
                b.release(z[i].t)
                yield
            for p in Y:
                p.release(tp)
            r, t = yield from side_rstd([(z[i][:, :], z[i].t) for i in range(4)], O512)
            yield
            G["p"] = []
            for i in range(4):
                v = DV(lambda e, i=i: e.scalar_tensor_tensor(out=z[i][:, :], in0=z[i][:, :], scalar=pc("norm_g", 4 * g + i),
                                                           in1=r[:, :], op0=ALU.mult, op1=ALU.mult), r.t, z[i].t, t)
                hi, lo = rp.take(), rp.take()
                tk = split(hi[:, :], lo[:, :], z[i][:, :], v, [hi.w, lo.w])
                z[i].release(tk)
                G["p"].append((hi, lo, tk))
            r.release(v)
            G["ready"] = True
            yield

        yssd = []

        def branch_group(g):
            G = grp[g]
            P = G["p"]
            for m2 in range(4):
                p = panel(d["wssd"][g, m2], KB * 128)
                for mi in range(2):
                    m = 2 * m2 + mi
                    b = MB.take()
                    t = matpanel(b, b.w, p, 4, 0, lambda k: P[k][0][:, :], lambda k: P[k][1][:, :], lambda k: P[k][2],
                                 True, True, off=4 * mi)
                    if g == 0:
                        y = fp.take()
                        y.t = AC(lambda e, y=y, b=b: e.copy(y[:, :], b[:, :]), t, y.w)
                        yssd.append(y)
                    else:
                        y = yssd[m]
                        y.t = DV(lambda e, y=y, b=b: e.tensor_tensor(y[:, :], y[:, :], b[:, :], ALU.add), t, y.t)
                    b.release(y.t)
                if m2 == 3:
                    for hi, lo, tk in P:
                        hi.release(t)
                        lo.release(t)
                    G["branched"] = True
                yield

        def ssd_side():
            yield from until(lambda: "dt" in acum)
            yield from decay_side(acum["dt"])
            for g in range(4):
                yield from until(lambda: "xs" in grp[g])
                yield from ssd_core(g)
                yield from until(lambda: len(grp[g].get("z", ())) == 4)
                yield from gate_group(g)

        def branch(g):
            yield from until(lambda: grp[g].get("ready"))
            yield from branch_group(g)

        lam = sm(8)
        lt = fp.take()
        t1 = DV(lambda e: e.tensor_tensor(lt[:, 0:128].rearrange("p (a b) -> p a b", a=2),
                                        pc("lam", 0, 256).rearrange("p (a c b) -> p a c b", a=2, c=2)[:, :, 0, :],
                                        pc("lam", 0, 256).rearrange("p (a c b) -> p a c b", a=2, c=2)[:, :, 1, :], ALU.mult),
                lt.w, t_par)
        t2 = DV(lambda e: e.reduce_sum(lam[:, 0:2], lt[:, 0:128].rearrange("p (a b) -> p a b", a=2), AX.X), t1)
        lt.release(t2)
        t3 = AC(lambda e: e.activation(lam[:, 2:4], lam[:, 0:2], ACT.Exp), t2)
        t4 = DV(lambda e: e.tensor_tensor(lam[:, 4:5], lam[:, 3:4], lam[:, 2:3], ALU.subtract), t3)
        t_lam = DV(lambda e: e.tensor_scalar(lam[:, 5:6], lam[:, 4:5], -LAM_INIT, None, ALU.add), t4)
        nlam = lam[:, 5:6]
        t_sg = DV(lambda e: e.tensor_scalar(lam[:, 6:7], pc("subln"), 1.0 - LAM_INIT, None, ALU.mult), t_par)
        sg = lam[:, 6:7]
        st = sm(64)
        heads = [dict() for _ in range(8)]
        stat = {"k": 0}

        def project_head(h):
            Hd = heads[h]
            for name, j in (("q", 40 + h), ("k", 48 + h), ("v", 56 + h)):
                b, t = yield from ugemm(WIN[j])
                s = fp.take()
                s.t = AC(lambda e, s=s, b=b, name=name: e.mul(s[:, :], b[:, :], 0.125) if name == "q" else e.copy(s[:, :], b[:, :]),
                         t, s.w)
                b.release(s.t)
                Hd[name] = s
                yield

        st_free = [None] * 4

        def att_head(h):
            Hd = heads[h]
            q, k, vT = Hd["q"], Hd["k"], Hd["v"]
            b = SB.take()
            tp = turn(b, b.w, vT, vT.t)
            vT.release(tp)
            V = fp.take()
            V.t = AC(lambda e: e.copy(V[:, :], b[:, :]), tp, V.w)
            b.release(V.t)
            yield
            o = fp.take()
            slope = float(2.0 ** (-8.0 * (h + 1) / 8))
            o.t = o.w

            def front(i):
                W = 128 * (i + 1)
                s_i = stat["k"] % 4
                stat["k"] += 1
                s0 = st[:, 16 * s_i:16 * s_i + 16]
                wst = st_free[s_i]
                Ps = []
                tm = []
                for m in range(2):
                    b = SB.take()
                    r = slice(64 * m, 64 * m + 64)
                    tp = PE(lambda e, r=r, b=b, i=i, W=W: e.matmul(b[:, 0:W], q[r, i * 128:(i + 1) * 128], k[r, 0:W],
                                                                 start=True, stop=True), q.t, k.t, b.w)
                    P = fp.take()
                    a0 = CCOLS["dist"][0]
                    v = DV(lambda e, b=b, P=P, i=i, W=W: e.scalar_tensor_tensor(
                        out=P[:, 0:W], in0=con[:, a0 + 384 - 128 * i:a0 + 512], scalar=slope, in1=b[:, 0:W],
                        op0=ALU.mult, op1=ALU.add), tp, P.w)
                    b.release(v)
                    P.t = v
                    tm.append(DV(lambda e, P=P, m=m, W=W, s0=s0: e.reduce_max(s0[:, m:m + 1], P[:, 0:W], AX.X), v, wst))
                    Ps.append(P)
                tm = DV(lambda e, s0=s0: e.tensor_scalar(s0[:, 2:4], s0[:, 0:2], -1.0, None, ALU.mult), tm)
                te = []
                for m in range(2):
                    te.append(AC(lambda e, P=Ps[m], m=m, W=W, s0=s0: e.activation(
                        P[:, 0:W], P[:, 0:W], ACT.Exp, bias=s0[:, 2 + m:3 + m], accum_out=s0[:, 4 + m:5 + m]), tm))
                v = DV(lambda e, s0=s0: e.reciprocal(s0[:, 6:8], s0[:, 4:6]), te)
                v2 = DV(lambda e, s0=s0: e.tensor_tensor(s0[:, 8:9], s0[:, 7:8], nlam, ALU.mult), v, t_lam)
                v3 = DV(lambda e, P=Ps[1], W=W, s0=s0: e.tensor_scalar(P[:, 0:W], P[:, 0:W], s0[:, 8:9], None, ALU.mult), v2, te)
                v4 = DV(lambda e, P=Ps[0], Q=Ps[1], W=W, s0=s0: e.scalar_tensor_tensor(
                    out=P[:, 0:W], in0=P[:, 0:W], scalar=s0[:, 6:7], in1=Q[:, 0:W], op0=ALU.mult, op1=ALU.add), v3, te)
                st_free[s_i] = v4
                Ps[1].release(v4)
                Ps[0].t = v4
                return Ps[0], W, tp

            Pq = [front(0)]
            yield
            for i in range(T4):
                if i < T4 - 1:
                    Pq.append(front(i + 1))
                    yield
                P, W, tp = Pq.pop(0)
                tpv = yield from pv(P, W, i, V, o)
                yield
            q.release(tp)
            k.release(tp)
            V.release(tpv)
            r, t = yield from side_rstd([(o[:, :], o.t)], O128)
            v = DV(lambda e: e.scalar_tensor_tensor(out=o[:, :], in0=o[:, :], scalar=sg, in1=r[:, :], op0=ALU.mult, op1=ALU.mult),
                   r.t, o.t, t, t_sg)
            r.release(v)
            hi, lo = rp.take(), rp.take()
            tk = split(hi[:, :], lo[:, :], o[:, :], v, [hi.w, lo.w])
            o.release(tk)
            Hd["o"] = (hi, lo, tk)
            yield

        def gates(names_m):
            for m in names_m:
                b, t = yield from ugemm(WIN[64 + m])
                s = fp.take()
                a = AC(lambda e, s=s, b=b, m=m: e.activation(s[:, :], b[:, :], ACT.Sigmoid, bias=pc("gate_b", m)), t, s.w, t_par)
                b.release(a)
                y = yssd[m]
                y.t = DV(lambda e, s=s, y=y: e.tensor_tensor(y[:, :], y[:, :], s[:, :], ALU.mult), a, y.t)
                s.release(y.t)
                yield

        def att_side():
            for h in range(0, 8, 2):
                yield from until(lambda: "v" in heads[h + 1] and "Y" in grp[3])
                yield from both(att_head(h), att_head(h + 1))

        def chained(h):
            yield from until(lambda: h < 4 or "o" in heads[h - 4])
            yield from project_head(h)

        main = chain(project_dt(), project_group(0), project_group(1), project_z(0),
                     room(8), project_group(2), branch(0), project_z(1), room(8), project_group(3), branch(1), project_z(2),
                     room(8), project_head(0), project_head(1), branch(2), project_z(3), room(8), project_head(2),
                     project_head(3), branch(3), chained(4), chained(5), chained(6), chained(7), gates(range(8)))
        schedule(main, [(ssd_side(), RATES[0]), (att_side(), RATES[1])])
        acum["ac"].release(acum["users"])
        yatt = []
        for m in range(KB):
            b = MB.take()
            t = matpanel(b, b.w, panel(d["wda"][m], KB * 128), KB, 0, lambda k: heads[k]["o"][0][:, :],
                         lambda k: heads[k]["o"][1][:, :], lambda k: heads[k]["o"][2], True, True)
            y = fp.take()
            y.t = AC(lambda e, y=y, b=b: e.copy(y[:, :], b[:, :]), t, y.w)
            b.release(y.t)
            yatt.append(y)
        for k in range(8):
            heads[k]["o"][0].release(t)
            heads[k]["o"][1].release(t)
        mg = []
        for m in range(KB):
            b, t = value(ugemm(WIN[72 + m]))
            s = fp.take()
            a = AC(lambda e, s=s, b=b, m=m: e.activation(s[:, :], b[:, :], ACT.Sigmoid, bias=pc("gate_b", 8 + m)), t, s.w, t_par)
            b.release(a)
            v = DV(lambda e, s=s, m=m: e.tensor_tensor(s[:, :], s[:, :], yatt[m][:, :], ALU.mult), a, yatt[m].t)
            yatt[m].release(v)
            v = DV(lambda e, s=s, m=m: e.tensor_tensor(s[:, :], s[:, :], yssd[m][:, :], ALU.add), v, yssd[m].t)
            yssd[m].release(v)
            hi, lo = rp.take(), rp.take()
            tk = split(hi[:, :], lo[:, :], s[:, :], v, [hi.w, lo.w])
            s.release(tk)
            mg.append((hi, lo, tk))
        y = []
        for m in range(KB):
            b = MB.take()
            t = matpanel(b, b.w, panel(d["wout"][m], KB * 128), KB, 0, lambda k: mg[k][0][:, :], lambda k: mg[k][1][:, :],
                         lambda k: mg[k][2], True, True)
            p = fp.take()
            p.t = AC(lambda e, p=p, b=b: e.copy(p[:, :], b[:, :]), t, p.w)
            b.release(p.t)
            y.append(p)
        for hi, lo, tk in mg:
            hi.release(t)
            lo.release(t)
        post_norm(y, "mix_post", False)
        t_all = drop_pages()

    if stop >= 3:
      with ExitStack() as ph:
        act = sb(ph, "act2", [128, 2, FB, L], R)
        t_phase = value(ffn(d["w2g"], d["w2u"], d["w2d"], "ffn2_pre", "ffn2_post", act, (t_all,)))

    if stop >= 4:
      with ExitStack() as ph:
        con = sb(ph, "con2", [128, NCB])
        t_con = ("c2", 16)
        SP(lambda e: e.dma_start(con[:, :], d["consts2"]).then_inc(sem("c2"), 16), t_phase)
        ident = con[:, 0:128]
        BDI, NEG = cc("bdincl"), cc("neg")
        fB = sb(ph, "fB2", [128, NB_, L])
        for i in range(NB_):
            fp.free.append((fB[:, i, :], [t_phase]))
        gxs = ExitStack()
        gxt = sb(gxs, "gx", [128, 16, L])
        gp = Pages([gxt[:, i, :] for i in range(16)], "gx pages")
        gp.free = [(b_, [t_phase]) for b_, _ in gp.free]
        norm_u("norm1")
        W2 = d["win2"]
        nar = NN = N3 = t_nar = t_NN = S0 = None

        def project_narrow():
            nonlocal S0
            S0 = yield from ugemm(W2[32])

        def narrow_side():
            nonlocal nar, NN, N3, t_nar, t_NN
            yield from until(lambda: S0 is not None)
            b, t = S0
            nar = fp.take()
            t0 = DV(lambda e: e.tensor_scalar(nar[:, :], b[:, :], pc("g_bias"), None, ALU.add), t, nar.w, t_par)
            t_b = AC(lambda e: e.activation(nar[32:64, :], nar[32:64, :], ACT.Sigmoid), t0)
            ISC = float((8 ** -0.5) * (64 ** -0.5))
            t_w = DV(lambda e: e.tensor_scalar(nar[64:96, :], nar[64:96, :], ISC, None, ALU.mult), t0)
            b.release(t0)
            gex = sm(1)
            ta = AC(lambda e: e.activation(gex, pc("g_alog"), ACT.Exp), t_par)
            tgs = []
            for r in (slice(0, 32), slice(96, 128)):
                t = softplus(nar, t0, r)
                t = DV(lambda e, r=r: e.tensor_scalar(nar[r, :], nar[r, :], gex[r, :], -1.0, ALU.mult, ALU.mult), t, ta)
                a0 = CCOLS["reset64"][0]
                g_ = fp.take()
                t = DV(lambda e, r=r, g_=g_: e.tensor_tensor_scan(g_[r, :], con[r, a0:a0 + L], nar[r, :], 0.0, ALU.mult, ALU.add), t, g_.w)
                if r.start == 0:
                    t = DV(lambda e, r=r, g_=g_: e.tensor_copy(nar[r, :], g_[r, :]), t)
                else:
                    t = DV(lambda e, r=r, g_=g_: e.tensor_tensor(
                        nar[r, :].rearrange("p (c l) -> p c l", l=64),
                        g_[r, :].rearrange("p (c l) -> p c l", l=64)[:, :, 63:64].broadcast_to([32, 8, 64]),
                        g_[r, :].rearrange("p (c l) -> p c l", l=64), ALU.subtract), t)
                g_.release(t)
                tgs.append(t)
            t_nar = [tgs, t_b, t_w]
            yield
            yield
            yield
            yield
            b = SB.take()
            tp = turn(b, b.w, nar, t_nar)
            NN = fp.take()
            t = AC(lambda e: e.copy(NN[:, :], b[:, :]), tp, NN.w)
            b.release(t)
            N3 = NN[:, :].rearrange("p (t c) -> p t c", t=T4)
            t1 = AC(lambda e: e.activation(N3[:, :, 8:16], N3[:, :, 0:8], ACT.Exp), t)
            t2 = DV(lambda e: e.tensor_tensor(N3[:, :, 8:16], N3[:, :, 8:16], N3[:, :, 32:40], ALU.mult), t1)
            t3 = AC(lambda e: e.activation(N3[:, :, 96:104], N3[:, :, 96:104], ACT.Exp), t)
            t_NN = [t, t1, t2, t3]

        def v3(p):
            return p[:, :].rearrange("p (t l) -> p t l", t=T4)

        def bc(col):
            return N3[:, :, col:col + 1].broadcast_to([128, T4, 128])

        def bm(ap):
            return ap[:, None, :].broadcast_to([128, T4, 128])

        S = [dict() for _ in range(8)]
        zg = [None] * 8

        def project_gdn(h):
            for name, j in (("q", h), ("k", 8 + h), ("v", 16 + h)):
                b, t = yield from ugemm(W2[j])
                S[h][name] = convsilu(b, t, "gconv_w", j, None)
                yield

        def project_zg(h):
            b, t = yield from ugemm(W2[24 + h])
            z = fp.take()
            a = AC(lambda e, z=z, b=b: e.activation(z[:, :], b[:, :], ACT.Silu), t, z.w)
            b.release(a)
            yield
            b, t = yield from ugemm(W2[50 + h])
            s = fp.take()
            a2 = AC(lambda e, s=s, b=b, h=h: e.activation(s[:, :], b[:, :], ACT.Sigmoid, bias=pc("bgb", h)), t, s.w, t_par)
            b.release(a2)
            z.t = DV(lambda e, s=s, z=z: e.tensor_tensor(z[:, :], z[:, :], s[:, :], ALU.mult), a, a2)
            s.release(z.t)
            zg[h] = z
            yield

        def l2(x, scale):
            r, t = yield from side_rstd([(x[:, :], x.t)], O1)
            x.t = DV(lambda e: e.scalar_tensor_tensor(out=x[:, :], in0=x[:, :], scalar=scale, in1=r[:, :], op0=ALU.mult, op1=ALU.mult),
                     r.t, x.t, t)
            r.release(x.t)

        def gdn_prep(h):
            H = S[h]
            q, k, v = H["q"], H["k"], H["v"]
            yield from both(l2(k, 1.0), l2(q, float(128 ** -0.5)))
            yield
            gb = SB.take()
            tg = PE(lambda e: e.matmul(gb[:, :], con[0:32, h:h + 1].broadcast_to([32, 128]), nar[0:32, :], start=True, stop=True),
                    t_nar, gb.w)
            eg = fp.take()
            eg.t = AC(lambda e: e.activation(eg[:, :], gb[:, :], ACT.Exp), tg, eg.w)
            gm = fp.take()
            t = DV(lambda e: e.tensor_tensor(v3(gm), v3(gb), bc(h), ALU.subtract), tg, eg.t, gm.w, t_NN)
            gb.release(eg.t, t)
            t = DV(lambda e: e.tensor_scalar(gm[:, :], gm[:, :], 0.0, None, ALU.min), t)
            t_g = AC(lambda e: e.activation(gm[:, :], gm[:, :], ACT.Exp), t)
            t_gm = DV(lambda e: e.tensor_tensor(v3(gm), v3(gm), bm(BDI), ALU.mult), t_g)
            yield
            bb = SB.take()
            tb = PE(lambda e: e.matmul(bb[:, :], con[32:64, 32 + h:33 + h].broadcast_to([32, 128]), nar[32:64, :], start=True, stop=True),
                    t_nar, bb.w)
            AT = gp.take()
            ta = DV(lambda e: e.tensor_tensor(AT[:, :], gm[:, :], bb[:, :], ALU.mult), tb, t_gm, AT.w)
            bb.release(ta)
            kk, qk = SB.take(), SB.take()
            for t in range(T4):
                c = slice(t * 128, (t + 1) * 128)
                t1 = PE(lambda e, c=c: e.matmul(kk[:, c], k[:, c], k[:, c], start=True, stop=True), k.t, kk.w)
                t2 = PE(lambda e, c=c: e.matmul(qk[:, c], k[:, c], q[:, c], start=True, stop=True), q.t, qk.w)
            AT.t = DV(lambda e: e.tensor_tensor(AT[:, :], AT[:, :], kk[:, :], ALU.mult), t1, ta)
            kk.release(AT.t)
            gm.t = DV(lambda e: e.tensor_tensor(gm[:, :], gm[:, :], qk[:, :], ALU.mult), t2, t_gm, ta)
            qk.release(gm.t)
            H["att"] = gm
            q.t = DV(lambda e: e.tensor_tensor(q[:, :], q[:, :], eg[:, :], ALU.mult), q.t, eg.t, t2)
            H["qg"], H["eg"] = q, eg
            yield
            b = SB.take()
            tp = turn(b, b.w, k, k.t)
            k.release(tp)
            kbe, kd = gp.take(), fp.take()
            kbe.t = DV(lambda e: e.tensor_tensor(v3(kbe), v3(b), bc(8 + h), ALU.mult), tp, kbe.w, t_NN)
            kd.t = DV(lambda e: e.tensor_tensor(v3(kd), v3(b), bc(96 + h), ALU.mult), tp, kd.w, t_NN)
            b.release(kbe.t, kd.t)
            H["kd"] = kd
            b2 = SB.take()
            tp = turn(b2, b2.w, v, v.t)
            v.release(tp)
            vb = gp.take()
            vb.t = DV(lambda e: e.tensor_tensor(v3(vb), v3(b2), bc(32 + h), ALU.mult), tp, vb.w, t_NN)
            b2.release(vb.t)
            yield
            lv = CCOLS["level"][0]
            U, Tm, Y, Ak = gp.take(), gp.take(), gp.take(), gp.take()
            t = DV(lambda e: e.tensor_tensor(v3(U), v3(AT), bm(con[:, lv:lv + 128]), ALU.mult), AT.t, U.w)
            tU = DV(lambda e: e.tensor_tensor(v3(U), bm(ident), v3(U), ALU.subtract), t)
            Ak2 = gp.take()
            Aks = {}

            def level(lev):
                A, w = ((Ak, Ak.w), (Ak2, Ak2.w))[lev % 2] if lev < 3 else (Aks[lev - 2][0], Aks[lev - 2][2])
                m = con[:, lv + 128 * lev:lv + 128 * lev + 128]
                t = GP(lambda e: e.tensor_tensor(v3(A), v3(AT), bm(m), ALU.mult), AT.t, w, t_con)
                Aks[lev] = [A, t, None]

            level(1)
            level(2)
            yield
            b = SB.take()
            tp = turn(b, b.w, U, tU)
            tT = AC(lambda e, b=b: e.copy(Tm[:, :], b[:, :]), tp, Tm.w)
            b.release(tT)
            wY = Y.w
            yield
            for lev in range(1, 6):
                A, tA, _ = Aks[lev]
                b = SB.take()
                for t in range(T4):
                    c = slice(t * 128, (t + 1) * 128)
                    tp = PE(lambda e, c=c, b=b: e.matmul(b[:, c], A[:, c], Tm[:, c], start=True, stop=True), tA, tT, b.w)
                wA = tp
                Aks[lev][2] = tp
                if lev < 4:
                    level(lev + 2)
                tY = AC(lambda e, b=b: e.copy(Y[:, :], b[:, :]), tp, wY)
                b.release(tY)
                yield
                b = SB.take()
                for t in range(T4):
                    c = slice(t * 128, (t + 1) * 128)
                    tp = PE(lambda e, c=c, b=b: e.matmul(b[:, c], Y[:, c], U[:, c], start=True, stop=True), tY, tU, b.w)
                if lev < 5:
                    b2 = SB.take()
                    for t in range(T4):
                        c = slice(t * 128, (t + 1) * 128)
                        tp2 = PE(lambda e, c=c, b2=b2: e.matmul(b2[:, c], U[:, c], Y[:, c], start=True, stop=True), b2.w)
                    tT = DV(lambda e, b2=b2: e.tensor_tensor(Tm[:, :], Tm[:, :], b2[:, :], ALU.subtract), tp2, tT, wA)
                    b2.release(tT)
                    tp = tp2
                wY = tp
                tU = DV(lambda e, b=b: e.tensor_tensor(U[:, :], U[:, :], b[:, :], ALU.subtract), tp, tU)
                b.release(tU)
                yield
            Tm.release(tT, wA)
            Y.release(wY)
            Ak.release(wA)
            Ak2.release(wA)
            AT.release(tA)
            b, b2 = SB.take(), SB.take()
            for t in range(T4):
                c = slice(t * 128, (t + 1) * 128)
                t1 = PE(lambda e, c=c: e.matmul(b[:, c], U[:, c], vb[:, c], start=True, stop=True), tU, vb.t, b.w)
                t2 = PE(lambda e, c=c: e.matmul(b2[:, c], kbe[:, c], U[:, c], start=True, stop=True), kbe.t, b2.w)
            uN, wT = fp.take(), fp.take()
            uN.t = AC(lambda e: e.copy(uN[:, :], b[:, :]), t1, uN.w)
            wT.t = AC(lambda e: e.copy(wT[:, :], b2[:, :]), t2, wT.w)
            b.release(uN.t)
            b2.release(wT.t)
            U.release(t2)
            vb.release(t1)
            kbe.release(t2)
            H["u"], H["w"] = uN, wT
            yield

        def gdn_scan(hs):
            n = len(hs)
            st_ = fp.take()
            vn = fp.take()
            o = {h: fp.take() for h in hs}
            t_S = [st_.w] * n
            t_Su = None
            wv = vn.w
            for c in range(8):
                t, half = c // 2, c % 2
                r = slice(64 * half, 64 * half + 64)
                cs = slice(c * 64, c * 64 + 64)
                if c:
                    b = SB.take()
                    for i, h in enumerate(hs):
                        tp = PE(lambda e, i=i, h=h, b=b, r=r, cs=cs: e.matmul(
                            b[r, i * 128:(i + 1) * 128], S[h]["w"][:, cs], st_[:, i * 128:(i + 1) * 128], start=True, stop=True),
                            S[h]["w"].t, t_S[i], b.w)
                tv = []
                for i, h in enumerate(hs):
                    ic = slice(i * 128, (i + 1) * 128)
                    tc = slice(t * 128, (t + 1) * 128)
                    if c:
                        tv.append(DV(lambda e, h=h, b=b, ic=ic, tc=tc, r=r: e.tensor_tensor(
                            vn[r, ic], S[h]["u"][r, tc], b[r, ic], ALU.subtract), tp, wv, S[h]["u"].t))
                    else:
                        tv.append(DV(lambda e, h=h, ic=ic, tc=tc, r=r: e.tensor_copy(vn[r, ic], S[h]["u"][r, tc]), wv, S[h]["u"].t))
                if c:
                    b.release(tv)
                yield
                if c < 7:
                    bs = SB.take()
                    for i, h in enumerate(hs):
                        ic = slice(i * 128, (i + 1) * 128)
                        tc = slice(t * 128, (t + 1) * 128)
                        ts = PE(lambda e, h=h, bs=bs, ic=ic, tc=tc, r=r: e.matmul(
                            bs[:, ic], S[h]["kd"][r, tc], vn[r, ic], start=True, stop=True), tv, S[h]["kd"].t, bs.w)
                if not half:
                    bo = SB.take()
                for i, h in enumerate(hs):
                    ic = slice(i * 128, (i + 1) * 128)
                    if c:
                        PE(lambda e: e.matmul(bo[r, ic], S[h]["qg"][:, cs], st_[:, ic], start=True, stop=False),
                           S[h]["qg"].t, bo.w, t_S[i])
                    to = PE(lambda e: e.matmul(bo[r, ic], S[h]["att"][r, cs], vn[r, ic], start=c == 0, stop=True),
                            tv, S[h]["att"].t, bo.w)
                wv = to
                if c < 7:
                    for i, h in enumerate(hs):
                        ic = slice(i * 128, (i + 1) * 128)
                        if c:
                            t_S[i] = DV(lambda e, h=h, bs=bs, ic=ic, c=c: e.scalar_tensor_tensor(
                                out=st_[:, ic], in0=st_[:, ic], scalar=S[h]["eg"][:, c * 64 + 63:c * 64 + 64], in1=bs[:, ic],
                                op0=ALU.mult, op1=ALU.add), ts, to, t_S[i], S[h]["eg"].t)
                        else:
                            t_S[i] = DV(lambda e, bs=bs, ic=ic: e.tensor_copy(st_[:, ic], bs[:, ic]), ts, t_S[i])
                    bs.release(*t_S)
                if half:
                    for i, h in enumerate(hs):
                        o[h].t = AC(lambda e: e.copy(o[h][:, t * 128:(t + 1) * 128], bo[:, i * 128:(i + 1) * 128]), to, o[h].w)
                    bo.release(o[hs[-1]].t)
                yield
            st_.release(to)
            vn.release(to)
            for h in hs:
                for name in ("w", "u", "kd", "qg", "att", "eg"):
                    S[h][name].release(to, t_S, tv)
            for h in hs:
                S[h]["o"] = o[h]

        def gdn_out(h):
            o = S[h]["o"]
            q = fp.take()
            a = AC(lambda e: e.activation(q[:, :], o[:, :], ACT.Square, scale=float(128 ** -0.5)), o.t, q.w)
            rs = ors[:, 4 * h:4 * h + 4]
            v = DV(lambda e: e.reduce_sum(rs, v3(q), AX.X), a)
            q.release(v)
            a = AC(lambda e: e.activation(rs, rs, ACT.Ln, bias=epsc), v, t_eps)
            a = AC(lambda e: e.activation(rs, rs, ACT.Exp, scale=-0.5), a)
            v = DV(lambda e: e.tensor_tensor(v3(o), v3(o), rs[:, :, None].broadcast_to([128, T4, 128]), ALU.mult), a, o.t)
            yield
            yield
            b = SB.take()
            tp = turn(b, b.w, o, v)
            o.release(tp)
            yield from until(lambda: zg[h] is not None)
            z = zg[h]
            z.t = DV(lambda e: e.scalar_tensor_tensor(out=z[:, :], in0=b[:, :], scalar=pc("gnorm"), in1=z[:, :],
                                                    op0=ALU.mult, op1=ALU.mult), tp, z.t)
            b.release(z.t)
            yield

        NGH = [(0, 1), (2, 3), (4, 5), (6, 7)]

        dq, dk, dv_, iq = [None] * 8, [None] * 2, [None] * 2, [None] * 4
        ikp = [None]

        def plain(j):
            b, t = yield from ugemm(W2[j])
            s = fp.take()
            s.t = AC(lambda e, s=s, b=b: e.copy(s[:, :], b[:, :]), t, s.w)
            b.release(s.t)
            return s

        def project_idx():
            x = yield from plain(49)
            yield
            b = SB.take()
            t = PE(lambda e: e.matmul(b[:, :], onesc[:, O128, :], x[:, :], start=True, stop=True), x.t, b.w)
            x.t = DV(lambda e: e.tensor_tensor(x[:, :], x[:, :], b[:, :], ALU.subtract), t)
            b.release(x.t)
            r, t = yield from side_rstd([(x[:, :], x.t)], O128)
            x.t = DV(lambda e: e.scalar_tensor_tensor(out=x[:, :], in0=x[:, :], scalar=pc("ikg"), in1=r[:, :], op0=ALU.mult, op1=ALU.mult),
                     r.t, x.t, t)
            r.release(x.t)
            ikp[0] = x
            yield
            for i in range(4):
                iq[i] = yield from plain(45 + i)
                yield

        def project_kv():
            for i in range(2):
                dk[i] = yield from plain(41 + i)
                yield
            for i in range(2):
                s = yield from plain(43 + i)
                b = SB.take()
                tp = turn(b, b.w, s, s.t)
                V = fp.take()
                V.t = AC(lambda e, V=V, b=b: e.copy(V[:, :], b[:, :]), tp, V.w)
                b.release(V.t)
                s.release(tp)
                dv_[i] = V
                yield

        masks = {}
        m8 = sm(8 * 3)
        cnt = sm(6)

        def indexer(i):
            W = 128 * (i + 1)
            x = ikp[0]
            sc = fp.take()
            sc.t = sc.w
            for h in range(8):
                r = slice(64 * (h % 2), 64 * (h % 2) + 64)
                b = SB.take()
                tp = PE(lambda e, h=h, r=r, b=b: e.matmul(b[:, 0:W], iq[h // 2][r, i * 128:(i + 1) * 128], x[r, 0:W],
                                                        start=True, stop=True), iq[h // 2].t, x.t, b.w)
                wcol = N3[:, i, 64 + h:65 + h]
                if h == 0:
                    v = DV(lambda e, b=b, wcol=wcol: e.tensor_scalar(sc[:, 0:W], b[:, 0:W], 0.0, wcol, ALU.max, ALU.mult),
                           tp, sc.t, t_NN)
                    b.release(v)
                else:
                    rl = fp.take()
                    a = AC(lambda e, b=b, rl=rl: e.activation(rl[:, 0:W], b[:, 0:W], ACT.Relu), tp, rl.w)
                    b.release(a)
                    v = DV(lambda e, rl=rl, wcol=wcol: e.scalar_tensor_tensor(
                        out=sc[:, 0:W], in0=rl[:, 0:W], scalar=wcol, in1=sc[:, 0:W], op0=ALU.mult, op1=ALU.add), a, sc.t, t_NN)
                    rl.release(v)
                sc.t = v
                if h % 2:
                    yield
            masks[i, "x"] = tp
            v = DV(lambda e: e.tensor_tensor(sc[:, W - 128:W], sc[:, W - 128:W], NEG, ALU.add), sc.t, t_con)
            wk = fp.take()
            top = m8[:, 8 * (i - 1):8 * i]
            t = DV(lambda e: e.max(top, sc[:, 0:W]), v)
            for n in range(15):
                src = sc if n == 0 else wk
                t = DV(lambda e, src=src: e.match_replace(out=wk[:, 0:W], in_to_replace=top, in_values=src[:, 0:W], imm_value=-3.0e38),
                       t, wk.w if n == 0 else None)
                t = DV(lambda e: e.max(top, wk[:, 0:W]), t)
                if n % 4 == 3:
                    yield
            c0, c1 = cnt[:, 2 * i - 2:2 * i - 1], cnt[:, 2 * i - 1:2 * i]
            gt, eq = wk, fp.take()
            thr = top[:, 7:8]
            t1 = DV(lambda e: e.tensor_scalar(gt[:, 0:W], sc[:, 0:W], thr, None, ALU.is_gt, ALU.add, accum_out=c0), t)
            t2 = DV(lambda e: e.tensor_scalar(eq[:, 0:W], sc[:, 0:W], thr, None, ALU.is_equal), t, eq.w)
            t3 = DV(lambda e: e.tensor_scalar(c1, c0, -1.0, 128.0, ALU.mult, ALU.add), t1)
            t4 = DV(lambda e: e.tensor_tensor_scan(sc[:, 0:W], onesc[:, O1, 0:1].broadcast_to([128, W]), eq[:, 0:W], 0.0, ALU.mult, ALU.add), t2, t_ones[O1])
            t5 = DV(lambda e: e.scalar_tensor_tensor(out=eq[:, 0:W], in0=sc[:, 0:W], scalar=c1, in1=eq[:, 0:W],
                                                   op0=ALU.is_le, op1=ALU.mult), t4, t3)
            t6 = DV(lambda e: e.tensor_tensor(gt[:, 0:W], gt[:, 0:W], eq[:, 0:W], ALU.add), t5, t1)
            t7 = DV(lambda e: e.tensor_scalar(gt[:, 0:W], gt[:, 0:W], -1.0, -NEGBIG, ALU.add, ALU.mult), t6)
            eq.release(t6)
            sc.release(t5)
            gt.t = t7
            masks[i] = gt
            yield

        stat2 = {"k": 0}
        st2_free = [None] * 8
        dsc = float(128 ** -0.5)

        def sparse_head(h):
            q, k, V = dq[h], dk[h // 4], dv_[h // 4]
            o = fp.take()

            def front(i):
                W = 128 * (i + 1)
                s_i = stat2["k"] % 8
                stat2["k"] += 1
                s0 = st2[:, 8 * s_i:8 * s_i + 8]
                wst = st2_free[s_i]
                b = SB.take()
                tp = PE(lambda e, b=b, i=i, W=W: e.matmul(b[:, 0:W], q[:, i * 128:(i + 1) * 128], k[:, 0:W], start=True, stop=True),
                        q.t, k.t, b.w)
                P = fp.take()
                mk = NEG if i == 0 else masks[i][:, 0:W]
                v = DV(lambda e, b=b, P=P, mk=mk, W=W: e.tensor_tensor(P[:, 0:W], b[:, 0:W], mk, ALU.add), tp, P.w,
                       masks[i].t if i else None)
                b.release(v)
                v = DV(lambda e, P=P, W=W, s0=s0: e.reduce_max(s0[:, 0:1], P[:, 0:W], AX.X), v, wst)
                v = DV(lambda e, s0=s0: e.tensor_scalar(s0[:, 1:2], s0[:, 0:1], -dsc, None, ALU.mult), v)
                a = AC(lambda e, P=P, W=W, s0=s0: e.activation(P[:, 0:W], P[:, 0:W], ACT.Exp, scale=dsc, bias=s0[:, 1:2],
                                                             accum_out=s0[:, 2:3]), v)
                v = DV(lambda e, s0=s0: e.reciprocal(s0[:, 3:4], s0[:, 2:3]), a)
                P.t = DV(lambda e, P=P, W=W, s0=s0: e.tensor_scalar(P[:, 0:W], P[:, 0:W], s0[:, 3:4], None, ALU.mult), v, a)
                st2_free[s_i] = P.t
                return P, W, tp

            Pq = [front(0)]
            yield
            for i in range(T4):
                if i < T4 - 1:
                    Pq.append(front(i + 1))
                    yield
                P, W, tp = Pq.pop(0)
                tpv = yield from pv(P, W, i, V, o)
                yield
            q.release(tp)
            S[h]["od"] = o
            S[h]["tpv"] = (tp, tpv)
            yield

        st2 = sm(64)
        ors = sm(32)

        def project_dq(h):
            dq[h] = yield from plain(33 + h)
            yield

        mg = [None] * 8

        def merge_heads(h):
            b, t = yield from ugemm(W2[58 + h])
            s = fp.take()
            a = AC(lambda e, s=s, b=b: e.activation(s[:, :], b[:, :], ACT.Sigmoid, bias=pc("bgb", 8 + h)), t, s.w)
            b.release(a)
            S[h]["sg"] = s
            s.t = a
            yield

        def merge_fin(h):
            s, o = S[h]["sg"], S[h]["od"]
            v = DV(lambda e: e.tensor_tensor(s[:, :], s[:, :], o[:, :], ALU.mult), s.t, o.t)
            o.release(v)
            v = DV(lambda e: e.tensor_tensor(s[:, :], s[:, :], zg[h][:, :], ALU.add), v, zg[h].t)
            zg[h].release(v)
            hi, lo = rp.take(), rp.take()
            tk = split(hi[:, :], lo[:, :], s[:, :], v, [hi.w, lo.w])
            s.release(tk)
            mg[h] = (hi, lo, tk)

        def gdn_side():
            yield from narrow_side()
            for hs in NGH:
                yield from until(lambda: "v" in S[hs[1]])
                yield from both(gdn_prep(hs[0]), gdn_prep(hs[1]))
                yield from gdn_scan(hs)
                yield from both(gdn_out(hs[0]), gdn_out(hs[1]))

        def index_side():
            yield from until(lambda: iq[3] is not None and NN is not None)
            yield from both(indexer(1), indexer(2))
            yield from indexer(3)
            ikp[0].release(masks[3, "x"])
            for x in iq:
                x.release(masks[3, "x"])

        def gate_b(h):
            yield from merge_heads(h)

        def pair(i):
            a, b_ = NGH[i]
            return chain(project_gdn(a), project_gdn(b_))

        def zgs(i):
            a, b_ = NGH[i]
            return chain(project_zg(a), project_zg(b_))

        def hold(i):
            return until(lambda: "w" in S[NGH[i][1]])

        main = chain(project_narrow(), pair(0), project_idx(), hold(0), zgs(0), pair(1), hold(1), zgs(1), pair(2),
                     hold(2), zgs(2), pair(3), hold(3), zgs(3), project_kv(), project_dq(0), project_dq(1))
        schedule(main, [(gdn_side(), RATES[2]), (index_side(), RATES[3])])
        assert len(gp.free) == 16
        gx_toks = [w for _, w in gp.free]
        gxs.close()
        mR = sb(ph, "mR2", [128, 16, L], R)
        rp = Pages([mR[:, i, :] for i in range(16)], "R pages")
        for i in range(16):
            rp.free[i] = (rp.free[i][0], gx_toks)

        def sparse_side():
            for h in range(0, 8, NZ):
                yield from until(lambda: all(dq[h + i] is not None for i in range(NZ)))
                yield from both(*[sparse_head(h + i) for i in range(NZ)])
                for i in range(NZ):
                    yield from until(lambda: "sg" in S[h + i])
                    merge_fin(h + i)
                    yield

        main = chain(merge_heads(0), merge_heads(1), *[chain(project_dq(h), project_dq(h + 1), room(9), merge_heads(h),
                                                             merge_heads(h + 1), room(9)) for h in (2, 4, 6)])
        schedule(main, [(sparse_side(), RATES[4])])
        for x in (*dk, *dv_):
            x.release(S[7]["tpv"])
        for i in (1, 2, 3):
            masks[i].release(S[7]["od"].t)
        nar.release(t_NN)
        NN.release(S[7]["od"].t)
        for m in range(KB):
            b = MB.take()
            t = matpanel(b, b.w, panel(d["wout2"][m], KB * 128), KB, 0, lambda k: mg[k][0][:, :], lambda k: mg[k][1][:, :],
                         lambda k: mg[k][2], True, True)
            t_h[m] = DV(lambda e, m=m, b=b: e.tensor_tensor(hT[:, m, :], hT[:, m, :], b[:, :], ALU.add), t, t_h[m])
            b.release(t_h[m])
        for hi, lo, tk in mg:
            hi.release(t)
            lo.release(t)
        t_all = drop_pages()

    if stop >= 5:
      with ExitStack() as ph:
        act = sb(ph, "act3", [128, 2, FB, L], R)
        norm_u("norm2")
        tact = []
        for j in range(FB):
            bg, tg = value(ugemm(d["w3"][j]))
            g_ = fp.take()
            t = conv(bg, tg, "fconv_w", 3, j, 44, "fconv_b", g_)
            a = AC(lambda e, g_=g_: e.activation(g_[:, :], g_[:, :], ACT.Silu), t)
            bu, tu_ = value(ugemm(d["w3"][FB + j]))
            u_ = fp.take()
            t = conv(bu, tu_, "fconv_w", 3, FB + j, 44, "fconv_b", u_)
            v = DV(lambda e, g_=g_, u_=u_: e.tensor_tensor(g_[:, :], g_[:, :], u_[:, :], ALU.mult), a, t)
            u_.release(v)
            tk = split(act[:, 0, j, :], act[:, 1, j, :], g_[:, :], v, [t_all])
            g_.release(tk)
            tact.append(tk)
        for m, b, t in down(d["w3d"], act, tact):
            t_h[m] = DV(lambda e, m=m, b=b: e.tensor_tensor(hT[:, m, :], hT[:, m, :], b[:, :], ALU.add), t, t_h[m])
            b.release(t_h[m])
        b = SB.take()
        t = sumsq(b, b.w, [(hT[:, k, :], t_h[k]) for k in range(KB)], O1024)
        r = rstd_of(b, t)
        for k in range(KB):
            t_h[k] = DV(lambda e, k=k: e.scalar_tensor_tensor(out=hT[:, k, :], in0=hT[:, k, :], scalar=pc("final", k), in1=r[:, :],
                                                            op0=ALU.mult, op1=ALU.mult), r.t, t_h[k], t)
    for k in range(KB):
        SP(lambda e, k=k: e.dma_start(out[k * 128:(k + 1) * 128, :], hT[:, k, :]).then_inc(sem("out"), 16), t_h[k])
    waits_at_end = [("out", 16 * KB)]

    queues = (SP, PE, AC, DV, GP)
    for q in queues:
        q.ops = [op for op in q.ops if op[0] is not None]
        for op in q.ops:
            op[1] = flat(op[1], [])
            for dep in op[1]:
                if isinstance(dep, Tok) and not (dep.eng is q and q is PE):
                    dep.used = True
    for q in queues:
        n = 0
        for op in q.ops:
            if op[2].used:
                n += 1
                op[2].val = n
        if n:
            sem(q.name)
    for q in queues:
        for op in q.ops:
            for dep in op[1]:
                if isinstance(dep, tuple):
                    sem(dep[0])

    def emit(q, eng):
        seen = {}
        table = None
        for fn, deps, tok in q.ops:
            need = {}
            for dep in deps:
                if isinstance(dep, Tok):
                    if dep.eng is q and q is PE:
                        continue
                    assert dep.val > 0
                    need[dep.eng.name] = max(need.get(dep.eng.name, 0), dep.val)
                else:
                    need[dep[0]] = max(need.get(dep[0], 0), dep[1])
            for s, v in need.items():
                if seen.get(s, 0) < v:
                    eng.wait_ge(sem(s), v)
                    seen[s] = v
            func = fn.a[2] if q is AC and len(fn.a) > 2 else None
            if func in (ACT.Ln, ACT.Exp) and table != "both":
                eng.preload_act_table_set("natural_log_exp_and_others")
                table = "both"
            elif func in (ACT.Silu, ACT.Sigmoid):
                table = func
            ins = fn.issue()
            if tok.used:
                ins.then_inc(sem(q.name), 1)

    with ctx:
        block = ctx.enter_context(nc.Block())

        @block.sync
        def _(e):
            emit(SP, e)
            for s, v in waits_at_end:
                e.wait_ge(sem(s), v)

        @block.tensor
        def _(e):
            emit(PE, e)

        @block.scalar
        def _(e):
            emit(AC, e)

        @block.vector
        def _(e):
            emit(DV, e)

        @block.gpsimd
        def _(e):
            emit(GP, e)


def blocks(w, n=128):
    K, M = w.shape
    return np.ascontiguousarray(w.reshape(K // 128, 128, M // n, n).transpose(2, 1, 0, 3).reshape(M // n, 128, K // 128 * n))


def constants():
    p = np.arange(128)[:, None]
    f = np.arange(128)[None, :]
    a = np.zeros((128, NCA), np.float32)
    b = np.zeros((128, NCB), np.float32)

    def put(x, name, v):
        at, n = CCOLS[name]
        x[:, at:at + n] = v

    put(a, "ident", p == f)
    put(b, "ident", p == f)
    put(a, "ssdmask", p <= f)
    k = np.arange(512)[None, :] - 384
    put(a, "dist", np.where(k <= p, (k - p).astype(np.float64), NEGBIG))
    put(a, "reset128", np.arange(512)[None, :] % 128 != 0)
    put(b, "reset64", np.arange(512)[None, :] % 64 != 0)
    put(b, "neg", np.where(f <= p, 0.0, NEGBIG))
    put(b, "bdincl", (p <= f) & (p // 64 == f // 64))
    for lev in range(6):
        n = 1 << lev
        m = (p // (2 * n) == f // (2 * n)) & (f // n % 2 == 1) & (p // n % 2 == 0)
        at = CCOLS["level"][0] + 128 * lev
        b[:, at:at + 128] = m
    return a, b


def parameters(z):
    out = np.zeros((128, NPAR), np.float32)

    def put(name, v, rows=slice(0, 128)):
        at, n = PCOLS[name]
        out[rows, at:at + n] = v

    def cols(v):
        v = np.asarray(v).reshape(-1, 128)
        return v.T

    def taps(v):
        return np.concatenate([cols(v[0, i]) for i in range(v.shape[1])], axis=1)

    for name, src in (("ffn1_pre", "ffn1_pre_g"), ("ffn1_post", "ffn1_post_g"), ("mix_pre", "mix_pre_g"),
                      ("gate_b", "gate_b"), ("conv_b", "ssd_conv_b"), ("norm_g", "ssd_norm_g"),
                      ("subln", "da_subln_g"), ("mix_post", "mix_post_g"), ("ffn2_pre", "ffn2_pre_g"),
                      ("ffn2_post", "ffn2_post_g"), ("norm1", "norm1_g_2"), ("gnorm", "gdn_norm_g_2"),
                      ("bgb", "branch_gate_b_2"), ("norm2", "norm2_g_2"), ("fconv_b", "ffn_conv_b_2"),
                      ("final", "final_g_2")):
        put(name, cols(z[src]))
    put("conv_w", taps(z["ssd_conv_w"]))
    put("gconv_w", taps(z["gdn_conv_w_2"]))
    put("fconv_w", taps(z["ffn_conv_w_2"]))
    put("dt_bias", z["ssd_dt_bias"].reshape(32, 1), slice(0, 32))
    put("a_log", z["ssd_A_log"].reshape(32, 1), slice(0, 32))
    put("D", z["ssd_D"].reshape(1, 32))
    put("lam", np.concatenate([z[n].reshape(1, 64) for n in
                               ("da_lambda_q1", "da_lambda_k1", "da_lambda_q2", "da_lambda_k2")], axis=1))
    for r in (0, 96):
        put("g_bias", z["gdn_dt_bias_2"].reshape(8, 1), slice(r, r + 8))
        put("g_alog", z["gdn_a_log_2"].reshape(8, 1), slice(r, r + 8))
    put("ikg", np.concatenate([z["idx_k_norm_g_2"].reshape(64, 1)] * 2))
    return out


def layout(z):
    a = {"xT": np.ascontiguousarray(z["x"][0].T), "params": parameters(z)}
    a["consts1"], a["consts2"] = constants()
    w = z["w_in"][0]
    gap = np.zeros((1024, 96), np.float32)
    a["win"] = blocks(np.concatenate([w[:, 0:5120], w[:, 5152:], w[:, 5120:5152], gap], axis=1))
    a["w1g"], a["w1u"], a["w1d"] = (blocks(z[n][0]) for n in ("ffn1_w_gate", "ffn1_w_up", "ffn1_w_down"))
    a["w2g"], a["w2u"], a["w2d"] = (blocks(z[n][0]) for n in ("ffn2_w_gate", "ffn2_w_up", "ffn2_w_down"))
    a["wssd"] = np.ascontiguousarray(
        z["ssd_w_branch"][0].reshape(4, 4, 128, 4, 2, 128).transpose(0, 3, 2, 4, 1, 5).reshape(4, 4, 128, 1024))
    a["wda"], a["wout"] = blocks(z["da_w_branch"][0]), blocks(z["w_out"][0])
    w = z["w_in_2"][0]
    at = [0, 3072, 4096, 4104, 4112, 5136, 5392, 5648, 6160, 6224, 6232, 7256, 8280]
    qkv, zz, ga, gb, dq, dk, dv, iq, ik, iw, gta, gtb = (w[:, i:j] for i, j in zip(at[:-1], at[1:]))
    n24 = gap[:, 0:24]
    a["win2"] = blocks(np.concatenate([qkv, zz, ga, n24, gb, n24, iw, n24, ga, n24, dq, dk, dv, iq, ik, ik, gta, gtb], axis=1))
    a["wout2"], a["w3"], a["w3d"] = (blocks(z[n][0]) for n in ("w_out_2", "ffn_w_up_2", "ffn_w_down_2"))
    return a


def kernel(**inputs):
    import concourse.bacc as bacc
    from concourse.bass_utils import run_bass_kernel_spmd

    z = {k: np.asarray(v) for k, v in inputs.items()}
    nc = bacc.Bacc("TRN2", target_bir_lowering=False, num_devices=1)
    arrays = layout(z)
    d = {k: nc.dram_tensor("in_" + k, v.shape, F, kind="ExternalInput").ap() for k, v in arrays.items()}
    out = nc.dram_tensor("outT", (1024, 512), F, kind="ExternalOutput").ap()
    build(nc, d, out)
    r = run_bass_kernel_spmd(nc, [{"in_" + k: v for k, v in arrays.items()}], core_ids=[0])
    return np.ascontiguousarray(r.results[0]["outT"].T)[None]
```

```python
from contextlib import ExitStack

import numpy as np

import concourse.bass as bass
from concourse import mybir

F = mybir.dt.float32
R = mybir.dt.float32r
ALU = mybir.AluOpType
ACT = mybir.ActivationFunctionType
AX = mybir.AxisListType

L = 512
T4 = 4
KB = 8
FB = 22
NRAW = 3
RATES = (0.648, 0.518, 0.736, 0.478, 0.505)
NZ = 2
STEP = 2
NW = (16, 4, 2, 2, 1)
ORDER1 = "t g0 g1 z0 r8 g2 b0 z1 r8 g3 b1 z2 r8 a0 a1 b2 z3 r8 a2 a3 c4 b3 c5 c6 c7 E"
ORDER2 = "n p0 x z0 h0 p1 z1 h1 p2 z2 h2 p3 z3 h3 k d0 d1"
LATE = (1, 0, 0, 0)
LAG1 = ((1, 2), 1)
LAG2 = ((1, 2), 1)
TABLES = (((ACT.Ln, ACT.Exp), "natural_log_exp_and_others"), ((ACT.Silu, ACT.Tanh), "silu_and_others"),
          ((ACT.Sigmoid,), "sigmoid_and_others"))
NB1, NB2 = 24, 24
NHL = 3
EPS = 1e-6
WAIT = "wait"
NEGBIG = -1.0e30
LAM_INIT = 0.2

PCOLS = {}


def _layout():
    at = 0
    for name, n in (
        ("ffn1_pre", 8), ("ffn1_post", 8), ("mix_pre", 8), ("gate_b", 16), ("conv_w", 96), ("conv_b", 24),
        ("norm_g", 16), ("subln", 1), ("mix_post", 8), ("ffn2_pre", 8), ("ffn2_post", 8),
        ("dt_bias", 1), ("a_log", 1), ("Dc", 16), ("lam", 256),
        ("norm1", 8), ("gconv_w", 96), ("g_bias", 1), ("g_alog", 1), ("gnorm", 1), ("ikg", 1), ("bgb", 16),
        ("norm2", 8), ("fconv_w", 132), ("fconv_b", 44), ("final", 8),
    ):
        PCOLS[name] = (at, n)
        at += n
    return at


NPAR = _layout()
CCOLS = {"ident": (0, 128), "ssdmask": (128, 128), "dist": (256, 512), "reset128": (768, 512),
         "neg": (128, 128), "bdincl": (256, 128), "level": (384, 768), "reset64": (1152, 512)}
NCA, NCB = 1280, 1664


class Tok:
    __slots__ = ("eng", "used", "val")

    def __init__(self, eng):
        self.eng, self.used, self.val = eng, False, 0


class Call:
    __slots__ = ("fn", "a", "k", "inc")

    def __init__(self, fn, a, k):
        self.fn, self.a, self.k, self.inc = fn, a, k, None

    def then_inc(self, sem, n):
        self.inc = (sem, n)
        return self

    def issue(self):
        ins = self.fn(*self.a, **self.k)
        if self.inc is not None:
            ins.then_inc(*self.inc)
        return ins


class Ops:

    def __init__(self, eng):
        self.eng = eng

    def dma_start(self, *a, **k):
        return Call(self.eng.dma_start, a, k)

    def matmul(self, *a, **k):
        return Call(self.eng.matmul, a, k)

    def transpose(self, *a, **k):
        return Call(self.eng.transpose, a, k)

    def activation(self, *a, **k):
        return Call(self.eng.activation, a, k)

    def copy(self, *a, **k):
        return Call(self.eng.copy, a, k)

    def mul(self, *a, **k):
        return Call(self.eng.mul, a, k)

    def memset(self, *a, **k):
        return Call(self.eng.memset, a, k)

    def tensor_copy(self, *a, **k):
        return Call(self.eng.tensor_copy, a, k)

    def tensor_tensor(self, *a, **k):
        return Call(self.eng.tensor_tensor, a, k)

    def tensor_scalar(self, *a, **k):
        return Call(self.eng.tensor_scalar, a, k)

    def scalar_tensor_tensor(self, *a, **k):
        return Call(self.eng.scalar_tensor_tensor, a, k)

    def tensor_tensor_scan(self, *a, **k):
        return Call(self.eng.tensor_tensor_scan, a, k)

    def reciprocal(self, *a, **k):
        return Call(self.eng.reciprocal, a, k)

    def reduce_max(self, *a, **k):
        return Call(self.eng.reduce_max, a, k)

    def reduce_sum(self, *a, **k):
        return Call(self.eng.reduce_sum, a, k)

    def max(self, *a, **k):
        return Call(self.eng.max, a, k)

    def match_replace(self, *a, **k):
        return Call(self.eng.match_replace, a, k)

class Queue:

    def __init__(self, name, eng):
        self.name, self.e, self.ops = name, Ops(eng), []

    def __call__(self, fn, *deps):
        t = Tok(self)
        self.ops.append([fn(self.e), deps, t])
        return t

    def later(self):
        t = Tok(self)
        op = [None, (), t]
        self.ops.append(op)
        return op


def flat(deps, out):
    for d in deps:
        if d is None:
            continue
        if isinstance(d, list) or (isinstance(d, tuple) and not (len(d) == 2 and isinstance(d[1], int))):
            flat(d, out)
        else:
            out.append(d)
    return out


class Pages:

    def __init__(self, bufs, name):
        self.free = [(b, []) for b in bufs]
        self.name = name
        self.low = len(bufs)

    def take(self):
        if not self.free:
            raise RuntimeError("out of " + self.name)
        b, w = self.free.pop(0)
        self.low = min(self.low, len(self.free))
        return Page(b, w, self)


class Page:
    __slots__ = ("b", "w", "pool", "t", "acc")

    def __init__(self, b, w, pool):
        self.b, self.w, self.pool, self.t = b, w, pool, None

    def __getitem__(self, k):
        return self.b[k]

    def release(self, *toks):
        self.pool.free.append((self.b, list(toks)))


def build(nc, d, out):
    SP, PE, AC = Queue("sp", nc.sync), Queue("pe", nc.tensor), Queue("act", nc.scalar)
    DV, GP = Queue("dve", nc.vector), Queue("pool", nc.gpsimd)
    ctx = ExitStack()
    sems = {}

    def sem(name):
        if name not in sems:
            sems[name] = ctx.enter_context(nc.semaphore("s_" + name))
        return sems[name]

    def sb(stack, name, shape, dt=F):
        return stack.enter_context(nc.sbuf_tensor(name, shape, dt))

    par = sb(ctx, "par", [128, NPAR])
    onesc = sb(ctx, "onesc", [128, 4, 128])
    small = sb(ctx, "small", [128, 1024])
    hT = sb(ctx, "hT", [128, KB, L])
    raw = [sb(ctx, f"raw{i}", [128, KB * 128]) for i in range(NRAW)]
    hl = [sb(ctx, f"hl{i}", [128, 2, KB * 128], R) for i in range(NHL)]
    uR = sb(ctx, "uR", [128, 2, KB, L], R)
    NA = 11
    fA = sb(ctx, "fA", [128, NA, L])
    banks = [ctx.enter_context(nc.psum_tensor(f"bank{i}", [128, L], F)) for i in range(8)]
    MB = Pages([b for b in banks[:3]], "main banks")
    SB = Pages([b for b in banks[3:]], "side banks")
    fp = Pages([fA[:, i, :] for i in range(NA)], "fA")

    def pc(name, j=0, n=1, rows=slice(0, 128)):
        a = PCOLS[name][0] + j
        return par[rows, a:a + n]

    def cc(name, rows=slice(0, 128)):
        a, n = CCOLS[name]
        return con[rows, a:a + n]

    small_at = [0]

    def sm(n):
        a = small_at[0]
        small_at[0] += n
        assert small_at[0] <= 1024, "small"
        return small[:, a:a + n]

    SP(lambda e: e.dma_start(par[:, :], d["params"]).then_inc(sem("p"), 16))
    for k in range(KB):
        AC(lambda e, k=k: e.dma_start(hT[:, k, :], d["xT"][k * 128:(k + 1) * 128, :]).then_inc(sem(f"x{k}"), 16))
    t_par = ("p", 16)
    t_h = [(f"x{k}", 16) for k in range(KB)]
    t_ones = [GP(lambda e, i=i, v=v: e.memset(onesc[:, i, :], v))
              for i, v in enumerate((1.0 / 1024, 1.0 / 512, 1.0 / 128, 1.0))]
    O1024, O512, O128, O1 = range(4)

    stream = {"n": 0, "late": {}, "done": {}, "split": {}}

    def reserve(j):
        a, v = AC.later(), DV.later()
        stream["late"][j] = (a, v)

    for j in range(NHL - 1):
        reserve(j)

    def panel(src, width):
        j = stream["n"]
        stream["n"] += 1
        a, v = stream["late"].pop(j)
        rs, hs = raw[j % NRAW], hl[j % NHL]
        landed = (f"raw{j % NRAW}", 16 * (j // NRAW + 1))
        SP(lambda e: e.dma_start(rs[:, 0:width], src).then_inc(sem(f"raw{j % NRAW}"), 16),
           stream["split"].get(j - NRAW))
        a[0] = AC.e.copy(hs[:, 0, 0:width], rs[:, 0:width])
        a[1] = (landed, stream["done"].get(j - NHL))
        v[0] = DV.e.tensor_tensor(hs[:, 1, 0:width], rs[:, 0:width], hs[:, 0, 0:width].bitcast(F), ALU.subtract)
        v[1] = (landed, a[2], stream["done"].get(j - NHL))
        stream["split"][j] = (v[2], a[2])
        reserve(j + NHL - 1)
        return j, hs, (a[2], v[2])

    def matpanel(bank, bw, p, kbs, kfirst, xhi, xlo, tx, first, last, off=0):
        j, hs, tw = p
        tok = None
        for q in range(kbs):
            k = kfirst + q
            w = slice((off + q) * 128, (off + q + 1) * 128)
            for i, (wi, x) in enumerate(((0, xhi), (0, xlo), (1, xhi))):
                st = first and q == 0 and i == 0
                sp_ = last and q == kbs - 1 and i == 2
                tok = PE(lambda e, wi=wi, w=w, x=x(k), st=st, sp_=sp_:
                         e.matmul(bank[:, :], hs[:, wi, w], x, start=st, stop=sp_),
                         tw, tx(k), bw if st else None)
        stream["done"][j] = tok
        return tok

    t_u = [None] * KB
    t_hr = [None] * KB
    late_r = {}
    t_ulast = []

    def uhi(k):
        return uR[:, 0, k, :]

    def ulo(k):
        return uR[:, 1, k, :]

    def tu(k):
        return t_u[k]

    def ugemm(src):
        b = MB.take()
        p = panel(src, KB * 128)
        for q in range(0, KB, STEP):
            t = matpanel(b, b.w, p, STEP, q, uhi, ulo, tu, q == 0, q + STEP == KB, off=q)
            if q + STEP < KB:
                yield
        t_ulast[:] = [t]
        if late_r:
            if late_r["r"] is None:
                c = late_r["acc"]
                b2 = SB.take()
                t2 = PE(lambda e: e.matmul(b2[:, :], onesc[:, O1024, :], c[:, :], start=True, stop=True), c.t, t_ones[O1024], b2.w)
                c.release(t2)
                late_r["r"] = rstd_of(b2, t2)
            r = late_r["r"]
            x = fp.take()
            v = DV(lambda e: e.tensor_tensor(x[:, :], b[:, :], r[:, :], ALU.mult), t, r.t, x.w)
            b.release(v)
            late_r["t"] = v
            return x, v
        return b, t

    def rstd_of(bank, tok):
        r = fp.take()
        s = AC(lambda e: e.activation(r[:, :], bank[:, :], ACT.Ln, bias=epsc), tok, r.w, t_eps)
        r.t = AC(lambda e: e.activation(r[:, :], r[:, :], ACT.Exp, scale=-0.5), s)
        bank.release(s)
        return r

    def sumsq(bank, wait, sources, which):
        n = len(sources)
        for i in range(0, n, 2):
            p, q = fp.take(), fp.take()
            a = AC(lambda e: e.activation(p[:, :], sources[i][0], ACT.Square), sources[i][1], p.w)
            a2 = AC(lambda e: e.activation(q[:, :], sources[i + 1][0], ACT.Square), sources[i + 1][1], q.w)
            s = (DV if i == n - 2 else GP)(lambda e: e.tensor_tensor(p[:, :], p[:, :], q[:, :], ALU.add), a, a2)
            q.release(s)
            t = PE(lambda e: e.matmul(bank[:, :], onesc[:, which, :], p[:, :], start=i == 0, stop=i == n - 2),
                   s, t_ones[which], wait if i == 0 else None)
            p.release(t)
        return t

    def split(hi, lo, x, tx, whi, eng=None):
        a = AC(lambda e: e.copy(hi, x), tx, whi)
        v = (eng or DV)(lambda e: e.tensor_tensor(lo, x, hi.bitcast(F), ALU.subtract), a, tx, whi)
        return (a, v)

    def side_rstd(sources, which):
        sq = []
        for x, tx in sources:
            q = fp.take()
            q.t = AC(lambda e: e.activation(q[:, :], x, ACT.Square), tx, q.w)
            sq.append(q)
        for _ in range(NW[2]):
            yield
        b = SB.take()
        n = len(sq)
        for i, q in enumerate(sq):
            t = PE(lambda e: e.matmul(b[:, :], onesc[:, which, :], q[:, :], start=i == 0, stop=i == n - 1),
                   q.t, t_ones[which], b.w)
            q.release(t)
        r = rstd_of(b, t)
        return r, t

    def norm_u(gname, late):
        last = list(t_ulast)
        if late:
            for k in range(KB):
                a = AC(lambda e: e.mul(uhi(k), hT[:, k, :], pc(gname, k)), t_h[k], t_par, last)
                v = DV(lambda e: e.scalar_tensor_tensor(out=ulo(k), in0=hT[:, k, :], scalar=pc(gname, k), in1=uhi(k).bitcast(F),
                                                       op0=ALU.mult, op1=ALU.subtract), a, t_h[k], t_par, last)
                t_u[k] = (a, v)
            acc = fp.take()
            t = None
            for k in range(KB):
                q = fp.take() if k else acc
                a = AC(lambda e: e.activation(q[:, :], hT[:, k, :], ACT.Square), t_h[k], q.w)
                t_hr[k] = (t_u[k], a)
                if k:
                    t = DV(lambda e: e.tensor_tensor(acc[:, :], acc[:, :], q[:, :], ALU.add), a, t)
                    q.release(t)
                else:
                    t = a
            acc.t = t
            late_r.update(acc=acc, r=None)
            return
        b = SB.take()
        t = sumsq(b, b.w, [(hT[:, k, :], t_h[k]) for k in range(KB)], O1024)
        r = rstd_of(b, t)
        ahead = []
        for k in range(KB + 1):
            if k < KB:
                x = fp.take()
                x.t = v = DV(lambda e: e.scalar_tensor_tensor(out=x[:, :], in0=hT[:, k, :], scalar=pc(gname, k), in1=r[:, :],
                                                            op0=ALU.mult, op1=ALU.mult), t_h[k], r.t, x.w, t_par)
                ahead.append(x)
            if k:
                x, i = ahead.pop(0), k - 1
                t_u[i] = split(uhi(i), ulo(i), x[:, :], x.t, last, GP if i % 2 else DV)
                t_hr[i] = t_u[i]
                x.release(t_u[i])
        r.release(v)

    def end_u():
        if late_r:
            late_r["r"].release(late_r["t"])
            late_r.clear()

    def collect(ys, b, t, gn):
        m = len(ys)
        q = fp.take()
        a = AC(lambda e: e.activation(q[:, :], b[:, :], ACT.Square), t, q.w)
        y = fp.take()
        y.t = AC(lambda e: e.mul(y[:, :], b[:, :], pc(gn, m)), t, y.w, t_par)
        b.release(y.t)
        if m == 0:
            q.t = a
            y.acc = q
        else:
            c = ys[0].acc
            eng = DV if m == KB - 1 else GP
            c.t = eng(lambda e: e.tensor_tensor(c[:, :], c[:, :], q[:, :], ALU.add), a, c.t)
            q.release(c.t)
        ys.append(y)

    def post_norm(y, half):
        c = y[0].acc
        b = SB.take()
        t = PE(lambda e: e.matmul(b[:, :], onesc[:, O1024, :], c[:, :], start=True, stop=True), c.t, b.w)
        c.release(t)
        r = rstd_of(b, t)
        def scale(k):
            y[k].t = (GP if k % 2 else DV)(lambda e: e.tensor_tensor(y[k][:, :], y[k][:, :], r[:, :], ALU.mult), y[k].t, r.t)

        def add(k):
            t_h[k] = DV(lambda e: e.scalar_tensor_tensor(out=hT[:, k, :], in0=y[k][:, :], scalar=0.5 if half else 1.0,
                                                       in1=hT[:, k, :], op0=ALU.mult, op1=ALU.add), y[k].t, t_h[k], t_hr[k])
            y[k].release(t_h[k])

        for k in (1, 3, 5, 7, 0):
            scale(k)
        add(0)
        for k in (2, 4, 6):
            scale(k)
            add(k)
            add(k - 1)
        add(7)
        r.release(t_h[KB - 1])

    def down(src, act, tact):
        for m in range(KB):
            b = MB.take()
            at = 0
            for n in (8, 8, 6):
                t = matpanel(b, b.w, panel(src[m, :, at * 128:(at + n) * 128], n * 128), n, at,
                             lambda k: act[:, 0, k, :], lambda k: act[:, 1, k, :], lambda k: tact[k],
                             at == 0, at + n == FB)
                at += n
            yield m, b, t

    def ffn(wg, wu, wd, gpre, gpost, act, wait):
        norm_u(gpre, LATE[0])
        tact = []
        for j in range(FB):
            bg, tg = yield from ugemm(wg[j])
            s = fp.take()
            a = AC(lambda e, s=s, bg=bg: e.activation(s[:, :], bg[:, :], ACT.Silu), tg, s.w)
            bg.release(a)
            bu, tu_ = yield from ugemm(wu[j])
            v = DV(lambda e, s=s, bu=bu: e.tensor_tensor(s[:, :], s[:, :], bu[:, :], ALU.mult), a, tu_)
            bu.release(v)
            tk = split(act[:, 0, j, :], act[:, 1, j, :], s[:, :], v, wait)
            s.release(tk)
            tact.append(tk)
        end_u()
        y = []
        for m, b, t in down(wd, act, tact):
            collect(y, b, t, gpost)
        post_norm(y, True)
        return t

    def conv(b, tb, wname, taps, col, ncol, bias, page):
        def w(i):
            return pc(wname, i * ncol + col)
        if bias is None:
            t = AC(lambda e: e.activation(page[:, :], b[:, :], ACT.Identity, scale=w(taps - 1)), tb, page.w, t_par)
        else:
            t = AC(lambda e: e.activation(page[:, :], b[:, :], ACT.Identity, scale=w(taps - 1), bias=pc(bias, col)),
                   tb, page.w, t_par)
        for s in range(1, taps):
            t = DV(lambda e, s=s: e.scalar_tensor_tensor(out=page[:, s:L], in0=b[:, 0:L - s], scalar=w(taps - 1 - s),
                                                       in1=page[:, s:L], op0=ALU.mult, op1=ALU.add), t)
        b.release(t)
        page.t = t
        return t

    def convsilu(b, tb, wname, col, bias):
        p = fp.take()
        t = conv(b, tb, wname, 4, col, 24, bias, p)
        p.t = AC(lambda e: e.activation(p[:, :], p[:, :], ACT.Silu), t)
        return p

    def turn(dst_bank, wait, src, tsrc, n=T4, cols=128):
        for t in range(n):
            tok = PE(lambda e, t=t: e.transpose(dst_bank[:, t * 128:(t + 1) * 128], src[:, t * 128:(t + 1) * 128], ident),
                     tsrc, wait, t_con)
        return tok

    def softplus(x, tx, rows):
        e1, w = fp.take(), fp.take()
        c = (rows, slice(0, L))
        t = DV(lambda e: e.scalar_tensor_tensor(out=e1[c], in0=x[c], scalar=-1.0, in1=x[c], op0=ALU.mult, op1=ALU.max), tx, e1.w)
        t = AC(lambda e: e.activation(e1[c], e1[c], ACT.Exp, scale=-1.0), t)
        ln = fp.take()
        tw = DV(lambda e: e.tensor_scalar(w[c], e1[c], 1.0, None, ALU.add), t, w.w)
        tl = AC(lambda e: e.activation(ln[c], w[c], ACT.Ln), tw, ln.w)
        t2 = DV(lambda e: e.scalar_tensor_tensor(out=e1[c], in0=w[c], scalar=-1.0, in1=e1[c], op0=ALU.add, op1=ALU.subtract), tw, t)
        t3 = AC(lambda e: e.activation(w[c], ln[c], ACT.Exp, scale=-1.0), t2, tl)
        t4 = DV(lambda e: e.tensor_tensor(e1[c], e1[c], w[c], ALU.mult), t3, t2)
        t5 = DV(lambda e: e.tensor_tensor(ln[c], ln[c], e1[c], ALU.subtract), t4, tl)
        t6 = DV(lambda e: e.scalar_tensor_tensor(out=x[c], in0=x[c], scalar=0.0, in1=ln[c], op0=ALU.max, op1=ALU.add), t5)
        e1.release(t5)
        w.release(t4)
        ln.release(t6)
        return t6

    def finish(gen):
        for _ in gen:
            pass

    def value(gen):
        while True:
            try:
                next(gen)
            except StopIteration as e:
                return e.value

    def until(cond):
        while not cond():
            yield WAIT

    def room(n):
        yield from until(lambda: len(fp.free) >= n)

    def chain(*gens):
        for x in gens:
            yield from x

    def both(*gens):
        live = list(gens)
        while live:
            n = WAIT
            for x in list(live):
                try:
                    if next(x) is not WAIT:
                        n = None
                except StopIteration:
                    live.remove(x)
                    n = None
            if live:
                yield n

    def schedule(main, sides):
        END = object()
        sides = [[x, rate, 0.0] for x, rate in sides]
        going = True
        while going or sides:
            moved = False
            if going:
                r = next(main, END)
                going = r is not END
                moved = r is not WAIT and going
            for side in list(sides):
                side[2] += side[1]
                while side[2] >= 1:
                    side[2] -= 1
                    r = next(side[0], END)
                    if r is END:
                        sides.remove(side)
                        moved = True
                        break
                    if r is WAIT:
                        side[2] = 0.0
                        break
                    moved = True
                else:
                    moved = moved or not going
            assert moved or not (going or sides) or any(x[2] > 0 for x in sides), "streams wait for each other"

    def drop_pages():
        assert len(fp.free) == NA + NB_ and len(rp.free) == 16, (len(fp.free), len(rp.free))
        toks = [w for _, w in fp.free] + [w for _, w in rp.free] + [t_h[KB - 1]]
        fp.free = [(fA[:, i, :], toks) for i in range(NA)]
        return toks

    def pv_turn(P, W, i):
        b = SB.take()
        for k in range(i + 1):
            tp = PE(lambda e, k=k: e.transpose(b[:, k * 128:(k + 1) * 128], P[:, k * 128:(k + 1) * 128], ident), P.t, b.w)
        P.release(tp)
        A = fp.take()
        A.t = AC(lambda e: e.copy(A[:, 0:W], b[:, 0:W]), tp, A.w)
        b.release(A.t)
        return A

    def pv_mul(A, i, V, o):
        b = SB.take()
        for k in range(i + 1):
            t = PE(lambda e, k=k: e.matmul(b[:, 0:128], V[:, k * 128:(k + 1) * 128], A[:, k * 128:(k + 1) * 128],
                                         start=k == 0, stop=k == i), A.t, V.t, b.w)
        A.release(t)
        o.t = AC(lambda e: e.copy(o[:, i * 128:(i + 1) * 128], b[:, 0:128]), t, o.w)
        b.release(o.t)
        return t

    def softmax_tiles(front, V, o, lag, split_front):
        P, A = {}, {}
        la, lb = lag
        for n in range(T4 + lb):
            if n < T4:
                P[n] = front(n)
            if not split_front:
                if 0 <= n - la < T4:
                    A[n - la] = pv_turn(P[n - la][0], P[n - la][1], n - la)
                yield
            else:
                yield
                if 0 <= n - la < T4:
                    A[n - la] = pv_turn(P[n - la][0], P[n - la][1], n - la)
                yield
            if 0 <= n - lb < T4:
                tpv = pv_mul(A[n - lb], n - lb, V, o)
            yield
        return P[T4 - 1][2], tpv

    epsc = sm(1)
    t_eps = DV(lambda e: e.memset(epsc, EPS))
    hb1, hb2 = sm(16), sm(16)
    t_hb = [DV(lambda e: e.tensor_scalar(hb1, pc("gate_b", 0, 16), 0.5, None, ALU.mult), t_par),
            DV(lambda e: e.tensor_scalar(hb2, pc("bgb", 0, 16), 0.5, None, ALU.mult), t_par)]

    with ExitStack() as ph:
        act = sb(ph, "act1", [128, 2, FB, L], R)
        t_phase = value(ffn(d["w1g"], d["w1u"], d["w1d"], "ffn1_pre", "ffn1_post", act, None))

    with ExitStack() as ph:
        con = sb(ph, "con1", [128, NCA])
        t_con = ("c1", 16)
        AC(lambda e: e.dma_start(con[:, :], d["consts1"]).then_inc(sem("c1"), 16), t_phase)
        ident = con[:, 0:128]
        SSDMASK = cc("ssdmask")
        mR = sb(ph, "mR1", [128, 18, L], R)
        idR = sb(ph, "idR", [128, 32], R)
        selR = sb(ph, "selR", [32, 4, 128], R)
        sel_free = [t_phase]
        t_idR = DV(lambda e: e.tensor_copy(idR[:, :], ident[:, 0:32]), t_con)
        NB_ = NB1
        fB = sb(ph, "fB1", [128, NB_, L])
        for i in range(NB_):
            fp.free.append((fB[:, i, :], [t_phase]))
        rp = Pages([mR[:, i, :] for i in range(16)], "R pages")
        for i in range(16):
            rp.free[i] = (rp.free[i][0], [t_phase])
        acN, alast, cdec, ea, ddec = sm(128), sm(128), sm(128), sm(128), sm(128)
        dtN = sm(128)

        def n3(x):
            return x.rearrange("p (t h) -> p t h", t=T4)

        norm_u("mix_pre", LATE[1])
        WIN = d["win"]
        acum = {}

        def decay_side(dt):
            t = softplus(dt, dt.t, slice(0, 32))
            aex = sm(1)
            ta = AC(lambda e: e.activation(aex[0:32, :], pc("a_log", rows=slice(0, 32)), ACT.Exp), t_par)
            a, ac = fp.take(), fp.take()
            t1 = DV(lambda e: e.tensor_scalar(a[0:32, :], dt[0:32, :], aex[0:32, :], -1.0, ALU.mult, ALU.mult), t, ta, a.w)
            t2 = DV(lambda e: e.tensor_tensor_scan(ac[0:32, :], con[0:32, CCOLS["reset128"][0]:CCOLS["reset128"][0] + L],
                                                 a[0:32, :], 0.0, ALU.mult, ALU.add), t1, ac.w, t_con)
            a.release(t2)
            ach, acl = mR[:, 16, :], mR[:, 17, :]
            t_s = split(ach[0:32, :], acl[0:32, :], ac[0:32, :], t2, t_phase)
            for _ in range(NW[1]):
                yield
            b = SB.take()
            for q in range(T4):
                PE(lambda e, q=q: e.transpose(b[:, q * 32:q * 32 + 32], ac[0:32, q * 128:(q + 1) * 128], con[0:32, 0:32]), t2, b.w)
            for q in range(T4):
                PE(lambda e, q=q: e.transpose(b[:, 128 + q * 32:160 + q * 32], dt[0:32, q * 128:(q + 1) * 128], con[0:32, 0:32]), t)
            for q in range(T4):
                lst = ac[0:32, q * 128 + 127:q * 128 + 128]
                tp = PE(lambda e, q=q, lst=lst: e.matmul(b[:, 256 + q * 32:288 + q * 32], lst.broadcast_to([32, 128]), con[0:32, 0:32],
                                              start=True, stop=True))
            t3 = DV(lambda e: e.tensor_copy(acN, b[:, 0:128]), tp)
            t4 = DV(lambda e: e.tensor_copy(dtN, b[:, 128:256]), tp)
            t5 = DV(lambda e: e.tensor_copy(alast, b[:, 256:384]), tp)
            b.release(t5)
            t6 = AC(lambda e: e.activation(cdec, alast, ACT.Exp), t5)
            t7 = AC(lambda e: e.activation(ea, acN, ACT.Exp), t3)
            t8 = DV(lambda e: e.tensor_tensor(ddec, alast, acN, ALU.subtract), t5, t3)
            t9 = AC(lambda e: e.activation(ddec, ddec, ACT.Exp), t8)
            dt.release(tp)
            ac.release(tp, t_s)
            acum.update(hi=ach, lo=acl, t=t_s, tn=(t3, t4, t5, t6, t7, t9))

        grp = [dict() for _ in range(4)]

        def project_group(g):
            G = grp[g]
            xs = []
            for i in range(4):
                b, t = yield from ugemm(WIN[16 + 4 * g + i])
                xs.append(convsilu(b, t, "conv_w", 4 * g + i, "conv_b"))
                yield
            b, t = yield from ugemm(WIN[32 + g])
            G["B"] = convsilu(b, t, "conv_w", 16 + g, "conv_b")
            yield
            b, t = yield from ugemm(WIN[36 + g])
            G["C"] = convsilu(b, t, "conv_w", 20 + g, "conv_b")
            G["xs"] = xs
            yield

        def project_dt():
            b, t = yield from ugemm(WIN[80])
            dt = fp.take()
            dt.t = DV(lambda e: e.tensor_scalar(dt[0:32, :], b[0:32, :], pc("dt_bias", rows=slice(0, 32)), None, ALU.add),
                      t, dt.w, t_par)
            b.release(dt.t)
            acum["dt"] = dt
            yield

        def ssd_core(g):
            G = grp[g]
            xs, B, C = G["xs"], G["B"], G["C"]
            Xd = []
            hs = slice(8 * g, 8 * g + 8)
            tn = acum["tn"]
            t_sel = GP(lambda e: e.tensor_copy(selR[:, :, :].rearrange("p i (a c) -> p (i a) c", a=2),
                                              con[0:32, hs][:, :, None].broadcast_to([32, 8, 64])), sel_free[0], t_con)
            for t in range(T4):
                b = SB.take()
                for i in range(4):
                    tp = PE(lambda e, i=i, t=t: e.transpose(b[:, i * 128:(i + 1) * 128], xs[i][:, t * 128:(t + 1) * 128], ident),
                            xs[i].t, b.w)
                x = fp.take()
                v1 = DV(lambda e, b=b, x=x, t=t: e.tensor_tensor(
                    x[:, :].rearrange("p (h q) -> p h q", q=64), b[:, :].rearrange("p (h q) -> p h q", q=64),
                    n3(dtN)[:, t, hs][:, :, None].broadcast_to([128, 8, 64]), ALU.mult), tp, tn, x.w)
                b.release(v1)
                x.t = v1
                Xd.append(x)
                yield
            Y = xs
            for i in range(4):
                Y[i].t = AC(lambda e: e.mul(Y[i][:, :], Y[i][:, :], pc("Dc", 4 * g + i)), Y[i].t, tp, t_par)
            b = SB.take()
            tp = turn(b, b.w, B, B.t)
            BN = fp.take()
            BN.t = AC(lambda e: e.copy(BN[:, :], b[:, :]), tp, BN.w)
            b.release(BN.t)
            b = SB.take()
            for t in range(T4):
                c = slice(t * 128, (t + 1) * 128)
                tc = PE(lambda e, c=c: e.matmul(b[:, c], B[:, c], C[:, c], start=True, stop=True), B.t, C.t, b.w)
            B.release(tc)
            CB = fp.take()
            m = SSDMASK[:, None, :].broadcast_to([128, T4, 128])
            CB.t = DV(lambda e: e.tensor_tensor(CB[:, :].rearrange("p (t l) -> p t l", t=T4),
                                              b[:, :].rearrange("p (t l) -> p t l", t=T4), m, ALU.mult), tc, CB.w)
            b.release(CB.t)
            yield
            xds, prev = [], []
            for t in range(1, T4):
                xd = fp.take()
                xd.t = DV(lambda e: e.tensor_tensor(
                    xd[:, :].rearrange("p (h q) -> p h q", q=64), Xd[t - 1][:, :].rearrange("p (h q) -> p h q", q=64),
                    n3(ddec)[:, t - 1, hs][:, :, None].broadcast_to([128, 8, 64]), ALU.mult), Xd[t - 1].t, xd.w, tn)
                xds.append(xd)
            yield
            yield
            for t in range(1, T4):
                xd = xds[t - 1]
                b = SB.take()
                ts = PE(lambda e: e.matmul(b[:, :], BN[:, (t - 1) * 128:t * 128], xd[:, :], start=True, stop=True),
                        xd.t, BN.t, b.w)
                if t == 1:
                    xd.release(ts)
                    new = fp.take()
                    new.t = AC(lambda e: e.copy(new[:, :], b[:, :]), ts, new.w)
                else:
                    new = xd
                    v = DV(lambda e: e.tensor_tensor(
                        new[:, :].rearrange("p (h q) -> p h q", q=64), prev[-1][:, :].rearrange("p (h q) -> p h q", q=64),
                        n3(cdec)[:, t - 1, hs][:, :, None].broadcast_to([128, 8, 64]), ALU.mult), prev[-1].t, ts, tn)
                    new.t = DV(lambda e: e.tensor_tensor(new[:, :], new[:, :], b[:, :], ALU.add), v, ts)
                b.release(new.t)
                prev.append(new)
            BN.release(ts)
            yield

            def front(hh):
                H = 8 * g + hh
                b = SB.take()
                sel = idR[0:32, H:H + 1].broadcast_to([32, 128])
                PE(lambda e: e.matmul(b[:, :], sel, acum["hi"][0:32, :], start=True, stop=False), acum["t"], t_idR, b.w)
                tp = PE(lambda e: e.matmul(b[:, :], sel, acum["lo"][0:32, :], start=False, stop=True))
                E = fp.take()
                v = DV(lambda e: e.tensor_tensor(
                    E[:, :].rearrange("p (t l) -> p t l", t=T4), b[:, :].rearrange("p (t l) -> p t l", t=T4),
                    n3(acN)[:, :, H][:, :, None].broadcast_to([128, T4, 128]), ALU.subtract), tp, E.w, tn)
                b.release(v)
                v = DV(lambda e: e.tensor_scalar(E[:, :], E[:, :], 0.0, None, ALU.min), v)
                a = AC(lambda e: e.activation(E[:, :], E[:, :], ACT.Exp), v)
                E.t = DV(lambda e: e.tensor_tensor(E[:, :], E[:, :], CB[:, :], ALU.mult), a, CB.t)
                return E

            Es = [front(0)]
            yield
            EAs = {}

            def from_state(i):
                b = SB.take()
                sel = selR[:, i, :]
                PE(lambda e: e.matmul(b[:, :], sel, acum["hi"][0:32, :], start=True, stop=False), acum["t"], t_sel, b.w)
                tp = PE(lambda e: e.matmul(b[:, :], sel, acum["lo"][0:32, :], start=False, stop=True))
                sel_free[0] = tp
                EA = fp.take()
                a = AC(lambda e: e.activation(EA[:, :], b[:, :], ACT.Exp), tp, EA.w)
                b.release(a)
                b = SB.take()
                for t in range(1, T4):
                    tp = PE(lambda e: e.matmul(b[:, t * 128:(t + 1) * 128], prev[t - 1][:, i * 128:(i + 1) * 128],
                                              C[:, t * 128:(t + 1) * 128], start=True, stop=True), prev[t - 1].t, C.t, b.w)
                v = DV(lambda e: e.tensor_tensor(EA[:, 128:L], EA[:, 128:L], b[:, 128:L], ALU.mult), a, tp)
                b.release(v)
                Y[i].t = DV(lambda e: e.tensor_tensor(Y[i][:, 128:L], Y[i][:, 128:L], EA[:, 128:L], ALU.add), v, Y[i].t)
                EA.release(Y[i].t)
                return tp

            for hh in range(8):
                if hh < 7:
                    Es.append(front(hh + 1))
                    yield
                e2, e1 = hh // 2, hh % 2
                if e1 == 0:
                    yb = SB.take()
                else:
                    tq = from_state(e2)
                E = Es.pop(0)
                for t in range(T4):
                    tp = PE(lambda e: e.matmul(
                        yb[64 * e1:64 * e1 + 64, t * 128:t * 128 + 128], Xd[t][:, hh * 64:hh * 64 + 64],
                        E[:, t * 128:(t + 1) * 128], start=True, stop=True), E.t, yb.w, Xd[t].t)
                E.release(tp)
                if e1 == 1:
                    v = DV(lambda e: e.tensor_tensor(Y[e2][:, :], Y[e2][:, :], yb[:, :], ALU.add), tp, Y[e2].t)
                    Y[e2].t = v
                    yb.release(v)
                yield
            for p in prev:
                p.release(tq)
            C.release(tq)
            CB.release(v)
            for p in Xd:
                p.release(tp)
            G["Y"] = Y
            yield

        def project_z(g):
            G = grp[g]
            G["z"] = []
            for i in range(4):
                b, t = yield from ugemm(WIN[4 * g + i])
                s = fp.take()
                s.t = AC(lambda e, s=s, b=b: e.activation(s[:, :], b[:, :], ACT.Silu), t, s.w)
                b.release(s.t)
                G["z"].append(s)
                yield

        def gate_group(g):
            G = grp[g]
            Y, z = G["Y"], G["z"]
            for i in range(4):
                z[i].t = DV(lambda e: e.tensor_tensor(z[i][:, :], z[i][:, :], Y[i][:, :], ALU.mult), z[i].t, Y[i].t)
                Y[i].release(z[i].t)
            r, t = yield from side_rstd([(z[i][:, :], z[i].t) for i in range(4)], O512)
            yield
            G["p"] = []
            for i in range(4):
                v = DV(lambda e, i=i: e.scalar_tensor_tensor(out=z[i][:, :], in0=z[i][:, :], scalar=pc("norm_g", 4 * g + i),
                                                           in1=r[:, :], op0=ALU.mult, op1=ALU.mult), r.t, z[i].t, t)
                hi, lo = rp.take(), rp.take()
                tk = split(hi[:, :], lo[:, :], z[i][:, :], v, [hi.w, lo.w])
                z[i].release(tk)
                G["p"].append((hi, lo, tk))
            r.release(v)
            G["ready"] = True
            yield

        yssd = []

        def branch_group(g):
            G = grp[g]
            P = G["p"]
            for m2 in range(4):
                p = panel(d["wssd"][g, m2], KB * 128)
                for mi in range(2):
                    m = 2 * m2 + mi
                    b = MB.take()
                    t = matpanel(b, b.w, p, 4, 0, lambda k: P[k][0][:, :], lambda k: P[k][1][:, :], lambda k: P[k][2],
                                 True, True, off=4 * mi)
                    if g == 0:
                        y = fp.take()
                        y.t = AC(lambda e, y=y, b=b: e.mul(y[:, :], b[:, :], 0.5), t, y.w)
                        yssd.append(y)
                    else:
                        y = yssd[m]
                        y.t = DV(lambda e, y=y, b=b: e.scalar_tensor_tensor(out=y[:, :], in0=b[:, :], scalar=0.5, in1=y[:, :],
                                                                        op0=ALU.mult, op1=ALU.add), t, y.t)
                    b.release(y.t)
                if m2 == 3:
                    for hi, lo, tk in P:
                        hi.release(t)
                        lo.release(t)
                    G["branched"] = True
                yield

        def ssd_side():
            yield from until(lambda: "dt" in acum)
            yield from decay_side(acum["dt"])
            for g in range(4):
                yield from until(lambda: "xs" in grp[g])
                yield from ssd_core(g)
                yield from until(lambda: len(grp[g].get("z", ())) == 4)
                yield from gate_group(g)

        def branch(g):
            yield from until(lambda: grp[g].get("ready"))
            yield from branch_group(g)

        lam = sm(8)
        lt = fp.take()
        t1 = DV(lambda e: e.tensor_tensor(lt[:, 0:128].rearrange("p (a b) -> p a b", a=2),
                                        pc("lam", 0, 256).rearrange("p (a c b) -> p a c b", a=2, c=2)[:, :, 0, :],
                                        pc("lam", 0, 256).rearrange("p (a c b) -> p a c b", a=2, c=2)[:, :, 1, :], ALU.mult),
                lt.w, t_par)
        t2 = DV(lambda e: e.reduce_sum(lam[:, 0:2], lt[:, 0:128].rearrange("p (a b) -> p a b", a=2), AX.X), t1)
        lt.release(t2)
        t3 = AC(lambda e: e.activation(lam[:, 2:4], lam[:, 0:2], ACT.Exp), t2)
        t4 = DV(lambda e: e.tensor_tensor(lam[:, 4:5], lam[:, 3:4], lam[:, 2:3], ALU.subtract), t3)
        t_lam = DV(lambda e: e.tensor_scalar(lam[:, 5:6], lam[:, 4:5], -LAM_INIT, None, ALU.add), t4)
        nlam = lam[:, 5:6]
        t_sg = DV(lambda e: e.tensor_scalar(lam[:, 6:7], pc("subln"), 1.0 - LAM_INIT, None, ALU.mult), t_par)
        sg = lam[:, 6:7]
        st = sm(64)
        heads = [dict() for _ in range(8)]
        stat = {"k": 0}

        def project_head(h):
            Hd = heads[h]
            for name, j in (("q", 40 + h), ("k", 48 + h), ("v", 56 + h)):
                b, t = yield from ugemm(WIN[j])
                s = fp.take()
                s.t = AC(lambda e, s=s, b=b, name=name: e.mul(s[:, :], b[:, :], 0.125) if name == "q" else e.copy(s[:, :], b[:, :]),
                         t, s.w)
                b.release(s.t)
                Hd[name] = s
                yield

        st_free = [None] * 4

        def att_head(h):
            Hd = heads[h]
            q, k, vT = Hd["q"], Hd["k"], Hd["v"]
            b = SB.take()
            tp = turn(b, b.w, vT, vT.t)
            vT.release(tp)
            V = fp.take()
            V.t = AC(lambda e: e.copy(V[:, :], b[:, :]), tp, V.w)
            b.release(V.t)
            yield
            o = fp.take()
            slope = float(2.0 ** (-8.0 * (h + 1) / 8))
            o.t = o.w

            def front(i):
                W = 128 * (i + 1)
                s_i = stat["k"] % 4
                stat["k"] += 1
                s0 = st[:, 16 * s_i:16 * s_i + 16]
                wst = st_free[s_i]
                Ps = []
                tm = []
                for m in range(2):
                    b = SB.take()
                    r = slice(64 * m, 64 * m + 64)
                    tp = PE(lambda e, r=r, b=b, i=i, W=W: e.matmul(b[:, 0:W], q[r, i * 128:(i + 1) * 128], k[r, 0:W],
                                                                 start=True, stop=True), q.t, k.t, b.w)
                    P = fp.take()
                    a0 = CCOLS["dist"][0]
                    v = DV(lambda e, b=b, P=P, i=i, W=W: e.scalar_tensor_tensor(
                        out=P[:, 0:W], in0=con[:, a0 + 384 - 128 * i:a0 + 512], scalar=slope, in1=b[:, 0:W],
                        op0=ALU.mult, op1=ALU.add), tp, P.w)
                    b.release(v)
                    P.t = v
                    tm.append(DV(lambda e, P=P, m=m, W=W, s0=s0: e.reduce_max(s0[:, m:m + 1], P[:, 0:W], AX.X), v, wst))
                    Ps.append(P)
                tm = DV(lambda e, s0=s0: e.tensor_scalar(s0[:, 2:4], s0[:, 0:2], -1.0, None, ALU.mult), tm)
                te = []
                for m in range(2):
                    te.append(AC(lambda e, P=Ps[m], m=m, W=W, s0=s0: e.activation(
                        P[:, 0:W], P[:, 0:W], ACT.Exp, bias=s0[:, 2 + m:3 + m], accum_out=s0[:, 4 + m:5 + m]), tm))
                v = DV(lambda e, s0=s0: e.reciprocal(s0[:, 6:8], s0[:, 4:6]), te)
                v2 = DV(lambda e, s0=s0: e.tensor_tensor(s0[:, 8:9], s0[:, 7:8], nlam, ALU.mult), v, t_lam)
                v3 = DV(lambda e, P=Ps[1], W=W, s0=s0: e.tensor_scalar(P[:, 0:W], P[:, 0:W], s0[:, 8:9], None, ALU.mult), v2, te)
                v4 = DV(lambda e, P=Ps[0], Q=Ps[1], W=W, s0=s0: e.scalar_tensor_tensor(
                    out=P[:, 0:W], in0=P[:, 0:W], scalar=s0[:, 6:7], in1=Q[:, 0:W], op0=ALU.mult, op1=ALU.add), v3, te)
                st_free[s_i] = v4
                Ps[1].release(v4)
                Ps[0].t = v4
                return Ps[0], W, tp

            tp, tpv = yield from softmax_tiles(front, V, o, *LAG1)
            q.release(tp)
            k.release(tp)
            V.release(tpv)
            r, t = yield from side_rstd([(o[:, :], o.t)], O128)
            v = DV(lambda e: e.scalar_tensor_tensor(out=o[:, :], in0=o[:, :], scalar=sg, in1=r[:, :], op0=ALU.mult, op1=ALU.mult),
                   r.t, o.t, t, t_sg)
            r.release(v)
            hi, lo = rp.take(), rp.take()
            tk = split(hi[:, :], lo[:, :], o[:, :], v, [hi.w, lo.w])
            o.release(tk)
            Hd["o"] = (hi, lo, tk)
            yield

        def gates(names_m):
            for m in names_m:
                b, t = yield from ugemm(WIN[64 + m])
                s = fp.take()
                a = AC(lambda e, s=s, b=b, m=m: e.activation(s[:, :], b[:, :], ACT.Tanh, scale=0.5, bias=hb1[:, m:m + 1]), t, s.w, t_hb)
                b.release(a)
                y = yssd[m]
                y.t = DV(lambda e, s=s, y=y: e.scalar_tensor_tensor(out=y[:, :], in0=s[:, :], scalar=1.0, in1=y[:, :],
                                                                op0=ALU.add, op1=ALU.mult), a, y.t)
                s.release(y.t)
                yield

        def att_side():
            for h in range(0, 8, 2):
                yield from until(lambda: "v" in heads[h + 1] and "Y" in grp[3])
                yield from both(att_head(h), att_head(h + 1))

        def chained(h):
            yield from until(lambda: h < 4 or "o" in heads[h - 4])
            yield from project_head(h)

        steps = {"t": lambda i: project_dt(), "g": project_group, "z": project_z, "r": room, "b": branch, "a": project_head,
                 "c": chained, "E": lambda i: gates(range(8))}
        main = chain(*[steps[w[0]](int(w[1:] or 0)) for w in ORDER1.split()])
        schedule(main, [(ssd_side(), RATES[0]), (att_side(), RATES[1])])
        yatt = []
        for m in range(KB):
            b = MB.take()
            t = matpanel(b, b.w, panel(d["wda"][m], KB * 128), KB, 0, lambda k: heads[k]["o"][0][:, :],
                         lambda k: heads[k]["o"][1][:, :], lambda k: heads[k]["o"][2], True, True)
            y = fp.take()
            y.t = AC(lambda e, y=y, b=b: e.mul(y[:, :], b[:, :], 0.5), t, y.w)
            b.release(y.t)
            yatt.append(y)
        for k in range(8):
            heads[k]["o"][0].release(t)
            heads[k]["o"][1].release(t)
        mg = []
        for m in range(KB):
            b, t = value(ugemm(WIN[72 + m]))
            s = fp.take()
            a = AC(lambda e, s=s, b=b, m=m: e.activation(s[:, :], b[:, :], ACT.Tanh, scale=0.5, bias=hb1[:, 8 + m:9 + m]), t, s.w, t_hb)
            b.release(a)
            v = DV(lambda e, s=s, m=m: e.scalar_tensor_tensor(out=s[:, :], in0=s[:, :], scalar=1.0, in1=yatt[m][:, :],
                                                            op0=ALU.add, op1=ALU.mult), a, yatt[m].t)
            yatt[m].release(v)
            v = DV(lambda e, s=s, m=m: e.tensor_tensor(s[:, :], s[:, :], yssd[m][:, :], ALU.add), v, yssd[m].t)
            yssd[m].release(v)
            hi, lo = rp.take(), rp.take()
            tk = split(hi[:, :], lo[:, :], s[:, :], v, [hi.w, lo.w])
            s.release(tk)
            mg.append((hi, lo, tk))
        end_u()
        y = []
        for m in range(KB):
            b = MB.take()
            t = matpanel(b, b.w, panel(d["wout"][m], KB * 128), KB, 0, lambda k: mg[k][0][:, :], lambda k: mg[k][1][:, :],
                         lambda k: mg[k][2], True, True)
            collect(y, b, t, "mix_post")
        for hi, lo, tk in mg:
            hi.release(t)
            lo.release(t)
        post_norm(y, False)
        t_all = drop_pages()

    with ExitStack() as ph:
        act = sb(ph, "act2", [128, 2, FB, L], R)
        t_phase = value(ffn(d["w2g"], d["w2u"], d["w2d"], "ffn2_pre", "ffn2_post", act, (t_all,)))

    with ExitStack() as ph:
        con = sb(ph, "con2", [128, NCB])
        t_con = ("c2", 16)
        AC(lambda e: e.dma_start(con[:, :], d["consts2"]).then_inc(sem("c2"), 16), t_phase)
        ident = con[:, 0:128]
        BDI, NEG = cc("bdincl"), cc("neg")
        NB_ = NB2
        fB = sb(ph, "fB2", [128, NB_, L])
        for i in range(NB_):
            fp.free.append((fB[:, i, :], [t_phase]))
        gxs = ExitStack()
        gxt = sb(gxs, "gx", [128, 16, L])
        gp = Pages([gxt[:, i, :] for i in range(16)], "gx pages")
        gp.free = [(b_, [t_phase]) for b_, _ in gp.free]
        norm_u("norm1", LATE[2])
        W2 = d["win2"]
        nar = NN = N3 = t_nar = t_NN = S0 = None

        def project_narrow():
            nonlocal S0
            S0 = yield from ugemm(W2[32])

        def narrow_side():
            nonlocal nar, NN, N3, t_nar, t_NN
            yield from until(lambda: S0 is not None)
            b, t = S0
            nar = fp.take()
            t0 = DV(lambda e: e.tensor_scalar(nar[:, :], b[:, :], pc("g_bias"), None, ALU.add), t, nar.w, t_par)
            t_b = AC(lambda e: e.activation(nar[32:64, :], nar[32:64, :], ACT.Sigmoid), t0)
            ISC = float((8 ** -0.5) * (64 ** -0.5))
            t_w = DV(lambda e: e.tensor_scalar(nar[64:96, :], nar[64:96, :], ISC, None, ALU.mult), t0)
            b.release(t0)
            gex = sm(1)
            ta = AC(lambda e: e.activation(gex, pc("g_alog"), ACT.Exp), t_par)
            w = fp.take()
            t = DV(lambda e: e.tensor_copy(w[:, :], nar[:, :]), t0, t_b, t_w, w.w)
            t = softplus(w, t, slice(0, 128))
            t = DV(lambda e: e.tensor_scalar(w[:, :], w[:, :], gex, -1.0, ALU.mult, ALU.mult), t, ta)
            a0 = CCOLS["reset64"][0]
            g_ = fp.take()
            t = DV(lambda e: e.tensor_tensor_scan(g_[:, :], con[:, a0:a0 + L], w[:, :], 0.0, ALU.mult, ALU.add), t, g_.w, t_con)
            w.release(t)
            r = slice(96, 128)
            tgs = [DV(lambda e: e.tensor_copy(nar[0:32, :], g_[0:32, :]), t),
                   DV(lambda e: e.tensor_tensor(
                       nar[r, :].rearrange("p (c l) -> p c l", l=64),
                       g_[r, :].rearrange("p (c l) -> p c l", l=64)[:, :, 63:64].broadcast_to([32, 8, 64]),
                       g_[r, :].rearrange("p (c l) -> p c l", l=64), ALU.subtract), t)]
            g_.release(tgs)
            t_nar = [tgs, t_b, t_w]
            for _ in range(NW[0]):
                yield
            b = SB.take()
            tp = turn(b, b.w, nar, t_nar)
            NN = fp.take()
            t = AC(lambda e: e.copy(NN[:, :], b[:, :]), tp, NN.w)
            b.release(t)
            N3 = NN[:, :].rearrange("p (t c) -> p t c", t=T4)
            t1 = AC(lambda e: e.activation(N3[:, :, 8:16], N3[:, :, 0:8], ACT.Exp), t)
            t2 = DV(lambda e: e.tensor_tensor(N3[:, :, 8:16], N3[:, :, 8:16], N3[:, :, 32:40], ALU.mult), t1)
            t3 = AC(lambda e: e.activation(N3[:, :, 96:104], N3[:, :, 96:104], ACT.Exp), t)
            t_NN = [t, t1, t2, t3]

        def v3(p):
            return p[:, :].rearrange("p (t l) -> p t l", t=T4)

        def bc(col):
            return N3[:, :, col:col + 1].broadcast_to([128, T4, 128])

        def bm(ap):
            return ap[:, None, :].broadcast_to([128, T4, 128])

        S = [dict() for _ in range(8)]
        zg = [None] * 8

        def project_gdn(h):
            for name, j in (("q", h), ("k", 8 + h), ("v", 16 + h)):
                b, t = yield from ugemm(W2[j])
                S[h][name] = convsilu(b, t, "gconv_w", j, None)
                yield

        def project_zg(h):
            b, t = yield from ugemm(W2[24 + h])
            z = fp.take()
            a = AC(lambda e, z=z, b=b: e.activation(z[:, :], b[:, :], ACT.Silu), t, z.w)
            b.release(a)
            yield
            b, t = yield from ugemm(W2[50 + h])
            s = fp.take()
            a2 = AC(lambda e, s=s, b=b, h=h: e.activation(s[:, :], b[:, :], ACT.Tanh, scale=0.5, bias=hb2[:, h:h + 1]), t, s.w, t_hb)
            b.release(a2)
            z.t = DV(lambda e, s=s, z=z: e.scalar_tensor_tensor(out=z[:, :], in0=s[:, :], scalar=1.0, in1=z[:, :],
                                                              op0=ALU.add, op1=ALU.mult), a, a2)
            s.release(z.t)
            zg[h] = z
            yield

        def l2(x, scale):
            r, t = yield from side_rstd([(x[:, :], x.t)], O1)
            x.t = DV(lambda e: e.scalar_tensor_tensor(out=x[:, :], in0=x[:, :], scalar=scale, in1=r[:, :], op0=ALU.mult, op1=ALU.mult),
                     r.t, x.t, t)
            r.release(x.t)

        def gdn_prep(h):
            H = S[h]
            q, k, v = H["q"], H["k"], H["v"]
            yield from both(l2(k, 1.0), l2(q, float(128 ** -0.5)))
            for _ in range(NW[3]):
                yield
            gb = SB.take()
            tg = PE(lambda e: e.matmul(gb[:, :], con[0:32, h:h + 1].broadcast_to([32, 128]), nar[0:32, :], start=True, stop=True),
                    t_nar, gb.w)
            eg = fp.take()
            eg.t = AC(lambda e: e.activation(eg[:, :], gb[:, :], ACT.Exp), tg, eg.w)
            gm = fp.take()
            t = DV(lambda e: e.tensor_tensor(v3(gm), v3(gb), bc(h), ALU.subtract), tg, eg.t, gm.w, t_NN)
            gb.release(eg.t, t)
            t = DV(lambda e: e.tensor_scalar(gm[:, :], gm[:, :], 0.0, None, ALU.min), t)
            t_g = AC(lambda e: e.activation(gm[:, :], gm[:, :], ACT.Exp), t)
            t_gm = DV(lambda e: e.tensor_tensor(v3(gm), v3(gm), bm(BDI), ALU.mult), t_g)
            yield
            bb = SB.take()
            tb = PE(lambda e: e.matmul(bb[:, :], con[32:64, 32 + h:33 + h].broadcast_to([32, 128]), nar[32:64, :], start=True, stop=True),
                    t_nar, bb.w)
            AT = gp.take()
            ta = DV(lambda e: e.tensor_tensor(AT[:, :], gm[:, :], bb[:, :], ALU.mult), tb, t_gm, AT.w)
            bb.release(ta)
            kk, qk = SB.take(), SB.take()
            for t in range(T4):
                c = slice(t * 128, (t + 1) * 128)
                t1 = PE(lambda e, c=c: e.matmul(kk[:, c], k[:, c], k[:, c], start=True, stop=True), k.t, kk.w)
                t2 = PE(lambda e, c=c: e.matmul(qk[:, c], k[:, c], q[:, c], start=True, stop=True), q.t, qk.w)
            AT.t = DV(lambda e: e.tensor_tensor(AT[:, :], AT[:, :], kk[:, :], ALU.mult), t1, ta)
            kk.release(AT.t)
            gm.t = DV(lambda e: e.tensor_tensor(gm[:, :], gm[:, :], qk[:, :], ALU.mult), t2, t_gm, ta)
            qk.release(gm.t)
            H["att"] = gm
            q.t = DV(lambda e: e.tensor_tensor(q[:, :], q[:, :], eg[:, :], ALU.mult), q.t, eg.t, t2)
            H["qg"], H["eg"] = q, eg
            for _ in range(NW[4]):
                yield
            b = SB.take()
            tp = turn(b, b.w, k, k.t)
            k.release(tp)
            kbe, kd = gp.take(), fp.take()
            kbe.t = DV(lambda e: e.tensor_tensor(v3(kbe), v3(b), bc(8 + h), ALU.mult), tp, kbe.w, t_NN)
            kd.t = DV(lambda e: e.tensor_tensor(v3(kd), v3(b), bc(96 + h), ALU.mult), tp, kd.w, t_NN)
            b.release(kbe.t, kd.t)
            H["kd"] = kd
            b2 = SB.take()
            tp = turn(b2, b2.w, v, v.t)
            v.release(tp)
            vb = gp.take()
            vb.t = DV(lambda e: e.tensor_tensor(v3(vb), v3(b2), bc(32 + h), ALU.mult), tp, vb.w, t_NN)
            b2.release(vb.t)
            yield
            lv = CCOLS["level"][0]
            U, Tm, Y, Ak = gp.take(), gp.take(), gp.take(), gp.take()
            t = DV(lambda e: e.tensor_tensor(v3(U), v3(AT), bm(con[:, lv:lv + 128]), ALU.mult), AT.t, U.w)
            tU = DV(lambda e: e.tensor_tensor(v3(U), bm(ident), v3(U), ALU.subtract), t)
            Ak2 = gp.take()
            Aks = {}

            def level(lev):
                A, w = ((Ak, Ak.w), (Ak2, Ak2.w))[lev % 2] if lev < 3 else (Aks[lev - 2][0], Aks[lev - 2][2])
                m = con[:, lv + 128 * lev:lv + 128 * lev + 128]
                t = GP(lambda e: e.tensor_tensor(v3(A), v3(AT), bm(m), ALU.mult), AT.t, w, t_con)
                Aks[lev] = [A, t, None]

            level(1)
            level(2)
            yield
            b = SB.take()
            tp = turn(b, b.w, U, tU)
            tT = AC(lambda e, b=b: e.copy(Tm[:, :], b[:, :]), tp, Tm.w)
            b.release(tT)
            wY = Y.w
            yield
            for lev in range(1, 6):
                A, tA, _ = Aks[lev]
                b = SB.take()
                for t in range(T4):
                    c = slice(t * 128, (t + 1) * 128)
                    tp = PE(lambda e, c=c, b=b: e.matmul(b[:, c], A[:, c], Tm[:, c], start=True, stop=True), tA, tT, b.w)
                wA = tp
                Aks[lev][2] = tp
                if lev < 4:
                    level(lev + 2)
                tY = AC(lambda e, b=b: e.copy(Y[:, :], b[:, :]), tp, wY)
                b.release(tY)
                yield
                b = SB.take()
                for t in range(T4):
                    c = slice(t * 128, (t + 1) * 128)
                    tp = PE(lambda e, c=c, b=b: e.matmul(b[:, c], Y[:, c], U[:, c], start=True, stop=True), tY, tU, b.w)
                if lev < 5:
                    b2 = SB.take()
                    for t in range(T4):
                        c = slice(t * 128, (t + 1) * 128)
                        tp2 = PE(lambda e, c=c, b2=b2: e.matmul(b2[:, c], U[:, c], Y[:, c], start=True, stop=True), b2.w)
                    tT = DV(lambda e, b2=b2: e.tensor_tensor(Tm[:, :], Tm[:, :], b2[:, :], ALU.subtract), tp2, tT, wA)
                    b2.release(tT)
                    tp = tp2
                wY = tp
                tU = DV(lambda e, b=b: e.tensor_tensor(U[:, :], U[:, :], b[:, :], ALU.subtract), tp, tU)
                b.release(tU)
                yield
            Tm.release(tT, wA)
            Y.release(wY)
            Ak.release(wA)
            Ak2.release(wA)
            AT.release(tA)
            b, b2 = SB.take(), SB.take()
            for t in range(T4):
                c = slice(t * 128, (t + 1) * 128)
                t1 = PE(lambda e, c=c: e.matmul(b[:, c], U[:, c], vb[:, c], start=True, stop=True), tU, vb.t, b.w)
                t2 = PE(lambda e, c=c: e.matmul(b2[:, c], kbe[:, c], U[:, c], start=True, stop=True), kbe.t, b2.w)
            uN, wT = fp.take(), fp.take()
            uN.t = AC(lambda e: e.copy(uN[:, :], b[:, :]), t1, uN.w)
            wT.t = AC(lambda e: e.copy(wT[:, :], b2[:, :]), t2, wT.w)
            b.release(uN.t)
            b2.release(wT.t)
            U.release(t2)
            vb.release(t1)
            kbe.release(t2)
            H["u"], H["w"] = uN, wT
            yield

        def gdn_scan(hs):
            n = len(hs)
            st_ = fp.take()
            vn = fp.take()
            o = {h: fp.take() for h in hs}
            t_S = [st_.w] * n
            t_Su = None
            wv = vn.w
            for c in range(8):
                t, half = c // 2, c % 2
                r = slice(64 * half, 64 * half + 64)
                cs = slice(c * 64, c * 64 + 64)
                if c:
                    b = SB.take()
                    for i, h in enumerate(hs):
                        tp = PE(lambda e, i=i, h=h, b=b, r=r, cs=cs: e.matmul(
                            b[r, i * 128:(i + 1) * 128], S[h]["w"][:, cs], st_[:, i * 128:(i + 1) * 128], start=True, stop=True),
                            S[h]["w"].t, t_S[i], b.w)
                tv = []
                for i, h in enumerate(hs):
                    ic = slice(i * 128, (i + 1) * 128)
                    tc = slice(t * 128, (t + 1) * 128)
                    if c:
                        tv.append(DV(lambda e, h=h, b=b, ic=ic, tc=tc, r=r: e.tensor_tensor(
                            vn[r, ic], S[h]["u"][r, tc], b[r, ic], ALU.subtract), tp, wv, S[h]["u"].t))
                    else:
                        tv.append(DV(lambda e, h=h, ic=ic, tc=tc, r=r: e.tensor_copy(vn[r, ic], S[h]["u"][r, tc]), wv, S[h]["u"].t))
                if c:
                    b.release(tv)
                yield
                if c < 7:
                    bs = SB.take()
                    for i, h in enumerate(hs):
                        ic = slice(i * 128, (i + 1) * 128)
                        tc = slice(t * 128, (t + 1) * 128)
                        ts = PE(lambda e, h=h, bs=bs, ic=ic, tc=tc, r=r: e.matmul(
                            bs[:, ic], S[h]["kd"][r, tc], vn[r, ic], start=True, stop=True), tv, S[h]["kd"].t, bs.w)
                if not half:
                    bo = SB.take()
                for i, h in enumerate(hs):
                    ic = slice(i * 128, (i + 1) * 128)
                    if c:
                        PE(lambda e: e.matmul(bo[r, ic], S[h]["qg"][:, cs], st_[:, ic], start=True, stop=False),
                           S[h]["qg"].t, bo.w, t_S[i])
                    to = PE(lambda e: e.matmul(bo[r, ic], S[h]["att"][r, cs], vn[r, ic], start=c == 0, stop=True),
                            tv, S[h]["att"].t, bo.w)
                wv = to
                if c < 7:
                    for i, h in enumerate(hs):
                        ic = slice(i * 128, (i + 1) * 128)
                        if c:
                            t_S[i] = DV(lambda e, h=h, bs=bs, ic=ic, c=c: e.scalar_tensor_tensor(
                                out=st_[:, ic], in0=st_[:, ic], scalar=S[h]["eg"][:, c * 64 + 63:c * 64 + 64], in1=bs[:, ic],
                                op0=ALU.mult, op1=ALU.add), ts, to, t_S[i], S[h]["eg"].t)
                        else:
                            t_S[i] = DV(lambda e, bs=bs, ic=ic: e.tensor_copy(st_[:, ic], bs[:, ic]), ts, t_S[i])
                    bs.release(*t_S)
                if half:
                    for i, h in enumerate(hs):
                        o[h].t = AC(lambda e: e.copy(o[h][:, t * 128:(t + 1) * 128], bo[:, i * 128:(i + 1) * 128]), to, o[h].w)
                    bo.release(o[hs[-1]].t)
                yield
            st_.release(to)
            vn.release(to)
            for h in hs:
                for name in ("w", "u", "kd", "qg", "att", "eg"):
                    S[h][name].release(to, t_S, tv)
            for h in hs:
                S[h]["o"] = o[h]

        def gdn_out(h):
            o = S[h]["o"]
            q = fp.take()
            a = AC(lambda e: e.activation(q[:, :], o[:, :], ACT.Square, scale=float(128 ** -0.5)), o.t, q.w)
            rs = ors[:, 4 * h:4 * h + 4]
            v = DV(lambda e: e.reduce_sum(rs, v3(q), AX.X), a)
            q.release(v)
            a = AC(lambda e: e.activation(rs, rs, ACT.Ln, bias=epsc), v, t_eps)
            a = AC(lambda e: e.activation(rs, rs, ACT.Exp, scale=-0.5), a)
            v = DV(lambda e: e.tensor_tensor(v3(o), v3(o), rs[:, :, None].broadcast_to([128, T4, 128]), ALU.mult), a, o.t)
            yield
            yield
            b = SB.take()
            tp = turn(b, b.w, o, v)
            o.release(tp)
            yield from until(lambda: zg[h] is not None)
            z = zg[h]
            z.t = DV(lambda e: e.scalar_tensor_tensor(out=z[:, :], in0=b[:, :], scalar=pc("gnorm"), in1=z[:, :],
                                                    op0=ALU.mult, op1=ALU.mult), tp, z.t)
            b.release(z.t)
            yield

        NGH = [(0, 1), (2, 3), (4, 5), (6, 7)]

        dq, dk, dv_, iq = [None] * 8, [None] * 2, [None] * 2, [None] * 4
        ikp = [None]

        def plain(j):
            b, t = yield from ugemm(W2[j])
            s = fp.take()
            s.t = AC(lambda e, s=s, b=b: e.copy(s[:, :], b[:, :]), t, s.w)
            b.release(s.t)
            return s

        def project_idx():
            x = yield from plain(49)
            yield
            b = SB.take()
            t = PE(lambda e: e.matmul(b[:, :], onesc[:, O128, :], x[:, :], start=True, stop=True), x.t, b.w)
            x.t = DV(lambda e: e.tensor_tensor(x[:, :], x[:, :], b[:, :], ALU.subtract), t)
            b.release(x.t)
            r, t = yield from side_rstd([(x[:, :], x.t)], O128)
            x.t = DV(lambda e: e.scalar_tensor_tensor(out=x[:, :], in0=x[:, :], scalar=pc("ikg"), in1=r[:, :], op0=ALU.mult, op1=ALU.mult),
                     r.t, x.t, t)
            r.release(x.t)
            ikp[0] = x
            yield
            for i in range(4):
                iq[i] = yield from plain(45 + i)
                yield

        def project_kv():
            for i in range(2):
                dk[i] = yield from plain(41 + i)
                yield
            for i in range(2):
                s = yield from plain(43 + i)
                b = SB.take()
                tp = turn(b, b.w, s, s.t)
                V = fp.take()
                V.t = AC(lambda e, V=V, b=b: e.copy(V[:, :], b[:, :]), tp, V.w)
                b.release(V.t)
                s.release(tp)
                dv_[i] = V
                yield

        masks = {}
        m8 = sm(8 * 3)
        cnt = sm(6)

        def indexer(i):
            W = 128 * (i + 1)
            x = ikp[0]
            sc = fp.take()
            sc.t = sc.w
            for h in range(8):
                r = slice(64 * (h % 2), 64 * (h % 2) + 64)
                b = SB.take()
                tp = PE(lambda e, h=h, r=r, b=b: e.matmul(b[:, 0:W], iq[h // 2][r, i * 128:(i + 1) * 128], x[r, 0:W],
                                                        start=True, stop=True), iq[h // 2].t, x.t, b.w)
                wcol = N3[:, i, 64 + h:65 + h]
                if h == 0:
                    v = DV(lambda e, b=b, wcol=wcol: e.tensor_scalar(sc[:, 0:W], b[:, 0:W], 0.0, wcol, ALU.max, ALU.mult),
                           tp, sc.t, t_NN)
                    b.release(v)
                else:
                    rl = fp.take()
                    a = AC(lambda e, b=b, rl=rl: e.activation(rl[:, 0:W], b[:, 0:W], ACT.Relu), tp, rl.w)
                    b.release(a)
                    v = DV(lambda e, rl=rl, wcol=wcol: e.scalar_tensor_tensor(
                        out=sc[:, 0:W], in0=rl[:, 0:W], scalar=wcol, in1=sc[:, 0:W], op0=ALU.mult, op1=ALU.add), a, sc.t, t_NN)
                    rl.release(v)
                sc.t = v
                if h % 2:
                    yield
            masks[i, "x"] = tp
            v = DV(lambda e: e.tensor_tensor(sc[:, W - 128:W], sc[:, W - 128:W], NEG, ALU.add), sc.t, t_con)
            wk = fp.take()
            top = m8[:, 8 * (i - 1):8 * i]
            t = DV(lambda e: e.max(top, sc[:, 0:W]), v)
            for n in range(15):
                src = sc if n == 0 else wk
                t = DV(lambda e, src=src: e.match_replace(out=wk[:, 0:W], in_to_replace=top, in_values=src[:, 0:W], imm_value=-3.0e38),
                       t, wk.w if n == 0 else None)
                t = DV(lambda e: e.max(top, wk[:, 0:W]), t)
                yield
            c0, c1 = cnt[:, 2 * i - 2:2 * i - 1], cnt[:, 2 * i - 1:2 * i]
            gt, eq = wk, fp.take()
            thr = top[:, 7:8]
            t1 = DV(lambda e: e.tensor_scalar(gt[:, 0:W], sc[:, 0:W], thr, None, ALU.is_gt, ALU.add, accum_out=c0), t)
            t2 = DV(lambda e: e.tensor_scalar(eq[:, 0:W], sc[:, 0:W], thr, None, ALU.is_equal), t, eq.w)
            t3 = DV(lambda e: e.tensor_scalar(c1, c0, -1.0, 128.0, ALU.mult, ALU.add), t1)
            t4 = DV(lambda e: e.tensor_tensor_scan(sc[:, 0:W], onesc[:, O1, 0:1].broadcast_to([128, W]), eq[:, 0:W], 0.0, ALU.mult, ALU.add), t2, t_ones[O1])
            t5 = DV(lambda e: e.scalar_tensor_tensor(out=eq[:, 0:W], in0=sc[:, 0:W], scalar=c1, in1=eq[:, 0:W],
                                                   op0=ALU.is_le, op1=ALU.mult), t4, t3)
            t6 = DV(lambda e: e.tensor_tensor(gt[:, 0:W], gt[:, 0:W], eq[:, 0:W], ALU.add), t5, t1)
            t7 = DV(lambda e: e.tensor_scalar(gt[:, 0:W], gt[:, 0:W], -1.0, -NEGBIG, ALU.add, ALU.mult), t6)
            eq.release(t6)
            sc.release(t5)
            gt.t = t7
            masks[i] = gt
            yield

        stat2 = {"k": 0}
        st2_free = [None] * 8
        dsc = float(128 ** -0.5)

        def sparse_head(h):
            q, k, V = dq[h], dk[h // 4], dv_[h // 4]
            o = fp.take()

            def front(i):
                W = 128 * (i + 1)
                s_i = stat2["k"] % 8
                stat2["k"] += 1
                s0 = st2[:, 8 * s_i:8 * s_i + 8]
                wst = st2_free[s_i]
                b = SB.take()
                tp = PE(lambda e, b=b, i=i, W=W: e.matmul(b[:, 0:W], q[:, i * 128:(i + 1) * 128], k[:, 0:W], start=True, stop=True),
                        q.t, k.t, b.w)
                P = fp.take()
                mk = NEG if i == 0 else masks[i][:, 0:W]
                v = DV(lambda e, b=b, P=P, mk=mk, W=W: e.tensor_tensor(P[:, 0:W], b[:, 0:W], mk, ALU.add), tp, P.w,
                       masks[i].t if i else None)
                b.release(v)
                v = DV(lambda e, P=P, W=W, s0=s0: e.reduce_max(s0[:, 0:1], P[:, 0:W], AX.X), v, wst)
                v = DV(lambda e, s0=s0: e.tensor_scalar(s0[:, 1:2], s0[:, 0:1], -dsc, None, ALU.mult), v)
                a = AC(lambda e, P=P, W=W, s0=s0: e.activation(P[:, 0:W], P[:, 0:W], ACT.Exp, scale=dsc, bias=s0[:, 1:2],
                                                             accum_out=s0[:, 2:3]), v)
                v = DV(lambda e, s0=s0: e.reciprocal(s0[:, 3:4], s0[:, 2:3]), a)
                P.t = DV(lambda e, P=P, W=W, s0=s0: e.tensor_scalar(P[:, 0:W], P[:, 0:W], s0[:, 3:4], None, ALU.mult), v, a)
                st2_free[s_i] = P.t
                return P, W, tp

            tp, tpv = yield from softmax_tiles(front, V, o, *LAG2)
            q.release(tp)
            S[h]["od"] = o
            S[h]["tpv"] = (tp, tpv)
            yield

        st2 = sm(64)
        ors = sm(32)

        def project_dq(h):
            dq[h] = yield from plain(33 + h)
            yield

        mg = [None] * 8

        def merge_heads(h):
            b, t = yield from ugemm(W2[58 + h])
            s = fp.take()
            a = AC(lambda e, s=s, b=b: e.activation(s[:, :], b[:, :], ACT.Tanh, scale=0.5, bias=hb2[:, 8 + h:9 + h]), t, s.w, t_hb)
            b.release(a)
            S[h]["sg"] = s
            s.t = a
            yield

        def merge_fin(h):
            s, o = S[h]["sg"], S[h]["od"]
            v = DV(lambda e: e.scalar_tensor_tensor(out=s[:, :], in0=s[:, :], scalar=1.0, in1=o[:, :],
                                                  op0=ALU.add, op1=ALU.mult), s.t, o.t)
            o.release(v)
            v = DV(lambda e: e.tensor_tensor(s[:, :], s[:, :], zg[h][:, :], ALU.add), v, zg[h].t)
            zg[h].release(v)
            hi, lo = rp.take(), rp.take()
            tk = split(hi[:, :], lo[:, :], s[:, :], v, [hi.w, lo.w])
            s.release(tk)
            mg[h] = (hi, lo, tk)

        def gdn_side():
            yield from narrow_side()
            for hs in NGH:
                yield from until(lambda: "v" in S[hs[1]])
                yield from both(gdn_prep(hs[0]), gdn_prep(hs[1]))
                yield from gdn_scan(hs)
                yield from both(gdn_out(hs[0]), gdn_out(hs[1]))

        def index_side():
            yield from until(lambda: iq[3] is not None and NN is not None)
            yield from both(indexer(1), indexer(2))
            yield from indexer(3)
            ikp[0].release(masks[3, "x"])
            for x in iq:
                x.release(masks[3, "x"])

        def pair(i):
            a, b_ = NGH[i]
            return chain(project_gdn(a), project_gdn(b_))

        def zgs(i):
            a, b_ = NGH[i]
            return chain(project_zg(a), project_zg(b_))

        def hold(i):
            return until(lambda: "w" in S[NGH[i][1]])

        steps = {"n": lambda i: project_narrow(), "p": pair, "x": lambda i: project_idx(), "h": hold, "z": zgs,
                 "k": lambda i: project_kv(), "d": project_dq, "r": room}
        main = chain(*[steps[w[0]](int(w[1:] or 0)) for w in ORDER2.split()])
        schedule(main, [(gdn_side(), RATES[2]), (index_side(), RATES[3])])
        assert len(gp.free) == 16
        gx_toks = [w for _, w in gp.free]
        gxs.close()
        mR = sb(ph, "mR2", [128, 16, L], R)
        rp = Pages([mR[:, i, :] for i in range(16)], "R pages")
        for i in range(16):
            rp.free[i] = (rp.free[i][0], gx_toks)

        def sparse_side():
            for h in range(0, 8, NZ):
                yield from until(lambda: all(dq[h + i] is not None for i in range(NZ)))
                yield from both(*[sparse_head(h + i) for i in range(NZ)])
                for i in range(NZ):
                    yield from until(lambda: "sg" in S[h + i])
                    merge_fin(h + i)
                    yield

        main = chain(merge_heads(0), merge_heads(1), *[chain(project_dq(h), project_dq(h + 1), room(9), merge_heads(h),
                                                             merge_heads(h + 1), room(9)) for h in (2, 4, 6)])
        schedule(main, [(sparse_side(), RATES[4])])
        end_u()
        for x in (*dk, *dv_):
            x.release(S[7]["tpv"])
        for i in (1, 2, 3):
            masks[i].release(S[7]["od"].t)
        nar.release(t_NN)
        NN.release(S[7]["od"].t)
        for m in range(KB):
            b = MB.take()
            t = matpanel(b, b.w, panel(d["wout2"][m], KB * 128), KB, 0, lambda k: mg[k][0][:, :], lambda k: mg[k][1][:, :],
                         lambda k: mg[k][2], True, True)
            t_h[m] = DV(lambda e: e.scalar_tensor_tensor(out=hT[:, m, :], in0=b[:, :], scalar=0.5, in1=hT[:, m, :],
                                                       op0=ALU.mult, op1=ALU.add), t, t_h[m])
            b.release(t_h[m])
        for hi, lo, tk in mg:
            hi.release(t)
            lo.release(t)
        t_all = drop_pages()

    with ExitStack() as ph:
        act = sb(ph, "act3", [128, 2, FB, L], R)
        norm_u("norm2", LATE[3])
        tact = []
        for j in range(FB):
            bg, tg = value(ugemm(d["w3"][j]))
            g_ = fp.take()
            t = conv(bg, tg, "fconv_w", 3, j, 44, "fconv_b", g_)
            a = AC(lambda e, g_=g_: e.activation(g_[:, :], g_[:, :], ACT.Silu), t)
            bu, tu_ = value(ugemm(d["w3"][FB + j]))
            u_ = fp.take()
            t = conv(bu, tu_, "fconv_w", 3, FB + j, 44, "fconv_b", u_)
            v = DV(lambda e, g_=g_, u_=u_: e.tensor_tensor(g_[:, :], g_[:, :], u_[:, :], ALU.mult), a, t)
            u_.release(v)
            tk = split(act[:, 0, j, :], act[:, 1, j, :], g_[:, :], v, [t_all])
            g_.release(tk)
            tact.append(tk)
        end_u()
        for m, b, t in down(d["w3d"], act, tact):
            t_h[m] = DV(lambda e, m=m, b=b: e.tensor_tensor(hT[:, m, :], hT[:, m, :], b[:, :], ALU.add), t, t_h[m])
            b.release(t_h[m])
        b = SB.take()
        t = sumsq(b, b.w, [(hT[:, k, :], t_h[k]) for k in range(KB)], O1024)
        r = rstd_of(b, t)
        for k in range(KB):
            t_h[k] = DV(lambda e, k=k: e.scalar_tensor_tensor(out=hT[:, k, :], in0=hT[:, k, :], scalar=pc("final", k), in1=r[:, :],
                                                            op0=ALU.mult, op1=ALU.mult), r.t, t_h[k], t)
    for k in range(KB):
        SP(lambda e, k=k: e.dma_start(out[k * 128:(k + 1) * 128, :], hT[:, k, :]).then_inc(sem("out"), 16), t_h[k])
    waits_at_end = [("out", 16 * KB)]

    queues = (SP, PE, AC, DV, GP)
    for q in queues:
        q.ops = [op for op in q.ops if op[0] is not None]
        for op in q.ops:
            op[1] = flat(op[1], [])
            for dep in op[1]:
                if isinstance(dep, Tok) and not (dep.eng is q and q is PE):
                    dep.used = True
    for q in queues:
        n = 0
        for op in q.ops:
            if op[2].used:
                n += 1
                op[2].val = n
        if n:
            sem(q.name)
    for q in queues:
        for op in q.ops:
            for dep in op[1]:
                if isinstance(dep, tuple):
                    sem(dep[0])

    def emit(q, eng):
        seen = {}
        table = None
        for fn, deps, tok in q.ops:
            func = fn.a[2] if q is AC and len(fn.a) > 2 else None
            want = next((name for funcs, name in TABLES if func in funcs), table)
            if want != table:
                eng.preload_act_table_set(want)
                table = want
            need = {}
            for dep in deps:
                if isinstance(dep, Tok):
                    if dep.eng is q and q is PE:
                        continue
                    assert dep.val > 0
                    need[dep.eng.name] = max(need.get(dep.eng.name, 0), dep.val)
                else:
                    need[dep[0]] = max(need.get(dep[0], 0), dep[1])
            for s, v in need.items():
                if seen.get(s, 0) < v:
                    eng.wait_ge(sem(s), v)
                    seen[s] = v
            ins = fn.issue()
            if tok.used:
                ins.then_inc(sem(q.name), 1)

    with ctx:
        block = ctx.enter_context(nc.Block())

        @block.sync
        def _(e):
            emit(SP, e)
            for s, v in waits_at_end:
                e.wait_ge(sem(s), v)

        @block.tensor
        def _(e):
            emit(PE, e)

        @block.scalar
        def _(e):
            emit(AC, e)

        @block.vector
        def _(e):
            emit(DV, e)

        @block.gpsimd
        def _(e):
            emit(GP, e)


def blocks(w, n=128):
    K, M = w.shape
    return np.ascontiguousarray(w.reshape(K // 128, 128, M // n, n).transpose(2, 1, 0, 3).reshape(M // n, 128, K // 128 * n))


def constants():
    p = np.arange(128)[:, None]
    f = np.arange(128)[None, :]
    a = np.zeros((128, NCA), np.float32)
    b = np.zeros((128, NCB), np.float32)

    def put(x, name, v):
        at, n = CCOLS[name]
        x[:, at:at + n] = v

    put(a, "ident", p == f)
    put(b, "ident", p == f)
    put(a, "ssdmask", p <= f)
    k = np.arange(512)[None, :] - 384
    put(a, "dist", np.where(k <= p, (k - p).astype(np.float64), NEGBIG))
    put(a, "reset128", np.arange(512)[None, :] % 128 != 0)
    put(b, "reset64", np.arange(512)[None, :] % 64 != 0)
    put(b, "neg", np.where(f <= p, 0.0, NEGBIG))
    put(b, "bdincl", (p <= f) & (p // 64 == f // 64))
    for lev in range(6):
        n = 1 << lev
        m = (p // (2 * n) == f // (2 * n)) & (f // n % 2 == 1) & (p // n % 2 == 0)
        at = CCOLS["level"][0] + 128 * lev
        b[:, at:at + 128] = m
    return a, b


def parameters(z):
    out = np.zeros((128, NPAR), np.float32)

    def put(name, v, rows=slice(0, 128)):
        at, n = PCOLS[name]
        out[rows, at:at + n] = v

    def cols(v):
        v = np.asarray(v).reshape(-1, 128)
        return v.T

    def taps(v):
        return np.concatenate([cols(v[0, i]) for i in range(v.shape[1])], axis=1)

    for name, src in (("ffn1_pre", "ffn1_pre_g"), ("ffn1_post", "ffn1_post_g"), ("mix_pre", "mix_pre_g"),
                      ("gate_b", "gate_b"), ("conv_b", "ssd_conv_b"), ("norm_g", "ssd_norm_g"),
                      ("subln", "da_subln_g"), ("mix_post", "mix_post_g"), ("ffn2_pre", "ffn2_pre_g"),
                      ("ffn2_post", "ffn2_post_g"), ("norm1", "norm1_g_2"), ("gnorm", "gdn_norm_g_2"),
                      ("bgb", "branch_gate_b_2"), ("norm2", "norm2_g_2"), ("fconv_b", "ffn_conv_b_2"),
                      ("final", "final_g_2")):
        put(name, cols(z[src]))
    put("conv_w", taps(z["ssd_conv_w"]))
    put("gconv_w", taps(z["gdn_conv_w_2"]))
    put("fconv_w", taps(z["ffn_conv_w_2"]))
    put("dt_bias", z["ssd_dt_bias"].reshape(32, 1), slice(0, 32))
    put("a_log", z["ssd_A_log"].reshape(32, 1), slice(0, 32))
    put("Dc", cols(np.repeat(z["ssd_D"].reshape(32), 64)))
    put("lam", np.concatenate([z[n].reshape(1, 64) for n in
                               ("da_lambda_q1", "da_lambda_k1", "da_lambda_q2", "da_lambda_k2")], axis=1))
    for r in (0, 96):
        put("g_bias", z["gdn_dt_bias_2"].reshape(8, 1), slice(r, r + 8))
        put("g_alog", z["gdn_a_log_2"].reshape(8, 1), slice(r, r + 8))
    put("ikg", np.concatenate([z["idx_k_norm_g_2"].reshape(64, 1)] * 2))
    return out


def layout(z):
    a = {"xT": np.ascontiguousarray(z["x"][0].T), "params": parameters(z)}
    a["consts1"], a["consts2"] = constants()
    w = z["w_in"][0]
    gap = np.zeros((1024, 96), np.float32)
    a["win"] = blocks(np.concatenate([w[:, 0:5120], w[:, 5152:], w[:, 5120:5152], gap], axis=1))
    a["w1g"], a["w1u"], a["w1d"] = (blocks(z[n][0]) for n in ("ffn1_w_gate", "ffn1_w_up", "ffn1_w_down"))
    a["w2g"], a["w2u"], a["w2d"] = (blocks(z[n][0]) for n in ("ffn2_w_gate", "ffn2_w_up", "ffn2_w_down"))
    a["wssd"] = np.ascontiguousarray(
        z["ssd_w_branch"][0].reshape(4, 4, 128, 4, 2, 128).transpose(0, 3, 2, 4, 1, 5).reshape(4, 4, 128, 1024))
    a["wda"], a["wout"] = blocks(z["da_w_branch"][0]), blocks(z["w_out"][0])
    w = z["w_in_2"][0]
    at = [0, 3072, 4096, 4104, 4112, 5136, 5392, 5648, 6160, 6224, 6232, 7256, 8280]
    qkv, zz, ga, gb, dq, dk, dv, iq, ik, iw, gta, gtb = (w[:, i:j] for i, j in zip(at[:-1], at[1:]))
    n24 = gap[:, 0:24]
    a["win2"] = blocks(np.concatenate([qkv, zz, ga, n24, gb, n24, iw, n24, ga, n24, dq, dk, dv, iq, ik, ik, gta, gtb], axis=1))
    a["wout2"], a["w3"], a["w3d"] = (blocks(z[n][0]) for n in ("w_out_2", "ffn_w_up_2", "ffn_w_down_2"))
    return a


def kernel(**inputs):
    import concourse.bacc as bacc
    from concourse.bass_utils import run_bass_kernel_spmd

    z = {k: np.asarray(v) for k, v in inputs.items()}
    nc = bacc.Bacc("TRN2", target_bir_lowering=False, num_devices=1)
    arrays = layout(z)
    d = {k: nc.dram_tensor("in_" + k, v.shape, F, kind="ExternalInput").ap() for k, v in arrays.items()}
    out = nc.dram_tensor("outT", (1024, 512), F, kind="ExternalOutput").ap()
    build(nc, d, out)
    r = run_bass_kernel_spmd(nc, [{"in_" + k: v for k, v in arrays.items()}], core_ids=[0])
    return np.ascontiguousarray(r.results[0]["outT"].T)[None]
```
